# Optimizing a Trainium2 kernel written in Bass

```python
import math
import jax, jax.numpy as jnp
from jax import lax
import numpy as np

D_MODEL = 1024
BATCH = 1
SEQ = 512
DEPTH = 1

D_MIX = D_MODEL
ATTN_WIDTH = D_MIX // 2
SSM_WIDTH = D_MIX - ATTN_WIDTH
QK_NOPE_DIM = 128
QK_ROPE_DIM = 64
V_HEAD_DIM = 128
N_ATTN_HEADS = ATTN_WIDTH // V_HEAD_DIM
Q_RANK = D_MODEL // 4
KV_RANK = D_MODEL // 8
ROPE_THETA = 10000.0
Q_BLOCK = 128
SSM_GROUP_CH = 16
SSM_GROUPS = SSM_WIDTH // SSM_GROUP_CH
SSM_STATE = 64
DT_MIN = 1e-3
DT_MAX = 1e-1
EPS = 1e-6
SPLITS = (Q_RANK, KV_RANK, QK_ROPE_DIM, ATTN_WIDTH, SSM_WIDTH, SSM_WIDTH)
D_IN = sum(SPLITS)


def _rms_norm(x, g):
    xf = x.astype(jnp.float32)
    y = xf * lax.rsqrt(jnp.mean(xf * xf, axis=-1, keepdims=True) + EPS)
    return (y * g.astype(jnp.float32)).astype(x.dtype)

def _rope_tables(positions, dim):
    inv_freq = ROPE_THETA ** (-jnp.arange(0, dim, 2, dtype=jnp.float32) / dim)
    ang = positions.astype(jnp.float32)[..., None] * inv_freq
    return jnp.cos(ang), jnp.sin(ang)

def _apply_rope(t, cos, sin):
    tf = t.astype(jnp.float32)
    t1, t2 = jnp.split(tf, 2, axis=-1)
    return jnp.concatenate([t1 * cos - t2 * sin, t1 * sin + t2 * cos], axis=-1).astype(t.dtype)

def _mla_attention(z_q, z_kv, z_kr, positions, q_norm_g, w_uq, kv_norm_g, w_ukv):
    bsz, seq, _ = z_q.shape
    q = (_rms_norm(z_q, q_norm_g) @ w_uq).reshape(bsz, seq, N_ATTN_HEADS, QK_NOPE_DIM + QK_ROPE_DIM)
    q_nope, q_rope = q[..., :QK_NOPE_DIM], q[..., QK_NOPE_DIM:]
    kv = (_rms_norm(z_kv, kv_norm_g) @ w_ukv).reshape(bsz, seq, N_ATTN_HEADS, QK_NOPE_DIM + V_HEAD_DIM)
    k_nope, v = kv[..., :QK_NOPE_DIM], kv[..., QK_NOPE_DIM:]
    cos, sin = _rope_tables(positions, QK_ROPE_DIM)
    q_rope = _apply_rope(q_rope, cos[:, :, None, :], sin[:, :, None, :])
    k_rope = _apply_rope(z_kr, cos, sin)
    n_blocks = seq // Q_BLOCK
    scale = (QK_NOPE_DIM + QK_ROPE_DIM) ** -0.5

    def to_blocks(t):
        return t.reshape(bsz, n_blocks, Q_BLOCK, *t.shape[2:]).swapaxes(0, 1)

    def attend_block(args):
        qn, qr = args
        s = (jnp.einsum('bqhd,bkhd->bhqk', qn, k_nope, preferred_element_type=jnp.float32)
             + jnp.einsum('bqhr,bkr->bhqk', qr, k_rope, preferred_element_type=jnp.float32))
        p = jax.nn.softmax(s * scale, axis=-1).astype(v.dtype)
        return jnp.einsum('bhqk,bkhd->bqhd', p, v)

    o = lax.map(attend_block, (to_blocks(q_nope), to_blocks(q_rope)))
    return o.swapaxes(0, 1).reshape(bsz, seq, N_ATTN_HEADS * V_HEAD_DIM)

def _diag_scan_op(e_i, e_j):
    a_i, b_i = e_i
    a_j, b_j = e_j
    return a_j * a_i, a_j * b_i + b_j

def _s5_bidirectional(u, lam_re, lam_im, log_dt, b_re, b_im, c_re, c_im, d_skip):
    bsz, seq, _ = u.shape
    u_t = u.astype(jnp.float32).reshape(bsz, seq, SSM_GROUPS, SSM_GROUP_CH).transpose(1, 0, 2, 3)
    u_c = u_t.astype(jnp.complex64)
    y = jnp.zeros_like(u_t)
    for direction, reverse in ((0, False), (1, True)):
        lam = lax.complex(jnp.minimum(lam_re[direction].astype(jnp.float32), -1e-4),
                          lam_im[direction].astype(jnp.float32))
        dt = jnp.exp(log_dt[direction].astype(jnp.float32))[:, None]
        lam_bar = jnp.exp(lam * dt)
        b = lax.complex(b_re[direction].astype(jnp.float32), b_im[direction].astype(jnp.float32))
        b_bar = ((lam_bar - 1.0) / lam)[..., None] * b
        c = lax.complex(c_re[direction].astype(jnp.float32), c_im[direction].astype(jnp.float32))
        bu = jnp.einsum('sbgh,gph->sbgp', u_c, b_bar)
        a = jnp.broadcast_to(lam_bar, (seq, 1, SSM_GROUPS, SSM_STATE))
        _, h = lax.associative_scan(_diag_scan_op, (a, bu), reverse=reverse, axis=0)
        y = y + jnp.real(jnp.einsum('sbgp,ghp->sbgh', h, c))
    y = y + d_skip.astype(jnp.float32).reshape(SSM_GROUPS, SSM_GROUP_CH) * u_t
    return y.transpose(1, 0, 2, 3).reshape(bsz, seq, SSM_WIDTH).astype(u.dtype)

def first_inputs(seed: int = 0) -> dict:
    key = jax.random.key(seed)
    ks = jax.random.split(key, 24)
    f32 = jnp.float32
    L, G, P, H = DEPTH, SSM_GROUPS, SSM_STATE, SSM_GROUP_CH

    def nrm(k, shape, std):
        return jax.random.normal(k, shape, f32) * std

    def gain(k, n):
        return 1.0 + 0.05 * jax.random.normal(k, (L, n), f32)

    x = jax.random.normal(ks[0], (BATCH, SEQ, D_MODEL), f32)
    inc = jax.random.randint(ks[1], (BATCH, SEQ), 1, 3, dtype=jnp.int32)
    positions = jnp.cumsum(inc, axis=1, dtype=jnp.int32) - 1
    n_idx = jnp.arange(P, dtype=f32)
    lam_re = -0.5 + 0.01 * jax.random.normal(ks[2], (L, 2, G, P), f32)
    lam_im = math.pi * n_idx + 0.01 * jax.random.normal(ks[3], (L, 2, G, P), f32)
    log_dt = jax.random.uniform(ks[4], (L, 2, G), f32, math.log(DT_MIN), math.log(DT_MAX))
    return {
        "x": x,
        "positions": positions,
        "pre_norm_g": gain(ks[5], D_MODEL),
        "w_in": nrm(ks[6], (L, D_MODEL, D_IN), D_MODEL ** -0.5),
        "q_norm_g": gain(ks[7], Q_RANK),
        "w_uq": nrm(ks[8], (L, Q_RANK, N_ATTN_HEADS * (QK_NOPE_DIM + QK_ROPE_DIM)), Q_RANK ** -0.5),
        "kv_norm_g": gain(ks[9], KV_RANK),
        "w_ukv": nrm(ks[10], (L, KV_RANK, N_ATTN_HEADS * (QK_NOPE_DIM + V_HEAD_DIM)), KV_RANK ** -0.5),
        "attn_out_g": gain(ks[11], ATTN_WIDTH),
        "s5_lam_re": lam_re,
        "s5_lam_im": lam_im,
        "s5_log_dt": log_dt,
        "s5_b_re": nrm(ks[12], (L, 2, G, P, H), (2.0 * H) ** -0.5),
        "s5_b_im": nrm(ks[13], (L, 2, G, P, H), (2.0 * H) ** -0.5),
        "s5_c_re": nrm(ks[14], (L, 2, G, H, P), (2.0 * P) ** -0.5),
        "s5_c_im": nrm(ks[15], (L, 2, G, H, P), (2.0 * P) ** -0.5),
        "s5_d": nrm(ks[16], (L, SSM_WIDTH), 1.0),
        "w_glu": nrm(ks[17], (L, SSM_WIDTH, SSM_WIDTH), SSM_WIDTH ** -0.5),
        "b_glu": nrm(ks[18], (L, SSM_WIDTH), 0.02),
        "ssm_out_g": gain(ks[19], SSM_WIDTH),
        "w_out": nrm(ks[20], (L, D_MIX, D_MODEL), D_MIX ** -0.5),
        "post_norm_g": gain(ks[21], D_MODEL),
    }

def first_block(x, positions, pre_norm_g, w_in, q_norm_g, w_uq, kv_norm_g, w_ukv, attn_out_g,
              s5_lam_re, s5_lam_im, s5_log_dt, s5_b_re, s5_b_im, s5_c_re, s5_c_im, s5_d,
              w_glu, b_glu, ssm_out_g, w_out, post_norm_g):
    split_points = list(np.cumsum(SPLITS)[:-1])
    for l in range(DEPTH):
        h = _rms_norm(x, pre_norm_g[l])
        z = h @ w_in[l]
        z_q, z_kv, z_kr, g_attn, u_ssm, g_ssm = jnp.split(z, split_points, axis=-1)
        attn = _mla_attention(z_q, z_kv, z_kr, positions, q_norm_g[l], w_uq[l], kv_norm_g[l], w_ukv[l])
        attn = _rms_norm(attn, attn_out_g[l]) * jax.nn.silu(g_attn)
        ssm = _s5_bidirectional(u_ssm, s5_lam_re[l], s5_lam_im[l], s5_log_dt[l], s5_b_re[l], s5_b_im[l],
                                s5_c_re[l], s5_c_im[l], s5_d[l])
        ssm = jax.nn.gelu(ssm)
        ssm = ssm * jax.nn.sigmoid(ssm @ w_glu[l] + b_glu[l])
        ssm = _rms_norm(ssm, ssm_out_g[l]) * jax.nn.silu(g_ssm)
        mixed = jnp.concatenate([attn, ssm], axis=-1) @ w_out[l]
        x = x + _rms_norm(mixed, post_norm_g[l])
    return x


DEPTH_2 = 2

HEAD_DIM = 64
N_NSA_HEADS = 8
N_NSA_KV = 2
NSA_GROUP = N_NSA_HEADS // N_NSA_KV
N_FOX_HEADS = 8
MIX_WIDTH = (N_NSA_HEADS + N_FOX_HEADS) * HEAD_DIM
N_BRANCH = 3
CMP_LEN = 32
CMP_STRIDE = 16
CMP_HIDDEN = 256
SEL_BLOCK = 64
SEL_TOPK = 16
WINDOW = 512
SEL_Q_BLOCK = 32
ROPE_THETA_2 = 500000.0
ROPE_DIMS = HEAD_DIM // 4
D_FF = 4 * D_MODEL
NORM_EPS = 1e-6
NEG_INF = -1e30
FORCED_SCORE = 1e4
NSA_Q_COLS = N_NSA_HEADS * HEAD_DIM
KV_COLS = N_NSA_KV * HEAD_DIM
NSA_GATE_COLS = N_NSA_HEADS * N_BRANCH
FOX_COLS = N_FOX_HEADS * HEAD_DIM
FOX_F_COLS = N_FOX_HEADS
COL_SIZES = (NSA_Q_COLS, KV_COLS, KV_COLS, KV_COLS, KV_COLS, KV_COLS, KV_COLS, NSA_GATE_COLS, FOX_COLS, FOX_COLS, FOX_COLS, FOX_F_COLS)
IN_COLS = NSA_Q_COLS + 6 * KV_COLS + NSA_GATE_COLS + 3 * FOX_COLS + FOX_F_COLS


def _rms_norm_2(x, g):
    xf = x.astype(jnp.float32)
    y = xf * lax.rsqrt(jnp.mean(xf * xf, axis=-1, keepdims=True) + NORM_EPS)
    return (y * g.astype(jnp.float32)).astype(x.dtype)

def _partial_rope(x, pos):
    half = ROPE_DIMS // 2
    inv_freq = ROPE_THETA_2 ** (-jnp.arange(half, dtype=jnp.float32) * 2.0 / ROPE_DIMS)
    ang = pos.astype(jnp.float32)[:, None] * inv_freq[None, :]
    cos, sin = jnp.cos(ang), jnp.sin(ang)
    xf = x.astype(jnp.float32)
    x1, x2 = xf[..., :half], xf[..., half:ROPE_DIMS]
    out = jnp.concatenate([x1 * cos - x2 * sin, x1 * sin + x2 * cos, xf[..., ROPE_DIMS:]], axis=-1)
    return out.astype(x.dtype)

def _masked_softmax(s, mask):
    return jax.nn.softmax(jnp.where(mask, s, NEG_INF), axis=-1)

def _unblock(t, axis):
    t = jnp.moveaxis(t, 0, axis)
    shp = t.shape
    return t.reshape(shp[:axis] + (shp[axis] * shp[axis + 1],) + shp[axis + 2:])

def _importance_map(seq):
    n_cmp = (seq - CMP_LEN) // CMP_STRIDE + 1
    n_sel = seq // SEL_BLOCK
    cs = np.arange(n_cmp)[:, None] * CMP_STRIDE
    ss = np.arange(n_sel)[None, :] * SEL_BLOCK
    overlap = np.clip(np.minimum(cs + CMP_LEN, ss + SEL_BLOCK) - np.maximum(cs, ss), 0, None)
    return jnp.asarray(overlap / CMP_LEN, dtype=jnp.float32)

def _compress(kv, pos_emb, w1, b1, w2, b2):
    b, g, s, d = kv.shape
    r = CMP_LEN // CMP_STRIDE
    n_chunk = s // CMP_STRIDE
    n_cmp = n_chunk - r + 1
    chunks = kv.reshape(b, g, n_chunk, CMP_STRIDE, d)
    blocks = jnp.concatenate([chunks[:, :, j:j + n_cmp] for j in range(r)], axis=3)
    blocks = (blocks + pos_emb).reshape(b, g, n_cmp, CMP_LEN * d)
    hid = jax.nn.gelu(blocks @ w1 + b1)
    return hid @ w2 + b2

def _nsa_mixer(q, k_c, v_c, k_s, v_s, k_w, v_w, gate_logits, gate_bias,
               pos_k, w1_k, b1_k, w2_k, b2_k, pos_v, w1_v, b1_v, w2_v, b2_v):
    b, s, _, d = q.shape
    pos = jnp.arange(s)
    scale = HEAD_DIM ** -0.5
    q = q.reshape(b, s, N_NSA_KV, NSA_GROUP, d).transpose(0, 2, 3, 1, 4)
    q_rot = _partial_rope(q, pos)
    k_c, v_c, k_s, v_s, k_w, v_w = (t.transpose(0, 2, 1, 3) for t in (k_c, v_c, k_s, v_s, k_w, v_w))
    kc = _compress(k_c, pos_k, w1_k, b1_k, w2_k, b2_k)
    vc = _compress(v_c, pos_v, w1_v, b1_v, w2_v, b2_v)
    n_cmp = kc.shape[2]
    cmp_end = jnp.arange(n_cmp) * CMP_STRIDE + CMP_LEN - 1
    imp_map = _importance_map(s)
    n_sel = s // SEL_BLOCK
    top_k = min(SEL_TOPK, n_sel)
    k_s_rot = _partial_rope(k_s, pos)
    pad = ((0, 0), (0, 0), (WINDOW, 0), (0, 0))
    k_w_pad = jnp.pad(_partial_rope(k_w, pos), pad)
    v_w_pad = jnp.pad(v_w, pad)
    blk = jnp.arange(n_sel)

    def block_fn(i):
        q0 = i * Q_BLOCK
        qpos = q0 + jnp.arange(Q_BLOCK)
        qp = lax.dynamic_slice_in_dim(q, q0, Q_BLOCK, axis=3)
        qr = lax.dynamic_slice_in_dim(q_rot, q0, Q_BLOCK, axis=3)
        sc = jnp.einsum('bghqd,bgnd->bghqn', qp, kc).astype(jnp.float32) * scale
        mc = cmp_end[None, :] <= qpos[:, None]
        pc = _masked_softmax(sc, mc) * mc
        o_cmp = jnp.einsum('bghqn,bgnd->bghqd', pc.astype(vc.dtype), vc)
        imp = jnp.einsum('bghqn,nj->bgqj', pc, imp_map)
        cur = qpos // SEL_BLOCK
        valid = blk[None, :] * SEL_BLOCK <= qpos[:, None]
        forced = (blk[None, :] == 0) | (blk[None, :] == cur[:, None]) | (blk[None, :] == cur[:, None] - 1)
        score = jnp.where(forced, FORCED_SCORE, jnp.where(valid, imp, -1.0))
        _, idx = lax.top_k(score, top_k)
        kw = lax.dynamic_slice_in_dim(k_w_pad, q0, WINDOW + Q_BLOCK, axis=2)
        vw = lax.dynamic_slice_in_dim(v_w_pad, q0, WINDOW + Q_BLOCK, axis=2)
        kpos = q0 - WINDOW + jnp.arange(WINDOW + Q_BLOCK)
        mw = (kpos[None, :] <= qpos[:, None]) & (kpos[None, :] > qpos[:, None] - WINDOW) & (kpos[None, :] >= 0)
        sw = jnp.einsum('bghqd,bgkd->bghqk', qr, kw).astype(jnp.float32) * scale
        pw = _masked_softmax(sw, mw)
        o_win = jnp.einsum('bghqk,bgkd->bghqd', pw.astype(vw.dtype), vw)
        return o_cmp, o_win, idx

    o_cmp, o_win, sel_idx = lax.map(block_fn, jnp.arange(s // Q_BLOCK))
    o_cmp = _unblock(o_cmp, 3)
    o_win = _unblock(o_win, 3)
    sel_idx = _unblock(sel_idx, 2)

    kb = k_s_rot.reshape(b, N_NSA_KV, n_sel, SEL_BLOCK, d)
    vb = v_s.reshape(b, N_NSA_KV, n_sel, SEL_BLOCK, d)
    gather = jax.vmap(jax.vmap(lambda blocks, ix: blocks[ix]))
    n_keys = top_k * SEL_BLOCK

    def sel_fn(c):
        q0 = c * SEL_Q_BLOCK
        qpos = q0 + jnp.arange(SEL_Q_BLOCK)
        qr = lax.dynamic_slice_in_dim(q_rot, q0, SEL_Q_BLOCK, axis=3)
        ix = lax.dynamic_slice_in_dim(sel_idx, q0, SEL_Q_BLOCK, axis=2)
        kg = gather(kb, ix)
        vg = gather(vb, ix).reshape(b, N_NSA_KV, SEL_Q_BLOCK, n_keys, d)
        kpos = ix[..., None] * SEL_BLOCK + jnp.arange(SEL_BLOCK)
        m = (kpos <= qpos[None, None, :, None, None]).reshape(b, N_NSA_KV, 1, SEL_Q_BLOCK, n_keys)
        ss = jnp.einsum('bghqd,bgqnkd->bghqnk', qr, kg).astype(jnp.float32) * scale
        ps = _masked_softmax(ss.reshape(b, N_NSA_KV, NSA_GROUP, SEL_Q_BLOCK, n_keys), m)
        return jnp.einsum('bghqm,bgqmd->bghqd', ps.astype(vg.dtype), vg)

    o_sel = _unblock(lax.map(sel_fn, jnp.arange(s // SEL_Q_BLOCK)), 3)

    g = jax.nn.sigmoid((gate_logits + gate_bias).astype(jnp.float32)).astype(q.dtype)
    g = g.reshape(b, s, N_NSA_KV, NSA_GROUP, N_BRANCH).transpose(0, 2, 3, 1, 4)
    o = g[..., 0:1] * o_cmp + g[..., 1:2] * o_sel + g[..., 2:3] * o_win
    return o.transpose(0, 3, 1, 2, 4).reshape(b, s, N_NSA_HEADS * d)

def _fox_mixer(q, k, v, f_logits, f_bias):
    b, s, h, d = q.shape
    scale = HEAD_DIM ** -0.5
    q, k, v = (t.transpose(0, 2, 1, 3) for t in (q, k, v))
    log_f = jax.nn.log_sigmoid(f_logits.astype(jnp.float32) + f_bias.astype(jnp.float32))
    cum = jnp.cumsum(log_f, axis=1).transpose(0, 2, 1)
    outs = []
    for i in range(s // Q_BLOCK):
        q0, q1 = i * Q_BLOCK, (i + 1) * Q_BLOCK
        logits = (jnp.einsum('bhqd,bhkd->bhqk', q[:, :, q0:q1], k[:, :, :q1]).astype(jnp.float32) * scale
                  + cum[:, :, q0:q1, None] - cum[:, :, None, :q1])
        mask = jnp.arange(q1)[None, :] <= jnp.arange(q0, q1)[:, None]
        p = _masked_softmax(logits, mask)
        outs.append(jnp.einsum('bhqk,bhkd->bhqd', p.astype(v.dtype), v[:, :, :q1]))
    o = jnp.concatenate(outs, axis=2)
    return o.transpose(0, 2, 1, 3).reshape(b, s, h * d)

def second_inputs(seed: int = 0) -> dict:
    key = jax.random.key(seed)
    ks = jax.random.split(key, 22)
    f32 = jnp.float32
    nrm = lambda k, shape, fan_in: jax.random.normal(k, shape, f32) * (fan_in ** -0.5)
    small = lambda k, shape, sc: sc * jax.random.normal(k, shape, f32)
    gain = lambda k: 1.0 + 0.05 * jax.random.normal(k, (DEPTH_2, D_MODEL), f32)
    cmp_in = CMP_LEN * HEAD_DIM
    return {
        "x": jax.random.normal(ks[0], (BATCH, SEQ, D_MODEL), f32),
        "w_in": nrm(ks[1], (DEPTH_2, D_MODEL, IN_COLS), D_MODEL),
        "b_nsa_gate": small(ks[2], (DEPTH_2, NSA_GATE_COLS), 0.01),
        "b_forget": jax.random.uniform(ks[3], (DEPTH_2, N_FOX_HEADS), f32, minval=1.0, maxval=6.0),
        "cmp_pos_k": small(ks[4], (DEPTH_2, CMP_LEN, HEAD_DIM), 0.1),
        "cmp_w1_k": nrm(ks[5], (DEPTH_2, cmp_in, CMP_HIDDEN), cmp_in),
        "cmp_b1_k": small(ks[6], (DEPTH_2, CMP_HIDDEN), 0.01),
        "cmp_w2_k": nrm(ks[7], (DEPTH_2, CMP_HIDDEN, HEAD_DIM), CMP_HIDDEN),
        "cmp_b2_k": small(ks[8], (DEPTH_2, HEAD_DIM), 0.01),
        "cmp_pos_v": small(ks[9], (DEPTH_2, CMP_LEN, HEAD_DIM), 0.1),
        "cmp_w1_v": nrm(ks[10], (DEPTH_2, cmp_in, CMP_HIDDEN), cmp_in),
        "cmp_b1_v": small(ks[11], (DEPTH_2, CMP_HIDDEN), 0.01),
        "cmp_w2_v": nrm(ks[12], (DEPTH_2, CMP_HIDDEN, HEAD_DIM), CMP_HIDDEN),
        "cmp_b2_v": small(ks[13], (DEPTH_2, HEAD_DIM), 0.01),
        "w_out": nrm(ks[14], (DEPTH_2, MIX_WIDTH, D_MODEL), MIX_WIDTH),
        "w_up": nrm(ks[15], (DEPTH_2, D_MODEL, D_FF), D_MODEL),
        "w_down": nrm(ks[16], (DEPTH_2, D_FF, D_MODEL), D_FF),
        "g_pre_mix": gain(ks[17]),
        "g_post_mix": gain(ks[18]),
        "g_pre_mlp": gain(ks[19]),
        "g_post_mlp": gain(ks[20]),
    }

def second_block(x, w_in, b_nsa_gate, b_forget, cmp_pos_k, cmp_w1_k, cmp_b1_k, cmp_w2_k, cmp_b2_k,
              cmp_pos_v, cmp_w1_v, cmp_b1_v, cmp_w2_v, cmp_b2_v, w_out, w_up, w_down,
              g_pre_mix, g_post_mix, g_pre_mlp, g_post_mlp):
    b, s, _ = x.shape
    split_at = [int(v) for v in np.cumsum(COL_SIZES)[:-1]]
    for l in range(DEPTH_2):
        h = _rms_norm_2(x, g_pre_mix[l])
        parts = jnp.split(h @ w_in[l], split_at, axis=-1)
        nq, kc, vc, ksel, vsel, kwin, vwin, gates, fq, fk, fv, ff = parts
        heads = lambda t, n: t.reshape(b, s, n, HEAD_DIM)
        o_nsa = _nsa_mixer(heads(nq, N_NSA_HEADS),
                           heads(kc, N_NSA_KV), heads(vc, N_NSA_KV),
                           heads(ksel, N_NSA_KV), heads(vsel, N_NSA_KV),
                           heads(kwin, N_NSA_KV), heads(vwin, N_NSA_KV),
                           gates, b_nsa_gate[l],
                           cmp_pos_k[l], cmp_w1_k[l], cmp_b1_k[l], cmp_w2_k[l], cmp_b2_k[l],
                           cmp_pos_v[l], cmp_w1_v[l], cmp_b1_v[l], cmp_w2_v[l], cmp_b2_v[l])
        o_fox = _fox_mixer(heads(fq, N_FOX_HEADS), heads(fk, N_FOX_HEADS), heads(fv, N_FOX_HEADS),
                           ff, b_forget[l])
        mix = jnp.concatenate([o_nsa, o_fox], axis=-1) @ w_out[l]
        x = x + _rms_norm_2(mix, g_post_mix[l])
        h = _rms_norm_2(x, g_pre_mlp[l])
        y = jnp.square(jax.nn.relu(h @ w_up[l])) @ w_down[l]
        x = x + _rms_norm_2(y, g_post_mlp[l])
    return x


def setup_inputs(seed=0):
    out = dict(first_inputs(seed))
    for name, value in second_inputs(seed + 1).items():
        if name != "x":
            out[name + "_2"] = value
    return out


def reference(
    x, positions, pre_norm_g, w_in, q_norm_g, w_uq, kv_norm_g, w_ukv, attn_out_g, s5_lam_re,
    s5_lam_im, s5_log_dt, s5_b_re, s5_b_im, s5_c_re, s5_c_im, s5_d, w_glu, b_glu, ssm_out_g,
    w_out, post_norm_g, w_in_2, b_nsa_gate_2, b_forget_2, cmp_pos_k_2, cmp_w1_k_2, cmp_b1_k_2,
    cmp_w2_k_2, cmp_b2_k_2, cmp_pos_v_2, cmp_w1_v_2, cmp_b1_v_2, cmp_w2_v_2, cmp_b2_v_2,
    w_out_2, w_up_2, w_down_2, g_pre_mix_2, g_post_mix_2, g_pre_mlp_2, g_post_mlp_2,
):
    x = first_block(
        x, positions, pre_norm_g, w_in, q_norm_g, w_uq, kv_norm_g, w_ukv, attn_out_g, s5_lam_re,
        s5_lam_im, s5_log_dt, s5_b_re, s5_b_im, s5_c_re, s5_c_im, s5_d, w_glu, b_glu, ssm_out_g,
        w_out, post_norm_g,
    )
    return second_block(
        x, w_in_2, b_nsa_gate_2, b_forget_2, cmp_pos_k_2, cmp_w1_k_2, cmp_b1_k_2, cmp_w2_k_2,
        cmp_b2_k_2, cmp_pos_v_2, cmp_w1_v_2, cmp_b1_v_2, cmp_w2_v_2, cmp_b2_v_2, w_out_2,
        w_up_2, w_down_2, g_pre_mix_2, g_post_mix_2, g_pre_mlp_2, g_post_mlp_2,
    )


_drawn_inputs = setup_inputs


def setup_inputs(seed=0):
    import zlib

    import numpy as np

    out = dict(_drawn_inputs(seed))
    spreads = {}
    factors = {'s5_lam_re': 200.0,
     'b_glu': 8.0,
     'b_nsa_gate_2': 36.326,
     'cmp_pos_k_2': 8.0,
     'cmp_b1_k_2': 64.0,
     'cmp_b2_k_2': 200.0,
     'cmp_b1_v_2': 8.0,
     'cmp_b2_v_2': 6.528,
     's5_lam_im': 24.896,
     's5_log_dt': 26.168,
     's5_b_re': 34.376,
     's5_b_im': 34.432,
     's5_c_re': 34.008,
     's5_c_im': 34.472}
    for name, (base, spread) in spreads.items():
        noise = np.random.default_rng([zlib.crc32(name.encode()), seed]).standard_normal(out[name].shape)
        drawn = base * np.exp(spread * noise) if base else spread * noise
        out[name] = __import__('jax').numpy.asarray(drawn.astype(out[name].dtype))
    for name, factor in factors.items():
        out[name] = (out[name] * factor).astype(out[name].dtype)
    return out
```

```python
from contextlib import ExitStack
from collections import namedtuple

import numpy as np
import concourse.bass as bass
from concourse import mybir

F32 = mybir.dt.float32
I32 = mybir.dt.int32
ALU = mybir.AluOpType
ACT = mybir.ActivationFunctionType
AX_X = mybir.AxisListType.X

P = 128
SEQ = 512
D = 1024
T = SEQ // P
KD = D // P
EPS = 1e-6

Q_RANK, KV_RANK, ROPE1 = 256, 128, 64
H1, NOPE, VD = 4, 128, 128
WIDE = 512
G, CH, ST = 32, 16, 64
L = 8
NC = SEQ // L
NQ, GQ = 4, 8
SCALE1 = float(NOPE + ROPE1) ** -0.5

DEPTH = 2
HD = 64
NH, KVG = 8, 2
CMP_LEN, CMP_STRIDE, CMP_HID = 32, 16, 256
NCMP = (SEQ - CMP_LEN) // CMP_STRIDE + 1
LP = CMP_LEN // 2
DFF = 4 * D
NF = DFF // P
SCALE2 = float(HD) ** -0.5
C_Q, C_KC, C_VC, C_KS, C_VS, C_KW, C_VW, C_GATE, C_FQ, C_FK, C_FV, C_FF = [
    int(v) for v in np.cumsum([0, 512, 128, 128, 128, 128, 128, 128, 24, 512, 512, 512])]
NGATE = 24
IN2 = C_FF + 8
BIG_NEG = 1e30

NS = 8
NPJ, NPM = 24, 6
NU = 96
ROWS = 128


def rope_table_2():
    half = HD // 4 // 2
    inv = np.float32(500000.0) ** (-np.arange(half, dtype=np.float32) * np.float32(2.0) / np.float32(HD // 4))
    ang = np.arange(SEQ, dtype=np.float32)[None, :] * inv.astype(np.float32)[:, None]
    c = np.ones((HD, SEQ), np.float32)
    s = np.zeros((HD, SEQ), np.float32)
    c[:half], c[half:2 * half] = np.cos(ang), np.cos(ang)
    s[:half], s[half:2 * half] = -np.sin(ang), np.sin(ang)
    return np.concatenate([c, c]), np.concatenate([s, s])


def swap_matrix(block, half, sign=1.0):
    m = np.zeros((P, P), np.float32)
    for b in range(0, P, block):
        for r in range(half):
            m[b + half + r, b + r] = 1.0
            m[b + r, b + half + r] = sign
    return m


def constants():
    q = np.arange(P)
    tri = np.zeros((P, SEQ), np.float32)
    tri[:, SEQ - P:] = np.where(q[None, :] <= q[:, None], 0.0, BIG_NEG)
    tok = np.arange(SEQ).reshape(T, P).T
    end = np.full(32, 10 ** 6)
    end[:NCMP] = np.arange(NCMP) * CMP_STRIDE + CMP_LEN - 1
    cmask = np.where(end[None, None, :] <= tok[:, :, None], 0.0, BIG_NEG).astype(np.float32)
    valid = (tok >= CMP_LEN - 1).astype(np.float32)
    c2, s2 = rope_table_2()
    inv1 = np.float32(10000.0) ** (-np.arange(0, ROPE1, 2, dtype=np.float32) / np.float32(ROPE1))
    col = np.zeros((P, 8), np.float32)
    col[:, 0] = np.tile(inv1, 4)
    col[:, 1] = np.tile(np.repeat([-1.0, 1.0], 32), 2)
    col[:, 2] = np.repeat([-1.0, 1.0], ST)
    return {
        "c_ident": np.eye(P, dtype=np.float32), "c_tri": tri, "c_cmask": cmask.reshape(P, T * 32),
        "c_valid": valid, "c_cos2": c2, "c_sin2": s2, "c_col": col,
        "c_swap2": swap_matrix(HD, HD // 8), "c_swap1": swap_matrix(ROPE1, ROPE1 // 2),
        "c_turn": swap_matrix(P, ST, -1.0),
    }


class Unit:

    def __init__(self, name, slots, pieces, used):
        self.name, self.slots = name, slots
        self.pieces = pieces
        self.used = used
        self.slot = self.landed = 0
        self.free = []

ONE_SEMS = (
    "par_in par_ps par dt_e par_exp par_trig amp "
    "u_ps u_sb uT_ps uT gs_ps gs za_ps za_sq za_rstd zn znT_ps znT ga_ps ga "
    "pos_in bglu_in angle trig rope_tab rope_ps rope_done "
    "bc_in cT_ps cT b_bar m1 m1T_ps w1T m3 tap_ps taps toep st_ps st_sb turn_ps turned state y_ps y_sb yT_ps yp "
    "ge geT_ps geT glu_ps glu_x glu_s glu_y mixer_sq mixer_rstd ssm_o "
    "qn_ps qn rq_ps rq kn_ps kn v1_ps v1 "
    "a_s_ps a_min a_exp a_pT_ps a_pT a_o_ps a_o at_o "
    "m1ix_ps m1ix").split()

TWO_PI = 2 * np.pi
PI2_A = 6.28125
PI2_B = float(np.float32(int((TWO_PI - PI2_A) * 2 ** 22) / 2 ** 22))
PI2_C = float(np.float32(TWO_PI - PI2_A - PI2_B))
ROUND = 12582912.0
PI_SAFE = 3.1415925
DG = 2 * G
DQ = 2 * GQ
NK = L + 1


def one_units(a, unit, colblock, quad, t_blocks, sem):
    w = a["w_in"][0]
    c_q, c_kr, c_ga, c_u, c_gs = 0, Q_RANK + KV_RANK, 448, 960, 1472
    quad("u", [((0, 512), t_blocks(w, (c_u, c_u + 512)))], sem.u_ps, T)
    quad("gs", [((0, 512), t_blocks(w, (c_gs, c_gs + 512)))], sem.gs_ps, T)
    quad("za", [((0, 448), t_blocks(w, (c_q, 448)))], sem.za_ps, T)
    quad("ga", [((0, 512), t_blocks(w, (c_ga, c_ga + 512)))], sem.ga_ps, T)
    quad("glu", [((0, 512), t_blocks(a["w_glu"][0], (0, 512)))], sem.glu_ps, T)
    w = a["w_uq"][0].rearrange("(k p) (h c) -> k p h c", p=P, h=H1)
    pieces = []
    for k in range(2):
        pieces.append((("q", k * 768, H1, NOPE), w[k, :, :, 0:NOPE]))
        pieces.append((("q", k * 768 + 512, H1, ROPE1), w[k, :, :, NOPE:NOPE + ROPE1]))
    unit("uq", 4, pieces, sem.rq_ps, 2)
    unit("ukv", 1, [(None, a["w_ukv"][0])], sem.v1_ps, T)
    for k in range(KD):
        unit(f"wo{k}", 1, [(None, a["w_out"][0][P * k:P * k + P, :])], sem.out_ps, 8)


def build(nc, a, out, first=True, second=True):
    names = (
        "x_in0 x_in1 x_in2 x_in3 wrows_zero rows_in consts_in small_in postgain_in wring0 wring1 wring2 wring3 wring4 wring5 wring6 wring7 "
        "cols_ps cols_ready const_set "
        "sq rstd xn xT hT x_new out_ps post_sq post_y post_rstd "
        "proj proj_sb perm rot rot_cos gate_x gate_e gate "
        "ff_T ff_z ff_abs ff_exp ff_ln ff_cum ff_rows aug_ones "
        "cmp_E hid_ps hid hid_rep kc_ps kc vc_ps vc "
        "cs_ps cs_exp cs_p cs_pT_ps cs_pT cs_o_ps cs_o "
        "s_ps s_masked s_exp pT_ps pT_act pT_dve o_ps o_sb "
        "mixT_ps mixT_act mixT_dve up_ps relu relu_sq down "
        "act_chain dve_chain pool_chain out_done").split()
    if first:
        names += ONE_SEMS
    with ExitStack() as ctx:
        sem = namedtuple("Semaphores", names)(*[ctx.enter_context(nc.semaphore("s_" + n)) for n in names])
        wring = [sem.wring0, sem.wring1, sem.wring2, sem.wring3, sem.wring4, sem.wring5, sem.wring6, sem.wring7]

        x_in = [sem.x_in0, sem.x_in1, sem.x_in2, sem.x_in3]

        def sb(name, *free, parts=P):
            return ctx.enter_context(nc.sbuf_tensor(name, [parts, *free], F32))

        ps = [ctx.enter_context(nc.psum_tensor(f"ps{b}", [P, 512], F32)) for b in range(8)]

        X = sb("X", T, D)
        HT = sb("HT", KD, SEQ)
        WR = sb("WR", NS, 1024)
        ident, swap2 = sb("ident", P), sb("swap2", P)
        tri, cos2, sin2 = sb("tri", SEQ), sb("cos2", SEQ), sb("sin2", SEQ)
        cmask, valid = sb("cmask", T, 32), sb("valid", T)
        rows, cols = sb("rows", P), sb("cols", ROWS)
        postg = sb("postg", D)
        gbias, b2v = sb("gbias", DEPTH, NGATE), sb("b2v", DEPTH, HD)
        w2k, w2v = sb("w2k", DEPTH, 2, P), sb("w2v", DEPTH, 2, HD)
        neghalf = sb("neghalf", T)
        ones = sb("ones", 1)
        ss, ms, rstd = sb("ss", T), sb("ms", T), sb("rstd", T)
        pss, pms, prstd = sb("pss", T, 2), sb("pms", T), sb("prstd", T)
        kcBD, vBD = sb("kcBD", KVG, 2, 32), sb("vBD", KVG, 4, HD)
        hidk, hidv, hidr = sb("hidk", 2, 64), sb("hidv", 2, KVG, 32), sb("hidr", 2, KVG, 4, 32)
        gf, gx, gate = sb("gf", T, 32), sb("gx", T, NGATE), sb("gate", T, NGATE)
        ffz, ffm, ffc = (sb(n, SEQ, parts=8) for n in ("ffz", "ffm", "ffc"))
        mn, rs, rg = sb("mn", 4), sb("rs", NU), sb("rg", 3, 4)
        cmn, csum = sb("cmn", NH), sb("csum", NH)

        BIGW = 28672
        BIG = sb("BIG", BIGW)

        def carve(at, *shape):
            n = int(np.prod(shape))
            assert at + n <= BIGW, (at, n)
            v = BIG[:, at:at + n]
            if len(shape) == 2:
                v = v.rearrange("p (a b) -> p a b", b=shape[1])
            if len(shape) == 3:
                v = v.rearrange("p (a b c) -> p a b c", b=shape[1], c=shape[2])
            return v

        qT, qrT = carve(0, 4, SEQ), carve(2048, 4, SEQ)
        ksT, kwT = carve(4096, 2, SEQ), carve(5120, 2, SEQ)
        fq, fk = carve(6144, NH, SEQ), carve(10240, NH, SEQ)
        vn, fv = carve(14336, T, 256), carve(15360, T, 512)
        O = carve(17408, T, D)
        uT = carve(0, NF, SEQ)
        Y = O
        A0 = 21504
        xn = carve(A0, 2, D)
        junk = carve(A0 + 2048, D)
        relu = carve(A0 + 3072, 2, SEQ)
        junk2 = carve(A0 + 4096, 512)
        kraw, rcos, rsin = carve(A0, 2, SEQ), carve(A0 + 1024, 2, SEQ), carve(A0 + 2048, 2, SEQ)
        X2 = [carve(A0 + 3072, 2, SEQ), carve(A0 + 4096, 2, SEQ)]
        E = [carve(A0 + 5120, LP, 2 * NCMP), carve(A0 + 5120 + LP * 2 * NCMP, LP, 2 * NCMP)]
        SM = carve(A0 + 3072, 3, SEQ)
        PR = carve(A0 + 4608, 2, SEQ)
        PT = carve(A0 + 5632, 2, SEQ)
        CS, CP = carve(A0, NH, 32), carve(A0 + 256, KVG, P)
        CX = carve(A0 + 512, KVG, P)

        R_PRE1, R_QN, R_KVN, R_AO, R_SO = 0, 8, 10, 11, 15
        R_NORM, R_B1, R_POS, R_B2K, R_BF = 19, 51, 59, 123, 125

        def t_blocks(w, n):
            return w.rearrange("(k p) c -> p k c", p=P)[:, :, n[0]:n[1]]

        units = []

        def unit(name, slots, pieces, sema, value):
            units.append(Unit(name, slots, pieces, (sema, value)))

        def colblock(name, w, c, n, sema, value):
            unit(name, 1, [((0, n), t_blocks(w, (c, c + n)))], sema, value)

        def quad(name, pieces, sema, value):
            unit(name, 4, pieces, sema, value)

        if first:
            one_units(a, unit, colblock, quad, t_blocks, sem)
        B1 = int(first)
        if second:
            for l in range(DEPTH):
                w = a["w_in_2"][l]
                at = 0
                pieces = []
                for c, n in ((C_VS, P), (C_VW, P), (C_GATE, NGATE), (C_FF, 8)):
                    pieces.append(((at, n), t_blocks(w, (c, c + n))))
                    at += n
                pj = lambda n: NPJ * l + n + 1
                quad(f"n1_{l}", pieces, sem.proj, pj(3))
                for i, c in enumerate((C_KC, C_VC, C_KS, C_KW)):
                    colblock(f"t{4 + i}_{l}", w, c, P, sem.proj, pj(4 + i))
                for i, kind in enumerate("kv"):
                    w1 = a[f"cmp_w1_{kind}_2"][l]
                    unit(f"w1{kind}_{l}", 4, [(None, w1.rearrange("(k p) c -> p k c", p=P))], sem.hid_ps, 2 * l + i + 1)
                for i in range(4):
                    colblock(f"t{8 + i}_{l}", w, C_Q + P * i, P, sem.proj, pj(8 + i))
                quad(f"n2_{l}", [((0, 512), t_blocks(w, (C_FV, C_FV + 512)))], sem.proj, pj(15))
                for i in range(8):
                    colblock(f"t{16 + i}_{l}", w, C_FQ + P * i, P, sem.proj, pj(16 + i))
                for k in range(KD):
                    unit(f"wo{k}_{l}", 1, [(None, a["w_out_2"][l][P * k:P * k + P, :])], sem.out_ps,
                         8 * (B1 + 2 * l) + 8)
                for f in range(NF):
                    colblock(f"up{f}_{l}", a["w_up_2"][l], P * f, P, sem.up_ps, NF * l + f + 1)
                for half in range(2):
                    for f in range(0, NF, 2):
                        wd = a["w_down_2"][l][P * f:P * f + 2 * P, 512 * half:512 * half + 512]
                        read = (sem.down, (NF - 2) * l + (NF // 2 - 1) * half + f // 2 + 1)
                        if f == NF - 2:
                            read = (sem.out_ps, 8 * (B1 + 2 * l + 1) + 4 * half + 4)
                        unit(f"dn{half}_{f}_{l}", 1, [(None, wd.rearrange("(k p) c -> p k c", p=P))], *read)

        by_name, at, owner, loads = {}, 0, [None] * NS, [0] * NS
        for u in units:
            if at % NS + u.slots > NS or (u.slots == 4 and at % 4):
                at += (-at) % 4
            u.slot = at % NS
            for s in range(u.slot, u.slot + u.slots):
                if owner[s] is not None and owner[s].used not in u.free:
                    u.free.append(owner[s].used)
                owner[s] = u
            loads[u.slot] += 16 * len(u.pieces)
            u.landed = loads[u.slot]
            by_name[u.name] = u
            at += u.slots

        def slots(u):
            return WR[:, u.slot:u.slot + u.slots, :].rearrange("p s n -> p (s n)")

        def arrived(pe, name):
            u = by_name[name]
            pe.wait_ge(wring[u.slot], u.landed)
            return slots(u)

        def block_of(name, pe, width=P):
            return arrived(pe, name).rearrange("p (k c) -> p k c", c=width)

        def norm_squares(act, v, x_count):
            for t in range(T):
                act.wait_ge(*x_count(t))
                if v or t:
                    act.wait_ge(sem.sq, T * v + t)
                if v and t == 0:
                    act.wait_ge(sem.rstd, T * v)
                nc.scalar.activation(junk if v + V0 else BIG[:, 6144:6144 + D], X[:, t, :], ACT.Square, accum_out=ss[:, t:t + 1]).then_inc(sem.sq, 1)

        def norm_rstd(pool, v):
            for t in range(T):
                pool.wait_ge(sem.sq, T * v + t + 1)
                if v:
                    pool.wait_ge(sem.xn, T * (v - 1) + t + 1)
                pool_link(nc.gpsimd.tensor_scalar(ms[:, t:t + 1], ss[:, t:t + 1], 1.0 / D, EPS, ALU.mult, ALU.add))
                nc.gpsimd.tensor_tensor(rstd[:, t:t + 1], ms[:, t:t + 1], neghalf[:, 0:1], ALU.pow).then_inc(sem.rstd, 1)

        def norm_scale(dve, v, t):
            dve.wait_ge(sem.rstd, T * v + t + 1)
            if T * v + t >= 2:
                dve.wait_ge(sem.xT, 2 * (T * v + t - 1))
            nc.vector.tensor_scalar(xn[:, t % 2, :], X[:, t, :], rstd[:, t:t + 1], None, ALU.mult).then_inc(sem.xn, 1)

        def norm_transpose(pe, v, t):
            pe.wait_ge(sem.xn, T * v + t + 1)
            for half in range(2):
                i = 2 * t + half
                if i >= 4:
                    pe.wait_ge(sem.hT, 8 * v + i - 3)
                for k in range(4):
                    last = nc.tensor.transpose(ps[i % 4][:, P * k:P * k + P],
                                               xn[:, t % 2, 512 * half + P * k:512 * half + P * k + P], ident[:])
                last.then_inc(sem.xT, 1)

        def norm_evacuate(dve, v, t, chunked):
            g0 = R_PRE1 if chunked else R_NORM + 8 * (v + V0 - 1)
            for half in range(2):
                i = 2 * t + half
                dve.wait_ge(sem.xT, 8 * v + i + 1)
                gain = cols[:, g0 + 4 * half:g0 + 4 * half + 4]
                if chunked:
                    for k in range(4):
                        src = ps[i % 4][:, P * k:P * k + P].rearrange("p (c i) -> p i c", i=L)
                        dst = HT[:, 4 * half + k, :].rearrange("p (i c) -> p i c", i=L)[:, :, t * (P // L):(t + 1) * (P // L)]
                        last = nc.vector.tensor_scalar(dst, src, gain[:, k:k + 1], None, ALU.mult)
                else:
                    last = nc.vector.tensor_tensor(
                        HT[:, 4 * half:4 * half + 4, P * t:P * t + P],
                        ps[i % 4][:].rearrange("p (k n) -> p k n", k=4),
                        gain[:, :, None].to_broadcast([P, 4, P]), ALU.mult)
                last.then_inc(sem.hT, 1)

        def norm_dve(dve, v, chunked=False):
            norm_scale(dve, v, 0)
            norm_scale(dve, v, 1)
            for t in range(T):
                norm_evacuate(dve, v, t, chunked)
                if t + 2 < T:
                    norm_scale(dve, v, t + 2)

        def post_squares(act, w, tile_half):
            for e in range(8):
                t, half = tile_half(e)
                act.wait_ge(sem.out_ps, 8 * w + e + 1)
                if w or e:
                    act.wait_ge(sem.post_sq, 8 * w + e)
                if w and e == 0:
                    act.wait_ge(sem.post_rstd, T * w)
                nc.scalar.activation(junk2, ps[e][:], ACT.Square,
                                     accum_out=pss[:, t, half:half + 1]).then_inc(sem.post_sq, 1)

        def post_factor(pool, w, tile_half):
            last_e = {tile_half(e)[0]: e for e in range(8)}
            for t in range(T):
                pool.wait_ge(sem.post_sq, 8 * w + last_e[t] + 1)
                if w:
                    pool.wait_ge(sem.x_new, T * (w - 1) + t + 1)
                pool_link(nc.gpsimd.tensor_tensor(pms[:, t:t + 1], pss[:, t, 0:1], pss[:, t, 1:2], ALU.add))
                pool_link(nc.gpsimd.tensor_scalar(pms[:, t:t + 1], pms[:, t:t + 1], 1.0 / D, EPS, ALU.mult, ALU.add))
                nc.gpsimd.tensor_tensor(prstd[:, t:t + 1], pms[:, t:t + 1], neghalf[:, 0:1], ALU.pow)\
                    .then_inc(sem.post_rstd, 1)

        def post_add(dve, w, tile_half):
            dve.wait_ge(sem.postgain_in, 16 * (w + 1))
            last_e = {tile_half(e)[0]: e for e in range(8)}

            def add(t):
                dve.wait_ge(sem.post_rstd, T * w + t + 1)
                dve.wait_ge(sem.post_y, 8 * w + last_e[t] + 1)
                nc.vector.scalar_tensor_tensor(X[:, t, :], Y[:, t, :], prstd[:, t:t + 1], X[:, t, :],
                                               ALU.mult, ALU.add).then_inc(sem.x_new, 1)

            waiting = []
            for e in range(8):
                t, half = tile_half(e)
                dve.wait_ge(sem.post_sq, 8 * w + e + 1)
                nc.vector.tensor_tensor(Y[:, t, 512 * half:512 * half + 512], ps[e][:],
                                        postg[:, 512 * half:512 * half + 512], ALU.mult).then_inc(sem.post_y, 1)
                if e == last_e[t]:
                    waiting.append(t)
                if len(waiting) > 1:
                    add(waiting.pop(0))
            for t in waiting:
                add(t)

        MIX = lambda e: (e // 2, e % 2)
        MLP = lambda e: (e % 4, e // 4)

        def out_projection(pe, w, weights):
            views = [arrived(pe, n) for n in weights]
            for e in range(8):
                t, half = MIX(e)
                for k in range(KD):
                    last = nc.tensor.matmul(ps[e][:], HT[:, k, P * t:P * t + P], views[k][:, 512 * half:512 * half + 512],
                                            start=(k == 0), stop=(k == KD - 1))
                last.then_inc(sem.out_ps, 1)

        chains = {"act": 0, "dve": 0, "pool": 0}

        def dve_link(ins, eng=nc.vector):
            chains["dve"] += 1
            ins.then_inc(sem.dve_chain, 1)
            eng.wait_ge(sem.dve_chain, chains["dve"])

        def pool_link(ins, eng=nc.gpsimd):
            chains["pool"] += 1
            ins.then_inc(sem.pool_chain, 1)
            eng.wait_ge(sem.pool_chain, chains["pool"])

        def act_link(ins, eng=nc.scalar):
            chains["act"] += 1
            ins.then_inc(sem.act_chain, 1)
            eng.wait_ge(sem.act_chain, chains["act"])

        if first:
            GA, GS = carve(0, T, WIDE), carve(2048, T, WIDE)
            ZT = carve(4096, 4, SEQ)
            YP = carve(6144, T, WIDE)
            ZN = carve(8192, 2, 512)
            UT = carve(9216, G, NC)
            W1 = carve(11264, DQ, P)
            M3 = carve(13312, DQ, NK * CH)
            U8 = BIG[0:NC, 11264:11264 + G * P].rearrange("p (g n) -> p g n", g=G)
            M1 = carve(15616, DQ, L * CH)
            KT = BIG[0:CH, 15616:15616 + GQ * 240].rearrange("p (g n) -> p g n", g=GQ)
            TMP = BIG[:, 17664:17664 + 1152]
            TT = carve(18816, GQ, P)
            CC, SS_ = carve(19840, DQ, NC), carve(20864, DQ, NC)
            SA, SV = carve(21888, DQ, NC), carve(22912, DQ, NC)
            B1_, B2_ = carve(23936, DQ, CH), carve(24192, DQ, CH)
            BB, BW = carve(24448, DQ, CH), carve(24704, DQ, CH)
            C1_, C2_ = carve(24960, 2, P), carve(25216, 2, P)
            CN = carve(25472, 4, P)
            AR, AI = carve(25984, NK, DG), carve(26560, NK, DG)
            WP = BIG[:, 27136:27136 + 2 * 6 * DG].rearrange("p (a n g) -> p a n g", a=2, n=6)
            YS = BIG[:, 17664:17664 + 512]
            LAM = BIG[0:DG, 27904:28160].rearrange("p (a n) -> p a n", a=2)
            DROW = BIG[0:G, 28160:28176]
            PA = BIG[:, 13312:15616].rearrange("p (n g) -> p n g", g=DG)
            LDT = BIG[:, 28176:28240]
            CRE, CIM = BIG[:, 28240:28304], BIG[:, 28304:28368]
            DT_ = BIG[0:CH, 28368:28400]
            DK = BIG[0:CH, 28400:28528].rearrange("p (g n) -> p g n", g=GQ)
            DECAY = BIG[:, 28528:28592]
            zss, zms, zrs = BIG[:, 28592:28594], BIG[:, 28594:28596], BIG[:, 28596:28604].rearrange("p (t n) -> p t n", n=2)
            QN, KN = carve(8192, H1, SEQ), carve(10240, H1, SEQ)
            QR, V1 = carve(12288, 2, SEQ), carve(13312, T, WIDE)
            COS1, SIN1 = BIG[:, 15360:15872], BIG[:, 15872:16384]
            O1 = carve(16384, T, WIDE)
            PR1, PT1 = carve(18432, 2, SEQ), carve(19456, 2, SEQ)
            YG, GT_ = carve(20480, T, WIDE), carve(22528, 4, SEQ)
            GTMP, BGLU = carve(24576, 2, WIDE), BIG[:, 25600:26112]
            ANG, ROT = carve(26112, 2, SEQ), carve(27136, 2, SEQ)
            POS = BIG[:, 24576:25088].bitcast(I32)
            JUNK1 = BIG[:, 28160:28672]
            KRT = ZT[:, 3, :]
            JUNK_Z = BIG[:, 17664:17664 + 256]
            col = sb("col", 8)
            swap1, turn = sb("swap1", P), sb("turn", P)
            ass, ams, ars = sb("ass", 2, T), sb("ams", T), sb("ars", 2, T)

        def one_small():
            return [(col[:], a["c_col"]), (swap1[:], a["c_swap1"]), (turn[:], a["c_turn"])]

        def one_params_dma(act):
            for i, n in enumerate(("s5_lam_re", "s5_lam_im")):
                for o in range(2):
                    act.dma_start(LAM[:, i, ST * o:ST * o + ST], a[n][0].rearrange("d g p -> (d g) p"))\
                        .then_inc(sem.par_in, 16)
            act.dma_start(LDT, a["s5_log_dt"].rearrange("a d g -> a (d g)").to_broadcast([P, DG])).then_inc(sem.par_in, 16)
            act.dma_start(DROW, a["s5_d"][0].rearrange("(g h) -> g h", h=CH)).then_inc(sem.par_in, 16)

        def one_bc_dma(act, q):
            if q:
                act.wait_ge(sem.b_bar, q)
                act.wait_ge(sem.cT_ps, q)
            gs_ = slice(GQ * q, GQ * q + GQ)
            for d in range(2):
                re, im = (a[n][0, d, gs_].rearrange("g p h -> p g h") for n in ("s5_b_re", "s5_b_im"))
                for dst, parts in ((B1_, (re, im)), (B2_, (im, re))):
                    for o in range(2):
                        act.dma_start(dst[ST * o:ST * o + ST, GQ * d:GQ * d + GQ, :], parts[o]).then_inc(sem.bc_in, 16)
                re, im = (a[n][0, d, gs_].rearrange("g h p -> (g h) p") for n in ("s5_c_re", "s5_c_im"))
                for order, parts in enumerate(((re, im), (im, re))):
                    for o in range(2):
                        act.dma_start(CN[:, 2 * order + d, ST * o:ST * o + ST], parts[o]).then_inc(sem.bc_in, 16)

        N_BC = 16 * 2 * 8

        def one_pe(pe):
            pe.wait_ge(sem.par_in, 16 * 6)
            for i in range(2):
                nc.tensor.transpose(ps[6][:, DG * i:DG * i + DG], LAM[:, i, :], ident[0:DG, 0:DG])
            nc.tensor.transpose(ps[6][0:CH, P:P + G], DROW, ident[0:G, 0:G]).then_inc(sem.par_ps, 1)
            for t in range(T):
                norm_transpose(pe, 0, t)
            pe.wait_ge(sem.hT, 8)

            def natural(name, n, m, width, done):
                wv = block_of(name, pe, 512)
                for k in range(KD):
                    last = nc.tensor.matmul(ps[n % 4][:, 0:width], HT[:, k, P * m:P * m + P], wv[:, k, 0:width],
                                            start=(k == 0), stop=(k == KD - 1))
                last.then_inc(done, 1)

            for m in range(T):
                natural("u", m, m, 512, sem.u_ps)
            for m in range(T):
                pe.wait_ge(sem.u_sb, m + 1)
                natural("gs", m, m, 512, sem.gs_ps)
            pe.wait_ge(sem.par, 1)
            for b in range(4):
                for g in range(8):
                    last = nc.tensor.transpose(ps[4 + b][:, NC * g:NC * g + NC], U8[:, 8 * b + g, :], ident[0:NC, 0:NC])
                last.then_inc(sem.uT_ps, 1)
            for m in range(T):
                pe.wait_ge(sem.gs, m + 1)
                natural("za", m, m, 448, sem.za_ps)
            for m in range(T):
                pe.wait_ge(sem.zn, m + 1)
                natural("ga", m, m, 512, sem.ga_ps)
                pe.wait_ge(sem.uT, m + 1)
                for k in range(4):
                    last = nc.tensor.transpose(ps[4 + m][:, P * k:P * k + P], ZN[:, m % 2, P * k:P * k + P], ident[:])
                last.then_inc(sem.znT_ps, 1)
            pe.wait_ge(sem.ga, T)
            pe.wait_ge(sem.znT, T)
            for q in range(NQ):
                s5_pe(pe, q)
            glu_pe(pe)
            latent_pe(pe)
            attention_pe(pe)
            mix_pe(pe)

        def s5_pe(pe, q):
            pe.wait_ge(sem.bc_in, N_BC * (q + 1))
            if q:
                pe.wait_ge(sem.yp, 2 * q)
            for j in range(4):
                last = nc.tensor.transpose(ps[4][:, P * j:P * j + P], CN[:, j, :], ident[:])
            last.then_inc(sem.cT_ps, 1)
            pe.wait_ge(sem.m1, q + 1)
            if q:
                pe.wait_ge(sem.y_sb, q)
                pe.wait_ge(sem.turned, 4 * q)
            for b in range(4):
                for j in range(4):
                    last = nc.tensor.transpose(ps[b][:, P * j:P * j + P], M1[:, 4 * b + j, :], ident[:])
                last.then_inc(sem.m1T_ps, 1)
            pe.wait_ge(sem.m3, q + 1)
            pe.wait_ge(sem.cT, q + 1)
            pe.wait_ge(sem.b_bar, q + 1)
            if q:
                pe.wait_ge(sem.taps, q)
            for b in range(2):
                for j in range(4):
                    g = 4 * b + j
                    lo = ps[4 + b][0:CH, P * j:P * j + P]
                    nc.tensor.matmul(lo, BB[:, GQ + g, :], M3[:, GQ + g, CH:NK * CH], start=True, stop=True)
                    nc.tensor.matmul(lo[:, P - CH:P], BB[:, g, :], M3[:, g, 0:CH], start=False, stop=True,
                                     skip_group_check=True)
                    last = nc.tensor.matmul(ps[6 + b][0:CH, 112 * j:112 * j + 112], BB[:, g, :], M3[:, g, CH:L * CH],
                                            start=True, stop=True)
                last.then_inc(sem.tap_ps, 1)
            pe.wait_ge(sem.w1T, 4 * (q + 1))
            for d in range(2):
                for g in range(GQ):
                    u = UT[:, GQ * q + g, :]
                    last = nc.tensor.matmul(ps[d][:, NC * g:NC * g + NC], W1[:, GQ * d + g, :], u[:, ::-1] if d else u,
                                            start=True, stop=True)
                last.then_inc(sem.st_ps, 1)
            for r in range(2):
                for d in range(2):
                    if r == 0:
                        pe.wait_ge(sem.st_sb, 2 * q + d + 1)
                    else:
                        pe.wait_ge(sem.state, 3 * q + d + 1)
                        pe.wait_ge(sem.turned, 4 * q + d + 1)
                    nc.tensor.matmul(ps[2 + d][:], turn[:], SA[:, GQ * d:GQ * d + GQ, :].rearrange("p g c -> p (g c)"),
                                     start=True, stop=True).then_inc(sem.turn_ps, 1)
            pe.wait_ge(sem.toep, 128 * (q + 1))
            pe.wait_ge(sem.state, 3 * q + 3)
            for g in range(GQ):
                y = ps[0][:, NC * g:NC * g + NC]
                nc.tensor.matmul(y, TT[:, g, :], UT[:, GQ * q + g, :], start=True, stop=True)
                nc.tensor.matmul(y[:, 1:NC], M3[:, g, CH:NK * CH], SV[:, g, 0:NC - 1], start=False, stop=True,
                                 skip_group_check=True)
                last = nc.tensor.matmul(y[:, 0:NC - 1], M3[:, GQ + g, 0:L * CH], SV[:, GQ + g, 0:NC - 1][:, ::-1],
                                        start=False, stop=True, skip_group_check=True)
            last.then_inc(sem.y_ps, 1)
            pe.wait_ge(sem.y_sb, q + 1)
            pe.wait_ge(sem.taps, q + 1)
            for b in range(2):
                for j in range(4):
                    g = 4 * b + j
                    last = nc.tensor.transpose(ps[4 + b][0:NC, P * j:P * j + P], YS[:, NC * g:NC * g + NC], ident[:])
                last.then_inc(sem.yT_ps, 1)

        def glu_pe(pe):
            pe.wait_ge(sem.ge, 1)
            pe.wait_ge(sem.yp, 2 * NQ)
            pe.wait_ge(sem.y_sb, NQ)
            pe.wait_ge(sem.turned, 4 * NQ)
            for m in range(T):
                for k in range(4):
                    last = nc.tensor.transpose(ps[m][:, P * k:P * k + P], YG[:, m, P * k:P * k + P], ident[:])
                last.then_inc(sem.geT_ps, 1)
            wv = block_of("glu", pe, 512)
            for m in range(T):
                pe.wait_ge(sem.geT, m + 1)
                for k in range(4):
                    last = nc.tensor.matmul(ps[4 + m][:], GT_[:, k, P * m:P * m + P], wv[:, k, :], start=(k == 0), stop=(k == 3))
                last.then_inc(sem.glu_ps, 1)

        def latent_pe(pe):
            wq = arrived(pe, "uq")
            for h in range(H1):
                pe.wait_ge(sem.geT, h + 1)
                for k in range(2):
                    last = nc.tensor.matmul(ps[h][:], wq[:, 768 * k + P * h:768 * k + P * h + P], ZT[:, k, :],
                                            start=(k == 0), stop=(k == 1))
                last.then_inc(sem.qn_ps, 1)
            for r in range(2):
                pe.wait_ge(sem.glu_x, r + 1)
                for k in range(2):
                    c = 768 * k + 512 + P * r
                    last = nc.tensor.matmul(ps[4 + r][:], wq[:, c:c + P], ZT[:, k, :], start=(k == 0), stop=(k == 1))
                last.then_inc(sem.rq_ps, 1)
            wk = arrived(pe, "ukv")
            for h in range(H1):
                pe.wait_ge(sem.qn, h + 1)
                nc.tensor.matmul(ps[h][:], wk[:, 256 * h:256 * h + P], ZT[:, 2, :], start=True, stop=True).then_inc(sem.kn_ps, 1)
            for r in range(3):
                b = 6 + r % 2
                if r == 0:
                    pe.wait_ge(sem.glu_x, 4)
                else:
                    pe.wait_ge(sem.rq, r)
                if r == 2:
                    pe.wait_ge(sem.rope_done, 1)
                nc.tensor.matmul(ps[b][:], swap1[:], KRT if r == 0 else QR[:, r - 1, :], start=True, stop=True)\
                    .then_inc(sem.rope_ps, 1)
            wvv = wk.rearrange("p (h c) -> p h c", h=H1)[:, :, NOPE:NOPE + VD]
            for m in range(T):
                pe.wait_ge(sem.kn, m + 1)
                nc.tensor.matmul(ps[m][:], ZT[:, 2, P * m:P * m + P], wvv, start=True, stop=True).then_inc(sem.v1_ps, 1)

        NU1 = H1 * T

        def attention_pe(pe):
            pe.wait_ge(sem.v1, T)
            pe.wait_ge(sem.rope_done, 3)
            pe.wait_ge(sem.rq, 2)
            pe.wait_ge(sem.qn, H1)
            pe.wait_ge(sem.kn, H1)
            for u in range(NU1 + 4):
                if u < NU1:
                    h, m = u // T, u % T
                    if u >= 3:
                        pe.wait_ge(sem.a_exp, u - 2)
                    tok = slice(P * m, P * m + P)
                    nc.tensor.matmul(ps[u % 3][:], QN[:, h, tok], KN[:, h, :], start=True, stop=False)
                    o = 64 * (h % 2)
                    nc.tensor.matmul(ps[u % 3][:], QR[o:o + 64, h // 2, tok], KRT[o:o + 64, :], start=False, stop=True)\
                        .then_inc(sem.a_s_ps, 1)
                w = u - 2
                if 0 <= w < NU1:
                    pe.wait_ge(sem.a_exp, w + 1)
                    if w >= 2:
                        pe.wait_ge(sem.a_pT, w - 1)
                    for b in range(T):
                        last = nc.tensor.transpose(ps[3 + w % 2][:, P * b:P * b + P], PR1[:, w % 2, P * b:P * b + P], ident[:])
                    last.then_inc(sem.a_pT_ps, 1)
                w = u - 3
                if 0 <= w < NU1:
                    h, m = w // T, w % T
                    pe.wait_ge(sem.a_pT, w + 1)
                    if m == 0 and h >= 2:
                        pe.wait_ge(sem.a_o, h - 1)
                    for b in range(T):
                        last = nc.tensor.matmul(ps[5 + h % 2][:, P * m:P * m + P], PT1[:, w % 2, P * b:P * b + P],
                                                V1[:, b, P * h:P * h + P], start=(b == 0), stop=(b == T - 1))
                    last.then_inc(sem.a_o_ps, 1)

        def mix_pe(pe):
            for i in range(8):
                m = i % 4
                if i < 4:
                    pe.wait_ge(sem.ssm_o, m + 1)
                    src = YG[:, m, :]
                else:
                    pe.wait_ge(sem.at_o, m + 1)
                    src = O1[:, m, :]
                if i == 0:
                    pe.wait_ge(sem.a_o, H1)
                for k in range(4):
                    last = nc.tensor.transpose(ps[i][:, P * k:P * k + P], src[:, P * k:P * k + P], ident[:])
                last.then_inc(sem.m1ix_ps, 1)
            pe.wait_ge(sem.m1ix, 8)
            out_projection(pe, 0, [f"wo{k}" for k in range(KD)])

        TT2 = nc.vector.tensor_tensor
        TS = nc.vector.tensor_scalar

        def reduce_angle(x, t1, t2):
            dve_link(TS(t1, x, 1.0 / TWO_PI, ROUND, ALU.mult, ALU.add))
            dve_link(TS(t1, t1, ROUND, None, ALU.subtract))
            for part in (PI2_A, PI2_B, PI2_C):
                dve_link(nc.vector.scalar_tensor_tensor(x, t1, -part, x, ALU.mult, ALU.add))
            dve_link(TS(t1, x, PI_SAFE, -PI_SAFE, ALU.min, ALU.max))
            dve_link(TS(t2, t1, -1.0, None, ALU.mult))
            dve_link(TT2(t2, t2, t1, ALU.max))
            return TS(t2, t2, -1.0, float(np.float32(np.pi / 2)), ALU.mult, ALU.add)

        def cmul(out_c, out_s, ac, as_, bc, bs, t1, t2):
            TT2(t1, as_, bs, ALU.mult)
            TT2(t2, as_, bc, ALU.mult)
            TT2(out_c, ac, bc, ALU.mult)
            dve_link(TT2(out_s, ac, bs, ALU.mult))
            TT2(out_c, out_c, t1, ALU.subtract)
            dve_link(TT2(out_s, out_s, t2, ALU.add))

        def one_params(dve):
            LR, LI, TH, ER, SN, CS_, DEN, T1, T2 = (PA[:, i, :] for i in range(9))
            UC, US, EA = PA[:, 9:18, :], PA[:, 18:27, :], PA[:, 27:36, :]
            dve.wait_ge(sem.par_ps, 1)
            TS(LR, ps[6][:, 0:DG], -1e-4, None, ALU.min)
            nc.vector.tensor_copy(LI, ps[6][:, DG:2 * DG])
            dve_link(nc.vector.tensor_copy(DT_, ps[6][0:CH, P:P + G]))
            dve.wait_ge(sem.dt_e, 1)
            dve_link(TT2(TH, LI, LDT, ALU.mult))
            TT2(ER, LR, LDT, ALU.mult).then_inc(sem.par_exp, 1)
            reduce_angle(TH, T1, T2).then_inc(sem.par_exp, 1)
            dve.wait_ge(sem.par_trig, 2)
            dve.wait_ge(sem.amp, NK)
            dve_link(TT2(T1, CS_, EA[:, 1, :], ALU.mult))
            TT2(T2, SN, EA[:, 1, :], ALU.mult)
            dve_link(TS(T1, T1, 1.0, None, ALU.subtract))
            TT2(CRE, T1, LR, ALU.mult)
            TT2(CIM, T2, LR, ALU.mult)
            dve_link(TT2(T1, T1, LI, ALU.mult))
            dve_link(TT2(T2, T2, LI, ALU.mult))
            dve_link(TT2(CRE, CRE, T2, ALU.add))
            dve_link(TT2(CIM, CIM, T1, ALU.subtract))
            dve_link(TT2(T1, LR, LR, ALU.mult))
            dve_link(TT2(DEN, LI, LI, ALU.mult))
            dve_link(TT2(DEN, DEN, T1, ALU.add))
            dve_link(nc.vector.reciprocal(DEN, DEN))
            dve_link(TT2(CRE, CRE, DEN, ALU.mult))
            dve_link(TT2(CIM, CIM, DEN, ALU.mult))
            dve_link(TS(CIM, CIM, col[:, 2:3], None, ALU.mult))
            nc.vector.memset(UC[:, 0, :], 1.0)
            nc.vector.memset(US[:, 0, :], 0.0)
            nc.vector.tensor_copy(UC[:, 1, :], CS_)
            dve_link(nc.vector.tensor_copy(US[:, 1, :], SN))
            n = 1
            while n < L:
                b = lambda v: v[:, n:n + 1, :].to_broadcast([P, n, DG])
                t1, t2 = TMP[:, 0:n * DG].rearrange("p (n g) -> p n g", g=DG), TMP[:, 512:512 + n * DG].rearrange("p (n g) -> p n g", g=DG)
                cmul(UC[:, n + 1:2 * n + 1, :], US[:, n + 1:2 * n + 1, :], UC[:, 1:n + 1, :], US[:, 1:n + 1, :], b(UC), b(US), t1, t2)
                n *= 2
            TT2(AR, UC, EA, ALU.mult)
            dve_link(TT2(AI, US, EA, ALU.mult))
            nc.vector.tensor_copy(DECAY, EA[:, L, :])
            nc.vector.tensor_copy(WP[:, 0, 0, :], UC[:, L, :])
            dve_link(nc.vector.tensor_copy(WP[:, 1, 0, :], US[:, L, :]))
            for n in range(5):
                c, s = WP[:, 0, n, :], WP[:, 1, n, :]
                cmul(WP[:, 0, n + 1, :], WP[:, 1, n + 1, :], c, s, c, s, TMP[:, 0:DG], TMP[:, DG:2 * DG])
            nc.vector.tensor_copy(T1, T1).then_inc(sem.par, 1)
            dve.wait_ge(sem.par, 1)

        def by_group(v, q, d):
            return v[:, :, G * d + GQ * q:G * d + GQ * q + GQ].rearrange("p k g -> p g k")

        def s5_prepare(dve, q):
            def pg(v, width):
                w = v.rearrange("p (d g) -> p d g", d=2)[:, :, GQ * q:GQ * q + GQ]
                return w[:, :, :, None].to_broadcast([P, 2, GQ, width])

            four = lambda v: v.rearrange("p (d g) n -> p d g n", d=2)
            if q:
                dve.wait_ge(sem.state, 3 * q)
            nc.vector.memset(CC[:, :, 0:1], 1.0)
            dve_link(nc.vector.memset(SS_[:, :, 0:1], 0.0))
            for s in range(6):
                n = 2 ** s
                t = TMP[:, 0:DQ * n].rearrange("p (d g n) -> p d g n", d=2, n=n)
                t2 = four(SA)[:, :, :, 0:n]
                wc, ws = pg(WP[:, 0, s, :], n), pg(WP[:, 1, s, :], n)
                cmul(four(CC)[:, :, :, n:2 * n], four(SS_)[:, :, :, n:2 * n], four(CC)[:, :, :, 0:n], four(SS_)[:, :, :, 0:n],
                     wc, ws, t, t2)
            dve.wait_ge(sem.bc_in, N_BC * (q + 1))
            if q:
                dve.wait_ge(sem.tap_ps, 2 * q)
            t = TMP[:, 0:DQ * CH].rearrange("p (d g n) -> p d g n", d=2, n=CH)
            t2 = TMP[:, 512:512 + DQ * CH].rearrange("p (d g n) -> p d g n", d=2, n=CH)
            TT2(four(BB), pg(CRE, CH), four(B1_), ALU.mult)
            TT2(t, pg(CIM, CH), four(B2_), ALU.mult)
            TT2(four(BW), pg(CRE, CH), four(B2_), ALU.mult)
            dve_link(TT2(t2, pg(CIM, CH), four(B1_), ALU.mult))
            TT2(four(BB), four(BB), t, ALU.add)
            TT2(four(BW), four(BW), t2, ALU.subtract).then_inc(sem.b_bar, 1)
            dve.wait_ge(sem.b_bar, q + 1)
            if q:
                dve.wait_ge(sem.toep, 128 * q)
            for d in range(2):
                step = slice(L - 1, None, -1) if d == 0 else slice(0, L)
                m = M1[:, GQ * d:GQ * d + GQ, :].rearrange("p g (k n) -> p g k n", n=CH)
                t = TMP[:, 0:GQ * P].rearrange("p (g k n) -> p g k n", g=GQ, n=CH)
                ar = by_group(AR, q, d)[:, :, step][:, :, :, None].to_broadcast([P, GQ, L, CH])
                ai = by_group(AI, q, d)[:, :, step][:, :, :, None].to_broadcast([P, GQ, L, CH])
                bb = BB[:, GQ * d:GQ * d + GQ, None, :].to_broadcast([P, GQ, L, CH])
                bw = BW[:, GQ * d:GQ * d + GQ, None, :].to_broadcast([P, GQ, L, CH])
                TT2(m, ar, bb, ALU.mult)
                dve_link(TT2(t, ai, bw, ALU.mult))
                last = nc.vector.scalar_tensor_tensor(
                    M1[:, GQ * d:GQ * d + GQ, :].rearrange("p g n -> p (g n)"), TMP[:, 0:GQ * P], col[:, 2:3],
                    M1[:, GQ * d:GQ * d + GQ, :].rearrange("p g n -> p (g n)"), ALU.mult, ALU.add)
                if d == 0:
                    dve_link(last)
            last.then_inc(sem.m1, 1)
            dve.wait_ge(sem.m1, q + 1)
            dve.wait_ge(sem.cT_ps, q + 1)
            TS(C1_.rearrange("p a n -> p (a n)"), ps[4][:, 0:256], col[:, 2:3], -1.0, ALU.mult, ALU.mult)
            TS(C2_.rearrange("p a n -> p (a n)"), ps[4][:, 256:512], -1.0, None, ALU.mult).then_inc(sem.cT, 1)
            dve.wait_ge(sem.cT, q + 1)
            if q:
                dve.wait_ge(sem.y_ps, q)
            for d in range(2):
                step = slice(0, NK) if d == 0 else slice(NK - 1, None, -1)
                m = M3[:, GQ * d:GQ * d + GQ, :].rearrange("p g (k n) -> p g k n", n=CH)
                t = TMP[:, 0:GQ * NK * CH].rearrange("p (g k n) -> p g k n", g=GQ, n=CH)
                ar = by_group(AR, q, d)[:, :, step][:, :, :, None].to_broadcast([P, GQ, NK, CH])
                ai = by_group(AI, q, d)[:, :, step][:, :, :, None].to_broadcast([P, GQ, NK, CH])
                c1 = C1_[:, d, :].rearrange("p (g n) -> p g n", g=GQ)[:, :, None, :].to_broadcast([P, GQ, NK, CH])
                c2 = C2_[:, d, :].rearrange("p (g n) -> p g n", g=GQ)[:, :, None, :].to_broadcast([P, GQ, NK, CH])
                TT2(m, ar, c1, ALU.mult)
                dve_link(TT2(t, ai, c2, ALU.mult))
                last = TT2(m, m, t, ALU.add)
                if d == 0:
                    dve_link(last)
            last.then_inc(sem.m3, 1)
            dve.wait_ge(sem.m3, q + 1)

        def s5_main(dve, q):
            for b in range(2):
                dve.wait_ge(sem.tap_ps, 2 * q + b + 1)
                r = slice(4 * b, 4 * b + 4)
                if b == 0:
                    dve.wait_ge(sem.m1T_ps, 4 * (q + 1))
                nc.vector.tensor_copy(KT[:, r, 0:P], ps[4 + b][0:CH, :].rearrange("p (g n) -> p g n", g=4))
                dve_link(nc.vector.tensor_copy(KT[:, r, P:P + 112], ps[6 + b][0:CH, 0:448].rearrange("p (g n) -> p g n", g=4)))
            dve_link(TT2(DK, ident[0:CH, None, 0:CH].to_broadcast([CH, GQ, CH]),
                         DT_[:, GQ * q:GQ * q + GQ, None].to_broadcast([CH, GQ, CH]), ALU.mult))
            TT2(KT[:, :, P - CH:P], KT[:, :, P - CH:P], DK, ALU.add).then_inc(sem.taps, 1)
            flat = lambda v, d: v[:, GQ * d:GQ * d + GQ, :].rearrange("p g c -> p (g c)")
            for d in range(2):
                dve.wait_ge(sem.st_sb, 2 * q + d + 1)
                TT2(flat(SV, d), flat(CC, d), flat(SA, d), ALU.mult)
                dve.wait_ge(sem.turn_ps, 4 * q + d + 1)
                dve_link(TT2(ps[2 + d][:], ps[2 + d][:], flat(SS_, d), ALU.mult))
                TT2(flat(SV, d), flat(SV, d), ps[2 + d][:], ALU.add).then_inc(sem.turned, 1)
                dve.wait_ge(sem.turned, 4 * q + d + 1)
                for g in range(GQ):
                    dg = G * d + GQ * q + g
                    last = nc.vector.tensor_tensor_scan(SA[:, GQ * d + g, :], DECAY[:, dg:dg + 1].to_broadcast([P, NC]),
                                                        SV[:, GQ * d + g, :], 0.0, ALU.mult, ALU.add)
                last.then_inc(sem.state, 1)
            for d in range(2):
                dve.wait_ge(sem.state, 3 * q + d + 1)
                dve.wait_ge(sem.turn_ps, 4 * q + d + 3)
                TT2(flat(SV, d), flat(CC, d), flat(SA, d), ALU.mult)
                dve_link(TT2(ps[2 + d][:], ps[2 + d][:], flat(SS_, d), ALU.mult))
                TT2(flat(SV, d), flat(SV, d), ps[2 + d][:], ALU.subtract).then_inc(sem.turned, 1)
                dve.wait_ge(sem.turned, 4 * q + d + 3)
            nc.vector.tensor_copy(DK[:, 0, 0:1], DK[:, 0, 0:1]).then_inc(sem.state, 1)
            for b in range(2):
                dve.wait_ge(sem.yT_ps, 2 * q + b + 1)
                src = ps[4 + b][0:NC, :].rearrange("p (g m i n) -> p i m g n", g=4, m=T, i=2)
                for i in range(2):
                    c = CH * (GQ * q + 4 * b)
                    dst = YP[NC * i:NC * i + NC, :, c:c + 4 * CH].rearrange("p m (g n) -> p m g n", g=4)
                    last = nc.vector.tensor_copy(dst, src[:, i, :, :, :])
                last.then_inc(sem.yp, 1)

        def one_dve(dve):
            one_params(dve)
            norm_dve(dve, 0, chunked=True)
            for b in range(4):
                dve.wait_ge(sem.uT_ps, b + 1)
                nc.vector.tensor_copy(UT[:, 8 * b:8 * b + 8, :], ps[4 + b][:].rearrange("p (g c) -> p g c", g=8)).then_inc(sem.uT, 1)
            for m in range(T):
                dve.wait_ge(sem.za_rstd, m + 1)
                if m >= 2:
                    dve.wait_ge(sem.znT_ps, m - 1)
                z = ZN[:, m % 2, :]
                TS(z[:, 0:256], ps[m][:, 0:256], zrs[:, m, 0:1], None, ALU.mult)
                TS(z[:, 256:384], ps[m][:, 256:384], zrs[:, m, 1:2], None, ALU.mult)
                nc.vector.tensor_copy(z[:, 384:448], ps[m][:, 384:448])
                nc.vector.tensor_copy(z[:, 448:512], ps[m][:, 384:448]).then_inc(sem.zn, 1)
                if m >= 1:
                    znT_copy(dve, m - 1)
            znT_copy(dve, T - 1)
            for q in range(NQ):
                s5_prepare(dve, q)
                s5_main(dve, q)
            for m in range(T):
                dve.wait_ge(sem.geT_ps, m + 1)
                nc.vector.tensor_copy(GT_[:, :, P * m:P * m + P], ps[m][:].rearrange("p (k n) -> p k n", k=4)).then_inc(sem.geT, 1)
            dve.wait_ge(sem.pos_in, 16)
            dve.wait_ge(sem.bglu_in, 16)
            ang = ANG[:, 0, :]
            dve_link(nc.vector.tensor_copy(ANG[:, 1, :].rearrange("p (i c) -> p i c", i=L), POS.rearrange("p (c i) -> p i c", i=L)))
            dve_link(TS(ang, ANG[:, 1, :], col[:, 0:1], None, ALU.mult))
            reduce_angle(ang, ROT[:, 0, :], ROT[:, 1, :]).then_inc(sem.angle, 1)
            dve.wait_ge(sem.trig, 2)
            TS(SIN1, SIN1, col[:, 1:2], None, ALU.mult).then_inc(sem.rope_tab, 1)
            dve.wait_ge(sem.rope_tab, 1)
            for m in range(T):
                dve.wait_ge(sem.glu_ps, m + 1)
                if m >= 2:
                    dve.wait_ge(sem.glu_y, m - 1)
                TT2(GTMP[:, m % 2, :], ps[4 + m][:], BGLU, ALU.add).then_inc(sem.glu_x, 1)
                if m >= 1:
                    glu_gate(dve, m - 1)
            glu_gate(dve, T - 1)
            for r in range(3):
                raw = KRT if r == 0 else QR[:, r - 1, :]
                b = 6 + r % 2
                dve.wait_ge(sem.rope_ps, r + 1)
                TT2(ROT[:, r % 2, :], raw, COS1, ALU.mult)
                dve_link(TT2(ps[b][:], ps[b][:], SIN1, ALU.mult))
                TT2(raw, ROT[:, r % 2, :], ps[b][:], ALU.add).then_inc(sem.rope_done, 1)
            for m in range(T):
                dve.wait_ge(sem.mixer_rstd, m + 1)
                nc.vector.scalar_tensor_tensor(YG[:, m, :], YG[:, m, :], ars[:, 0, m:m + 1], GS[:, m, :], ALU.mult, ALU.mult)\
                    .then_inc(sem.ssm_o, 1)
            for u in range(NU1 + 4):
                if u < NU1:
                    dve.wait_ge(sem.a_s_ps, u + 1)
                    if u >= 4:
                        dve.wait_ge(sem.a_exp, u - 3)
                    nc.vector.tensor_reduce(mn[:, u % 4:u % 4 + 1], ps[u % 3][:], AX_X, ALU.min).then_inc(sem.a_min, 1)
                z = u - 2
                if 0 <= z < NU1:
                    dve.wait_ge(sem.a_pT_ps, z + 1)
                    if z >= 2:
                        dve.wait_ge(sem.a_o_ps, z - 1)
                    nc.vector.tensor_copy(PT1[:, z % 2, :], ps[3 + z % 2][:]).then_inc(sem.a_pT, 1)
                z = u - 4
                if z >= 0 and z % 4 == 3:
                    h = z // 4
                    dve.wait_ge(sem.a_exp, z + 1)
                    r = rg[:, h % 3, :]
                    dve_link(nc.vector.reciprocal(r, rs[:, 4 * h:4 * h + 4]))
                    dve.wait_ge(sem.a_o_ps, z + 1)
                    for m in range(T):
                        last = TS(O1[:, m, P * h:P * h + P], ps[5 + h % 2][:, P * m:P * m + P], r[:, m:m + 1], None, ALU.mult)
                    last.then_inc(sem.a_o, 1)
            for m in range(T):
                mix1_copy(dve, m, m, R_SO, 4)
            for m in range(T):
                dve.wait_ge(sem.mixer_rstd, T + m + 1)
                nc.vector.scalar_tensor_tensor(O1[:, m, :], O1[:, m, :], ars[:, 1, m:m + 1], GA[:, m, :], ALU.mult, ALU.mult)\
                    .then_inc(sem.at_o, 1)
            for m in range(T):
                mix1_copy(dve, 4 + m, m, R_AO, 0)
            post_add(dve, 0, MIX)

        def mix1_copy(dve, i, m, row, k0):
            dve.wait_ge(sem.m1ix_ps, i + 1)
            dst = HT[:, k0:k0 + 4, :].rearrange("p k (c i) -> p k i c", i=L)[:, :, 2 * m:2 * m + 2, :]
            for k in range(4):
                last = TS(dst[:, k, :, :], ps[i][:, P * k:P * k + P].rearrange("p (i c) -> p i c", i=2),
                          cols[:, row + k:row + k + 1], None, ALU.mult)
            last.then_inc(sem.m1ix, 1)

        def znT_copy(dve, m):
            dve.wait_ge(sem.znT_ps, m + 1)
            src = ps[4 + m][:].rearrange("p (k n) -> p k n", k=4)
            TT2(ZT[:, 0:3, P * m:P * m + P], src[:, 0:3, :], cols[:, R_QN:R_QN + 3, None].to_broadcast([P, 3, P]), ALU.mult)
            nc.vector.tensor_copy(ZT[:, 3, P * m:P * m + P], src[:, 3, :]).then_inc(sem.znT, 1)

        def glu_gate(dve, m):
            dve.wait_ge(sem.glu_s, m + 1)
            TT2(YG[:, m, :], YG[:, m, :], GTMP[:, m % 2, :], ALU.mult).then_inc(sem.glu_y, 1)

        def one_act(act, post_gain):
            one_params_dma(act)
            one_bc_dma(act, 0)
            act.wait_ge(sem.par_in, 16 * 6)
            nc.scalar.activation(LDT, LDT, ACT.Exp).then_inc(sem.dt_e, 1)
            EA, CS_, SN, T1, T2, ER = PA[:, 27:36, :], PA[:, 5, :], PA[:, 4, :], PA[:, 7, :], PA[:, 8, :], PA[:, 3, :]
            act.wait_ge(sem.par_exp, 1)
            for k in range(NK):
                nc.scalar.activation(EA[:, k, :], ER, ACT.Exp, scale=float(k)).then_inc(sem.amp, 1)
            act.wait_ge(sem.par_exp, 2)
            nc.scalar.activation(SN, T1, ACT.Sin).then_inc(sem.par_trig, 1)
            nc.scalar.activation(CS_, T2, ACT.Sin).then_inc(sem.par_trig, 1)
            norm_squares(act, 0, lambda t: x_tile(-1, t))
            post_gain(0, a["post_norm_g"])
            act.wait_ge(sem.par, 1)
            for m in range(T):
                act.wait_ge(sem.u_ps, m + 1)
                for i in range(2):
                    dst = U8[:, :, CH * (2 * m + i):CH * (2 * m + i) + CH]
                    last = nc.scalar.activation(dst, ps[m][NC * i:NC * i + NC, :].rearrange("p (g n) -> p g n", g=G), ACT.Copy)
                last.then_inc(sem.u_sb, 1)
            for m in range(T):
                act.wait_ge(sem.gs_ps, m + 1)
                nc.scalar.activation(GS[:, m, :], ps[m][:], ACT.Silu).then_inc(sem.gs, 1)
            for m in range(T):
                act.wait_ge(sem.za_ps, m + 1)
                if m:
                    act.wait_ge(sem.za_rstd, m)
                act_link(nc.scalar.activation(JUNK_Z[:, 0:256], ps[m][:, 0:256], ACT.Square, accum_out=zss[:, 0:1]))
                nc.scalar.activation(JUNK_Z[:, 0:128], ps[m][:, 256:384], ACT.Square, accum_out=zss[:, 1:2]).then_inc(sem.za_sq, 1)
                if m < T - 1:
                    act.wait_ge(sem.za_sq, m + 1)
            for m in range(T):
                act.wait_ge(sem.ga_ps, m + 1)
                nc.scalar.activation(GA[:, m, :], ps[m][:], ACT.Silu).then_inc(sem.ga, 1)
            for q in range(NQ):
                for b in range(4):
                    act.wait_ge(sem.m1T_ps, 4 * q + b + 1)
                    if b == 0:
                        act.wait_ge(sem.uT_ps, 4)
                        if q:
                            act.wait_ge(sem.st_ps, 2 * q)
                    nc.scalar.activation(W1[:, 4 * b:4 * b + 4, :], ps[b][:].rearrange("p (g n) -> p g n", g=4), ACT.Copy)\
                        .then_inc(sem.w1T, 1)
                act.wait_ge(sem.taps, q + 1)
                if q:
                    act.wait_ge(sem.y_ps, q)
                for i in range(L):
                    c = CH * (L - 1 - i)
                    act.dma_start(TT[CH * i:CH * i + CH, :, :], KT[:, :, c:c + P]).then_inc(sem.toep, 16)
                if q + 1 < NQ:
                    one_bc_dma(act, q + 1)
                for d in range(2):
                    act.wait_ge(sem.st_ps, 2 * q + d + 1)
                    nc.scalar.activation(SA[:, GQ * d:GQ * d + GQ, :], ps[d][:].rearrange("p (g c) -> p g c", g=GQ), ACT.Copy)\
                        .then_inc(sem.st_sb, 1)
                act.wait_ge(sem.y_ps, q + 1)
                nc.scalar.activation(YS, ps[0][:], ACT.Copy).then_inc(sem.y_sb, 1)
            act.wait_ge(sem.yp, 2 * NQ)
            nc.scalar.activation(YG, YP, ACT.Gelu_apprx_tanh).then_inc(sem.ge, 1)
            act.wait_ge(sem.state, 3 * NQ)
            act.dma_start(POS, a["positions"].to_broadcast([P, SEQ])).then_inc(sem.pos_in, 16)
            act.dma_start(BGLU, a["b_glu"].to_broadcast([P, WIDE])).then_inc(sem.bglu_in, 16)
            act.wait_ge(sem.angle, 1)
            nc.scalar.activation(SIN1, ROT[:, 0, :], ACT.Sin).then_inc(sem.trig, 1)
            nc.scalar.activation(COS1, ROT[:, 1, :], ACT.Sin).then_inc(sem.trig, 1)
            for m in range(T):
                act.wait_ge(sem.glu_x, m + 1)
                nc.scalar.activation(GTMP[:, m % 2, :], GTMP[:, m % 2, :], ACT.Sigmoid).then_inc(sem.glu_s, 1)
            for h in range(H1):
                act.wait_ge(sem.qn_ps, h + 1)
                nc.scalar.activation(QN[:, h, :], ps[h][:], ACT.Copy, scale=-SCALE1).then_inc(sem.qn, 1)
            for r in range(2):
                act.wait_ge(sem.rq_ps, r + 1)
                nc.scalar.activation(QR[:, r, :], ps[4 + r][:], ACT.Copy, scale=-SCALE1).then_inc(sem.rq, 1)
            for h in range(H1):
                act.wait_ge(sem.kn_ps, h + 1)
                nc.scalar.activation(KN[:, h, :], ps[h][:], ACT.Copy).then_inc(sem.kn, 1)
            for m in range(T):
                act.wait_ge(sem.v1_ps, m + 1)
                nc.scalar.activation(V1[:, m, :], ps[m][:], ACT.Copy).then_inc(sem.v1, 1)
            for m in range(T):
                act.wait_ge(sem.glu_y, m + 1)
                if m:
                    act.wait_ge(sem.mixer_sq, m)
                nc.scalar.activation(JUNK1, YG[:, m, :], ACT.Square, accum_out=ass[:, 0, m:m + 1]).then_inc(sem.mixer_sq, 1)
            for u in range(NU1):
                act.wait_ge(sem.a_min, u + 1)
                if u >= 2:
                    act.wait_ge(sem.a_pT_ps, u - 1)
                nc.scalar.activation(PR1[:, u % 2, :], ps[u % 3][:], ACT.Exp, bias=mn[:, u % 4:u % 4 + 1], scale=-1.0,
                                     accum_out=rs[:, u:u + 1]).then_inc(sem.a_exp, 1)
            for m in range(T):
                act.wait_ge(sem.a_o, H1)
                act.wait_ge(sem.mixer_sq, T + m)
                nc.scalar.activation(JUNK1, O1[:, m, :], ACT.Square, accum_out=ass[:, 1, m:m + 1]).then_inc(sem.mixer_sq, 1)
            post_squares(act, 0, MIX)

        def one_pool(pool):
            norm_rstd(pool, 0)
            for m in range(T):
                pool.wait_ge(sem.za_sq, m + 1)
                pool_link(nc.gpsimd.tensor_scalar(zms[:, 0:1], zss[:, 0:1], 1.0 / Q_RANK, EPS, ALU.mult, ALU.add))
                pool_link(nc.gpsimd.tensor_scalar(zms[:, 1:2], zss[:, 1:2], 1.0 / KV_RANK, EPS, ALU.mult, ALU.add))
                nc.gpsimd.tensor_tensor(zrs[:, m, :], zms, neghalf[:, 0:2], ALU.pow).then_inc(sem.za_rstd, 1)
            for o in range(2):
                for m in range(T):
                    pool.wait_ge(sem.mixer_sq, T * o + m + 1)
                    pool_link(nc.gpsimd.tensor_scalar(ams[:, m:m + 1], ass[:, o, m:m + 1], 1.0 / WIDE, EPS, ALU.mult, ALU.add))
                    nc.gpsimd.tensor_tensor(ars[:, o, m:m + 1], ams[:, m:m + 1], neghalf[:, 0:1], ALU.pow).then_inc(sem.mixer_rstd, 1)
            post_factor(pool, 0, MIX)

        HEADS = [("sel", h) for h in range(NH)] + [("win", h) for h in range(NH)] + [("fox", h) for h in range(NH)]

        def q_of(kind, h, t):
            tok = slice(P * t, P * t + P)
            if kind == "fox":
                return fq[0:HD + 2, h, tok]
            o = HD * (h % 2)
            return qrT[o:o + HD, h // 2, tok]

        def k_of(kind, h, n):
            if kind == "fox":
                return fk[0:HD + 2, h, 0:n]
            o = HD * (h % 2)
            return {"sel": ksT, "win": kwT}[kind][o:o + HD, h // 4, 0:n]

        def v_of(kind, h, b):
            if kind == "fox":
                return fv[:, b, HD * h:HD * h + HD]
            o = {"sel": 0, "win": P}[kind] + HD * (h // 4)
            return vn[:, b, o:o + HD]

        def o_of(kind, h, t):
            c = HD * h + (512 if kind == "fox" else 0)
            return O[:, t, c:c + HD]

        def two_pe(pe, l):
            v = 1 + 2 * l
            w0 = B1 + 2 * l
            if w0:
                pe.wait_ge(sem.post_y, 8 * w0)
            for t in range(T):
                norm_transpose(pe, v - V0, t)
            pe.wait_ge(sem.hT, 8 * (v - V0) + 8)

            def bank_free(n):
                if n >= 4:
                    pe.wait_ge(sem.proj_sb, NPJ * l + n - 3)

            def natural(n, t, name, width):
                bank_free(n)
                wv = block_of(name, pe, 512)
                for k in range(KD):
                    last = nc.tensor.matmul(ps[n % 4][:, 0:width], HT[:, k, P * t:P * t + P], wv[:, k, 0:width],
                                            start=(k == 0), stop=(k == KD - 1))
                last.then_inc(sem.proj, 1)

            def transposed(n):
                bank_free(n)
                wv = block_of(f"t{n}_{l}", pe)
                for k in range(KD):
                    last = nc.tensor.matmul(ps[n % 4][:], wv[:, k, :], HT[:, k, :], start=(k == 0), stop=(k == KD - 1))
                last.then_inc(sem.proj, 1)

            def permute(m):
                n = 6 + m
                pe.wait_ge(sem.proj_sb, NPJ * l + n + 1)
                if m >= 2:
                    pe.wait_ge(sem.rot, NPM * l + m - 1)
                src = kraw[:, m, :] if m < 2 else qT[:, m - 2, :]
                nc.tensor.matmul(ps[4 + m % 2][:], swap2[:], src, start=True, stop=True).then_inc(sem.perm, 1)

            def hidden(i):
                pe.wait_ge(sem.cmp_E, 2 * l + i + 1)
                if l:
                    pe.wait_ge(sem.cs_o, T * l)
                wv = block_of(f"w1{'kv'[i]}_{l}", pe, CMP_HID)
                for j in range(2):
                    for k in range(LP):
                        last = nc.tensor.matmul(ps[6 + i][:, 64 * j:64 * j + 2 * NCMP], wv[:, k, P * j:P * j + P],
                                                E[i][:, k, :], start=(k == 0), stop=(k == LP - 1))
                last.then_inc(sem.hid_ps, 1)

            def compressed():
                pe.wait_ge(sem.hid, 4 * l + 2)
                for j in range(2):
                    last = nc.tensor.matmul(ps[6][:, 0:2 * NCMP], w2k[:, l, j, :], hidk[:, j, 0:2 * NCMP],
                                            start=(j == 0), stop=(j == 1))
                last.then_inc(sem.kc_ps, 1)
                pe.wait_ge(sem.hid_rep, l + 1)
                for g in range(KVG):
                    for j in range(2):
                        last = nc.tensor.matmul(ps[7][:, HD * g:HD * g + HD], hidr[:, j, g, :, :].rearrange("p r n -> p (r n)"),
                                                w2v[:, l, j, :], start=(j == 0), stop=(j == 1))
                last.then_inc(sem.vc_ps, 1)

            def forget_transpose():
                pe.wait_ge(sem.proj_sb, NPJ * l + 4)
                if l:
                    pe.wait_ge(sem.vc, l)
                for t in range(T):
                    last = nc.tensor.transpose(ps[7][0:8, P * t:P * t + P], gf[:, t, NGATE:NGATE + 8], ident[:])
                last.then_inc(sem.ff_T, 1)

            def cmp_scores(t):
                if t == 0:
                    pe.wait_ge(sem.kc, l + 1)
                    pe.wait_ge(sem.rot, NPM * (l + 1))
                else:
                    pe.wait_ge(sem.cs_p, T * l + t)
                for j in range(4):
                    last = nc.tensor.matmul(ps[4][:, HD * j:HD * j + HD], qT[:, j, P * t:P * t + P],
                                            kcBD[:, j // 2, :, :].rearrange("p o n -> p (o n)"), start=True, stop=True)
                last.then_inc(sem.cs_ps, 1)

            def cmp_transpose(t):
                pe.wait_ge(sem.cs_p, T * l + t + 1)
                if t:
                    pe.wait_ge(sem.cs_pT, T * l + t)
                for g in range(KVG):
                    last = nc.tensor.transpose(ps[5][:, P * g:P * g + P], CP[:, g, :], ident[:])
                last.then_inc(sem.cs_pT_ps, 1)

            def cmp_values(t):
                pe.wait_ge(sem.cs_pT, T * l + t + 1)
                if t == 0:
                    pe.wait_ge(sem.vc, l + 1)
                    pe.wait_ge(sem.kc, l + 1)
                else:
                    pe.wait_ge(sem.cs_o, T * l + t)
                for g in range(KVG):
                    last = nc.tensor.matmul(ps[6][:, 256 * g:256 * g + 256], CX[:, g, :],
                                            vBD[:, g, :, :].rearrange("p h d -> p (h d)"), start=True, stop=True)
                last.then_inc(sem.cs_o_ps, 1)

            for n in range(4):
                natural(n, n, f"n1_{l}", 288)
            transposed(4)
            transposed(5)
            forget_transpose()
            transposed(6)
            transposed(7)
            permute(0)
            hidden(0)
            pe.wait_ge(sem.ff_z, l + 1)
            hidden(1)
            permute(1)
            transposed(8)
            transposed(9)
            permute(2)
            compressed()
            transposed(10)
            permute(3)
            transposed(11)
            permute(4)
            for n in range(12, 16):
                natural(n, n - 12, f"n2_{l}", 512)
                if n == 12:
                    permute(5)
            for n in range(16, 24):
                transposed(n)
                t = n - 16
                if t < T:
                    cmp_scores(t)
                if 1 <= t <= T:
                    cmp_transpose(t - 1)
                if 2 <= t <= T + 1:
                    cmp_values(t - 2)

            pe.wait_ge(sem.proj_sb, NPJ * (l + 1))
            pe.wait_ge(sem.aug_ones, l + 1)
            pe.wait_ge(sem.ff_rows, 32 * (l + 1))
            pe.wait_ge(sem.cs_o, T * (l + 1))
            for u in range(NU + 4):
                if u < NU:
                    kind, h = HEADS[u // 4]
                    t = u % 4
                    if u >= 3:
                        pe.wait_ge(sem.s_masked, NU * l + u - 2)
                    nc.tensor.matmul(ps[u % 3][:, 0:P * (t + 1)], q_of(kind, h, t), k_of(kind, h, P * (t + 1)),
                                     start=True, stop=True).then_inc(sem.s_ps, 1)
                w = u - 2
                if 0 <= w < NU:
                    pe.wait_ge(sem.s_exp, NU * l + w + 1)
                    if w >= 2:
                        pt_wait(pe, l, w - 2)
                    for b in range(w % 4 + 1):
                        last = nc.tensor.transpose(ps[3 + w % 2][:, P * b:P * b + P], PR[:, w % 2, P * b:P * b + P], ident[:])
                    last.then_inc(sem.pT_ps, 1)
                w = u - 3
                if 0 <= w < NU:
                    kind, h = HEADS[w // 4]
                    t, gr = w % 4, w // 4
                    pt_wait(pe, l, w)
                    if t == 0 and gr >= 2:
                        pe.wait_ge(sem.o_sb, NU // 4 * l + gr - 1)
                    for b in range(t + 1):
                        last = nc.tensor.matmul(ps[5 + gr % 2][:, HD * t:HD * t + HD], PT[:, w % 2, P * b:P * b + P],
                                                v_of(kind, h, b), start=(b == 0), stop=(b == t))
                    last.then_inc(sem.o_ps, 1)

            pe.wait_ge(sem.o_sb, NU // 4 * (l + 1))
            for i in range(8):
                t, half = i // 2, i % 2
                for k in range(4):
                    c = 512 * half + P * k
                    last = nc.tensor.transpose(ps[i][:, P * k:P * k + P], O[:, t, c:c + P], ident[:])
                last.then_inc(sem.mixT_ps, 1)
            pe.wait_ge(sem.mixT_act, 4 * (l + 1))
            pe.wait_ge(sem.mixT_dve, 4 * (l + 1))
            out_projection(pe, w0, [f"wo{k}_{l}" for k in range(KD)])

            pe.wait_ge(sem.post_y, 8 * (w0 + 1))
            for t in range(T):
                norm_transpose(pe, v + 1 - V0, t)
            pe.wait_ge(sem.hT, 8 * (v + 1 - V0) + 8)
            for f in range(NF):
                if f >= 4:
                    pe.wait_ge(sem.relu, NF * l + f - 3)
                wv = block_of(f"up{f}_{l}", pe)
                for k in range(KD):
                    last = nc.tensor.matmul(ps[4 + f % 4][:], wv[:, k, :], HT[:, k, :], start=(k == 0), stop=(k == KD - 1))
                last.then_inc(sem.up_ps, 1)
            for half in range(2):
                if half:
                    pe.wait_ge(sem.relu, NF * (l + 1))
                for f in range(NF):
                    pe.wait_ge(sem.relu_sq, NF * l + f + 1)
                    wv = block_of(f"dn{half}_{f - f % 2}_{l}", pe, 512)
                    for t in range(T):
                        last = nc.tensor.matmul(ps[4 * half + t][:], uT[:, f, P * t:P * t + P], wv[:, f % 2, :],
                                                start=(f == 0), stop=(f == NF - 1))
                        if f == NF - 1:
                            last.then_inc(sem.out_ps, 1)
                    if f % 2 and f < NF - 1:
                        last.then_inc(sem.down, 1)

        def pt_wait(eng, l, u):
            if on_act(u):
                eng.wait_ge(sem.pT_act, N_ACT * l + ACT_BEFORE[u] + 1)
            else:
                eng.wait_ge(sem.pT_dve, (NU - N_ACT) * l + u - ACT_BEFORE[u] + 1)

        def two_act(act, l, post_gain):
            v = 1 + 2 * l - V0
            w0 = B1 + 2 * l
            norm_squares(act, v, lambda t: x_tile(2 * l, t))
            post_gain(w0, a["g_post_mix_2"][l:l + 1, :])

            def copy(dst, src, scale=1.0):
                return nc.scalar.activation(dst, src, ACT.Copy, scale=scale)

            def evacuate(n):
                act.wait_ge(sem.proj, NPJ * l + n + 1)
                src = ps[n % 4]
                if n < 4:
                    copy(vn[:, n, :], src[:, 0:256])
                    last = copy(gf[:, n, :], src[:, 256:288])
                elif n < 6:
                    for g in range(KVG):
                        mine = src[HD * g:HD * g + HD, :]
                        copy(X2[n - 4][0:HD, g, :], mine)
                        last = copy(X2[n - 4][HD:P, g, 0:SEQ - 1], mine[:, 1:SEQ])
                elif n < 8:
                    last = copy(kraw[:, n - 6, :], src[:])
                elif n < 12:
                    last = copy(qT[:, n - 8, :], src[:], -SCALE2)
                elif n < 16:
                    last = copy(fv[:, n - 12, :], src[:])
                else:
                    dst, scale = (fq, -SCALE2) if n < 20 else (fk, 1.0)
                    for o in range(2):
                        last = copy(dst[0:HD, 2 * (n % 4) + o, :], src[HD * o:HD * o + HD, :], scale)
                last.then_inc(sem.proj_sb, 1)

            def gelu_hidden(i):
                act.wait_ge(sem.hid_ps, 2 * l + i + 1)
                for j in range(2):
                    bias = cols[:, R_B1 + 4 * i + 2 * l + j:R_B1 + 4 * i + 2 * l + j + 1]
                    src = ps[6 + i][:, 64 * j:64 * j + 2 * NCMP]
                    if i == 0:
                        dst = hidk[:, j, 0:2 * NCMP]
                    else:
                        dst = hidv[:, j, :, 0:NCMP]
                        src = src.rearrange("p (g n) -> p g n", g=KVG)
                    nc.scalar.activation(dst, src, ACT.Gelu_apprx_tanh, bias=bias).then_inc(sem.hid, 1)

            def cmp_exp(t):
                act.wait_ge(sem.cs_exp, 2 * (T * l + t) + 1)
                nc.scalar.activation(CP.rearrange("p g n -> p (g n)"), CS.rearrange("p h n -> p (h n)"), ACT.Exp)\
                    .then_inc(sem.cs_exp, 1)

            act.wait_ge(sem.hT, 8 * v + 8)
            for n in range(4):
                evacuate(n)
            act.wait_ge(sem.gate_x, l + 1)
            nc.scalar.activation(gx[:], gx[:], ACT.Exp, scale=-1.0).then_inc(sem.gate_e, 1)
            evacuate(4)
            evacuate(5)
            act.wait_ge(sem.ff_z, l + 1)
            nc.scalar.activation(ffm[:], ffz[:], ACT.Abs).then_inc(sem.ff_abs, 1)
            act.wait_ge(sem.ff_abs, l + 1)
            nc.scalar.activation(ffm[:], ffm[:], ACT.Exp, scale=-1.0).then_inc(sem.ff_exp, 1)
            act.wait_ge(sem.ff_exp, l + 1)
            nc.scalar.activation(ffm[:], ffm[:], ACT.Ln, bias=1.0).then_inc(sem.ff_ln, 1)
            evacuate(6)
            evacuate(7)
            act.wait_ge(sem.ff_cum, 2 * (l + 1))
            act.wait_ge(sem.aug_ones, l + 1)
            act.dma_start(fk[HD:HD + 1, :, :], ffc[:]).then_inc(sem.ff_rows, 16)
            act.dma_start(fq[HD + 1:HD + 2, :, :], ffz[:]).then_inc(sem.ff_rows, 16)
            gelu_hidden(0)
            gelu_hidden(1)
            for n in range(8, 16):
                evacuate(n)
            for n in range(16, 24):
                evacuate(n)
                if n - 16 < T:
                    cmp_exp(n - 16)

            for u in range(NU + 2):
                if u < NU:
                    act.wait_ge(sem.s_masked, NU * l + u + 1)
                    if u >= 2:
                        act.wait_ge(sem.pT_ps, NU * l + u - 1)
                    w = P * (u % 4 + 1)
                    nc.scalar.activation(PR[:, u % 2, 0:w], SM[:, u % 3, 0:w], ACT.Exp, bias=mn[:, u % 4:u % 4 + 1],
                                         scale=-1.0, accum_out=rs[:, u:u + 1]).then_inc(sem.s_exp, 1)
                z = u - 2
                if z >= 0 and on_act(z):
                    act.wait_ge(sem.pT_ps, NU * l + z + 1)
                    if z >= 2:
                        act.wait_ge(sem.o_ps, NU * l + z - 1)
                    w = P * (z % 4 + 1)
                    copy(PT[:, z % 2, 0:w], ps[3 + z % 2][:, 0:w]).then_inc(sem.pT_act, 1)

            for i in range(0, 8, 2):
                mixT_copy(act, l, i, lambda d, s: copy(d, s), sem.mixT_act)
            post_squares(act, w0, MIX)
            norm_squares(act, v + 1, lambda t: x_tile(2 * l + 1, t))
            for f in range(NF):
                act.wait_ge(sem.up_ps, NF * l + f + 1)
                if f >= 2:
                    act.wait_ge(sem.relu_sq, NF * l + f - 1)
                nc.scalar.activation(relu[:, f % 2, :], ps[4 + f % 4][:], ACT.Relu).then_inc(sem.relu, 1)
            post_gain(w0 + 1, a["g_post_mlp_2"][l:l + 1, :])
            post_squares(act, w0 + 1, MLP)

        def mixT_copy(eng, l, i, copy, done):
            t, half = i // 2, i % 2
            eng.wait_ge(sem.mixT_ps, 8 * l + i + 1)
            copy(HT[:, 4 * half:4 * half + 4, P * t:P * t + P], ps[i][:].rearrange("p (k n) -> p k n", k=4))\
                .then_inc(done, 1)

        def x_tile(i, t):
            n = B1 + i
            return (sem.x_new, T * (n - 1) + t + 1) if n else (x_in[t], 16)

        def two_dve(dve, l):
            v = 1 + 2 * l - V0
            w0 = B1 + 2 * l
            norm_dve(dve, v)

            def rotate(m):
                dve.wait_ge(sem.perm, NPM * l + m + 1)
                dve_link(nc.vector.tensor_tensor(rsin[:, m % 2, :], ps[4 + m % 2][:], sin2[:], ALU.mult))
                dve.wait_ge(sem.rot_cos, NPM * l + m + 1)
                if m < 2:
                    dst = (ksT, kwT)[m]
                    for g in range(KVG):
                        for o in range(2):
                            a_, b_ = slice(HD * g, HD * g + HD), slice(HD * o, HD * o + HD)
                            last = nc.vector.tensor_tensor(dst[b_, g, :], rcos[a_, m % 2, :], rsin[a_, m % 2, :], ALU.add)
                else:
                    last = nc.vector.tensor_tensor(qrT[:, m - 2, :], rcos[:, m % 2, :], rsin[:, m % 2, :], ALU.add)
                last.then_inc(sem.rot, 1)

            def compressed():
                dve.wait_ge(sem.hid, 4 * l + 4)
                for j in range(2):
                    last = nc.vector.tensor_copy(hidr[:, j, :, :, :], hidv[:, j, :, None, :].to_broadcast([P, KVG, 4, 32]))
                last.then_inc(sem.hid_rep, 1)
                dve.wait_ge(sem.kc_ps, l + 1)
                for o in range(2):
                    r = slice(HD * o, HD * o + HD)
                    last = nc.vector.tensor_scalar(kcBD[r, :, o, 0:NCMP], ps[6][r, 0:2 * NCMP].rearrange("p (g n) -> p g n", g=KVG),
                                                   cols[r, R_B2K + l:R_B2K + l + 1], None, ALU.add)
                last.then_inc(sem.kc, 1)
                dve.wait_ge(sem.vc_ps, l + 1)
                for i in range(4):
                    r = slice(32 * i, 32 * i + 32)
                    last = nc.vector.tensor_tensor(vBD[r, :, i, :], ps[7][r, 0:P].rearrange("p (g d) -> p g d", g=KVG),
                                                   b2v[r, l, None, :].to_broadcast([32, KVG, HD]), ALU.add)
                last.then_inc(sem.vc, 1)

            def cmp_softmax(t):
                dve.wait_ge(sem.cs_ps, T * l + t + 1)
                if t:
                    dve.wait_ge(sem.cs_pT_ps, T * l + t)
                dve_link(nc.vector.tensor_tensor(CS, ps[4][:, 0:256].rearrange("p (h n) -> p h n", n=32),
                                                 cmask[:, t, None, :].to_broadcast([P, NH, 32]), ALU.add))
                dve_link(nc.vector.tensor_reduce(cmn[:], CS, AX_X, ALU.min))
                nc.vector.tensor_tensor(CS, cmn[:, :, None].to_broadcast([P, NH, 32]), CS, ALU.subtract)\
                    .then_inc(sem.cs_exp, 1)
                dve.wait_ge(sem.cs_exp, 2 * (T * l + t) + 2)
                pv = CP.rearrange("p g (h n) -> p (g h) n", n=32)
                dve_link(nc.vector.tensor_reduce(csum[:], pv, AX_X, ALU.add))
                dve_link(nc.vector.reciprocal(csum[:], csum[:]))
                dve_link(nc.vector.scalar_tensor_tensor(csum[:], gate[:, t, :].rearrange("p (h b) -> p b h", b=3)[:, 0, :],
                                                        valid[:, t:t + 1], csum[:], ALU.mult, ALU.mult))
                nc.vector.tensor_tensor(pv, pv, csum[:, :, None].to_broadcast([P, NH, 32]), ALU.mult).then_inc(sem.cs_p, 1)

            def cmp_pT(t):
                dve.wait_ge(sem.cs_pT_ps, T * l + t + 1)
                if t:
                    dve.wait_ge(sem.cs_o_ps, T * l + t)
                nc.vector.tensor_copy(CX, ps[5][:, 0:256].rearrange("p (g n) -> p g n", g=KVG)).then_inc(sem.cs_pT, 1)

            def cmp_out(t):
                dve.wait_ge(sem.cs_o_ps, T * l + t + 1)
                nc.vector.tensor_copy(O[:, t, 0:512], ps[6][:]).then_inc(sem.cs_o, 1)

            dve.wait_ge(sem.proj_sb, NPJ * l + 4)
            nc.vector.tensor_tensor(gx[:], gf[:, :, 0:NGATE], gbias[:, l, None, :].to_broadcast([P, T, NGATE]), ALU.add)\
                .then_inc(sem.gate_x, 1)
            dve.wait_ge(sem.ff_T, l + 1)
            if l:
                dve.wait_ge(sem.ff_rows, 32 * l)
            nc.vector.tensor_scalar(ffz[:], ps[7][0:8, :], cols[0:8, R_BF + l:R_BF + l + 1], None, ALU.add)\
                .then_inc(sem.ff_z, 1)
            dve.wait_ge(sem.gate_e, l + 1)
            dve_link(nc.vector.tensor_scalar(gx[:], gx[:], 1.0, None, ALU.add))
            nc.vector.reciprocal(gate[:], gx[:]).then_inc(sem.gate, 1)
            dve.wait_ge(sem.ff_ln, l + 1)
            dve_link(nc.vector.scalar_tensor_tensor(ffz[:], ffz[:], 0.0, ffm[:], ALU.min, ALU.subtract))
            nc.vector.tensor_tensor_scan(ffc[:], ones[0:8, 0:1].to_broadcast([8, SEQ]), ffz[:], 0.0, ALU.mult, ALU.add).then_inc(sem.ff_cum, 1)
            dve.wait_ge(sem.ff_cum, 2 * l + 1)
            nc.vector.tensor_scalar(ffz[:], ffc[:], -1.0, None, ALU.mult).then_inc(sem.ff_cum, 1)
            dve.wait_ge(sem.gate, l + 1)
            rotate(0)
            rotate(1)
            compressed()
            for m in range(2, 6):
                rotate(m)
            for t in range(T + 2):
                if t < T:
                    cmp_softmax(t)
                if 1 <= t <= T:
                    cmp_pT(t - 1)
                if t >= 2:
                    cmp_out(t - 2)

            for u in range(NU + 4):
                if u < NU:
                    dve.wait_ge(sem.s_ps, NU * l + u + 1)
                    if u >= 3:
                        dve.wait_ge(sem.s_exp, NU * l + u - 2)
                    if u >= 4:
                        dve.wait_ge(sem.s_exp, NU * l + u - 3)
                    t = u % 4
                    w = P * (t + 1)
                    nc.vector.tensor_tensor_reduce(SM[:, u % 3, 0:w], ps[u % 3][:, 0:w], tri[:, SEQ - w:SEQ], 1.0,
                                                   3.0e38, ALU.add, ALU.min, mn[:, t:t + 1]).then_inc(sem.s_masked, 1)
                z = u - 2
                if 0 <= z < NU and not on_act(z):
                    dve.wait_ge(sem.pT_ps, NU * l + z + 1)
                    if z >= 2:
                        dve.wait_ge(sem.o_ps, NU * l + z - 1)
                    w = P * (z % 4 + 1)
                    nc.vector.tensor_copy(PT[:, z % 2, 0:w], ps[3 + z % 2][:, 0:w]).then_inc(sem.pT_dve, 1)
                z = u - 4
                if z >= 0 and z % 4 == 3:
                    gr = z // 4
                    kind, h = HEADS[gr]
                    dve.wait_ge(sem.s_exp, NU * l + z + 1)
                    r = rg[:, gr % 3, :]
                    dve_link(nc.vector.reciprocal(r, rs[:, 4 * gr:4 * gr + 4]))
                    if kind != "fox":
                        b = 1 if kind == "sel" else 2
                        dve_link(nc.vector.tensor_tensor(r, r, gate[:, :, 3 * h + b], ALU.mult))
                    dve.wait_ge(sem.o_ps, NU * l + z + 1)
                    for t in range(T):
                        src = ps[5 + gr % 2][:, HD * t:HD * t + HD]
                        dst = o_of(kind, h, t)
                        if kind == "fox":
                            last = nc.vector.tensor_scalar(dst, src, r[:, t:t + 1], None, ALU.mult)
                        else:
                            last = nc.vector.scalar_tensor_tensor(dst, src, r[:, t:t + 1], dst, ALU.mult, ALU.add)
                    last.then_inc(sem.o_sb, 1)

            for i in range(1, 8, 2):
                mixT_copy(dve, l, i, lambda d, s: nc.vector.tensor_copy(d, s), sem.mixT_dve)
            post_add(dve, w0, MIX)
            norm_dve(dve, v + 1)
            post_add(dve, w0 + 1, MLP)

        def two_pool(pool, l):
            v = 1 + 2 * l - V0
            w0 = B1 + 2 * l
            norm_rstd(pool, v)
            pool.wait_ge(sem.hT, 8 * v + 8)
            nc.gpsimd.memset(fq[HD:HD + 2, :, :], 1.0)
            nc.gpsimd.memset(fk[HD:HD + 2, :, :], 1.0).then_inc(sem.aug_ones, 1)
            pool.wait_ge(sem.aug_ones, l + 1)
            for i in range(2):
                pool.wait_ge(sem.proj_sb, NPJ * l + 5 + i)
                r0 = R_POS + 32 * i + LP * l
                for g in range(KVG):
                    src = window(X2[i], g)
                    last = nc.gpsimd.tensor_tensor(E[i][:, :, NCMP * g:NCMP * g + NCMP], src,
                                                   cols[:, r0:r0 + LP, None].to_broadcast([P, LP, NCMP]), ALU.add)
                last.then_inc(sem.cmp_E, 1)
            for m in range(NPM):
                pool.wait_ge(sem.proj_sb, NPJ * l + 7 + m)
                if m >= 2:
                    pool.wait_ge(sem.rot, NPM * l + m - 1)
                src = kraw[:, m, :] if m < 2 else qT[:, m - 2, :]
                nc.gpsimd.tensor_tensor(rcos[:, m % 2, :], src, cos2[:], ALU.mult).then_inc(sem.rot_cos, 1)
            post_factor(pool, w0, MIX)
            norm_rstd(pool, v + 1)
            for f in range(NF):
                pool.wait_ge(sem.relu, NF * l + f + 1)
                nc.gpsimd.tensor_tensor(uT[:, f, :], relu[:, f % 2, :], relu[:, f % 2, :], ALU.mult).then_inc(sem.relu_sq, 1)
            post_factor(pool, w0 + 1, MLP)

        def window(x2, g):
            v = x2[:, g, 0:SEQ]
            ap = [list(d) for d in v.ap]
            return bass.AP(v.tensor, v.offset, [ap[0], [2, LP], [CMP_STRIDE, NCMP]])

        V0 = 0 if first else 1
        on_act = lambda u: u % 5 in (1, 3)
        ACT_BEFORE = [sum(on_act(x) for x in range(u)) for u in range(NU)]
        N_ACT = sum(on_act(u) for u in range(NU))

        vectors = []
        if first:
            vectors += [(R_PRE1, a["pre_norm_g"][0]), (R_QN, a["q_norm_g"][0]), (R_KVN, a["kv_norm_g"][0]),
                        (R_AO, a["attn_out_g"][0]), (R_SO, a["ssm_out_g"][0])]
        for l in range(DEPTH):
            vectors += [(R_NORM + 16 * l, a["g_pre_mix_2"][l]), (R_NORM + 16 * l + 8, a["g_pre_mlp_2"][l]),
                        (R_B1 + 2 * l, a["cmp_b1_k_2"][l]), (R_B1 + 4 + 2 * l, a["cmp_b1_v_2"][l]),
                        (R_POS + LP * l, a["cmp_pos_k_2"][l].rearrange("(k o) d -> (k o d)", o=2)),
                        (R_POS + 32 + LP * l, a["cmp_pos_v_2"][l].rearrange("(k o) d -> (k o d)", o=2))]
        small = [(swap2[:], a["c_swap2"]), (tri[:], a["c_tri"]), (cos2[:], a["c_cos2"]), (sin2[:], a["c_sin2"]),
                 (cmask[:], a["c_cmask"].rearrange("p (t n) -> p t n", t=T)), (valid[:], a["c_valid"])]
        for l in range(DEPTH):
            small += [(gbias[:, l, :], a["b_nsa_gate_2"][l:l + 1, :].to_broadcast([P, NGATE])),
                      (b2v[:, l, :], a["cmp_b2_v_2"][l:l + 1, :].to_broadcast([P, HD])),
                      (w2k[:, l, :, 0:HD], a["cmp_w2_k_2"][l].rearrange("(j p) d -> p j d", p=P)),
                      (w2k[:, l, :, HD:P], a["cmp_w2_k_2"][l].rearrange("(j p) d -> p j d", p=P)),
                      (w2v[:, l, :, :], a["cmp_w2_v_2"][l].rearrange("(j p) d -> p j d", p=P))]
        if first:
            small += one_small()
        N_ROWS, N_SMALL = 16 * (len(vectors) + 3), 16 * len(small)

        block = ctx.enter_context(nc.Block())

        @block.sync
        def _(sp):
            for u in units:
                for s, n in u.free:
                    sp.wait_ge(s, n)
                for where, src in u.pieces:
                    dst = slots(u)
                    if where is not None:
                        width = 512 if u.slots == 4 else P
                    if where is not None and where[0] == "q":
                        _, c, h, n = where
                        dst = dst[:, c:c + h * n].rearrange("p (h n) -> p h n", h=h)
                    elif where is not None:
                        dst = dst.rearrange("p (k c) -> p k c", c=width)[:, 0:src.shape[1], where[0]:where[0] + where[1]]
                    elif len(src.shape) == 3:
                        dst = dst.rearrange("p (k c) -> p k c", c=src.shape[2])[:, 0:src.shape[1], :]
                    else:
                        dst = dst[:, 0:src.shape[1]]
                    sp.dma_start(dst, src).then_inc(wring[u.slot], 16)
            sp.wait_ge(sem.out_done, 16 * T)

        @block.gpsimd
        def _(pool):
            nc.gpsimd.memset(neghalf[:], -0.5).then_inc(sem.const_set, 1)
            nc.gpsimd.memset(rows[:], 0.0).then_inc(sem.wrows_zero, 1)
            nc.gpsimd.memset(ones[:], 1.0).then_inc(sem.const_set, 1)
            nc.gpsimd.memset(kcBD[:], 0.0).then_inc(sem.const_set, 1)
            nc.gpsimd.memset(vBD[:], 0.0).then_inc(sem.const_set, 1)
            nc.gpsimd.memset(hidv[:], 0.0).then_inc(sem.const_set, 1)
            pool.wait_ge(sem.const_set, 5)
            if first:
                one_pool(pool)
            if second:
                pool.wait_ge(sem.cols_ready, 1)
                for l in range(DEPTH):
                    two_pool(pool, l)

        @block.scalar
        def _(act):
            act.dma_start(ident[:], a["c_ident"]).then_inc(sem.consts_in, 16)
            for t in range(T):
                act.dma_start(X[:, t, :], a["x"][P * t:P * t + P, :]).then_inc(x_in[t], 16)
            act.wait_ge(sem.wrows_zero, 1)
            for r, src in vectors:
                k = src.shape[0] // P
                act.dma_start(rows[r:r + k, :], src.rearrange("(k p) -> k p", p=P)).then_inc(sem.rows_in, 16)
            for o in range(2):
                act.dma_start(rows[R_B2K:R_B2K + DEPTH, HD * o:HD * o + HD], a["cmp_b2_k_2"][0:DEPTH, :]).then_inc(sem.rows_in, 16)
            act.dma_start(rows[R_BF:R_BF + DEPTH, 0:8], a["b_forget_2"][0:DEPTH, :]).then_inc(sem.rows_in, 16)
            for dst, src in small:
                act.dma_start(dst, src).then_inc(sem.small_in, 16)
            act.wait_ge(sem.cols_ready, 1)
            act.wait_ge(sem.small_in, N_SMALL)
            act.wait_ge(sem.const_set, 5)

            def post_gain(w, src):
                if w:
                    act.wait_ge(sem.post_y, 8 * w)
                act.dma_start(postg[:], src.to_broadcast([P, D])).then_inc(sem.postgain_in, 16)

            if first:
                one_act(act, post_gain)
            if second:
                for l in range(DEPTH):
                    two_act(act, l, post_gain)
            n = (B1 + 2 * DEPTH if second else 1)
            for t in range(T):
                act.wait_ge(sem.x_new, T * (n - 1) + t + 1)
                act.dma_start(out[P * t:P * t + P, :], X[:, t, :]).then_inc(sem.out_done, 16)

        @block.tensor
        def _(pe):
            pe.wait_ge(sem.consts_in, 16)
            pe.wait_ge(sem.rows_in, N_ROWS)
            nc.tensor.transpose(ps[7][:, 0:ROWS], rows[:], ident[:]).then_inc(sem.cols_ps, 1)
            pe.wait_ge(sem.small_in, N_SMALL)
            pe.wait_ge(sem.const_set, 5)
            if first:
                one_pe(pe)
            if second:
                for l in range(DEPTH):
                    two_pe(pe, l)

        @block.vector
        def _(dve):
            dve.wait_ge(sem.cols_ps, 1)
            nc.vector.tensor_copy(cols[:], ps[7][:, 0:ROWS]).then_inc(sem.cols_ready, 1)
            dve.wait_ge(sem.cols_ready, 1)
            dve.wait_ge(sem.small_in, N_SMALL)
            dve.wait_ge(sem.const_set, 5)
            if first:
                one_dve(dve)
            if second:
                for l in range(DEPTH):
                    two_dve(dve, l)


_INS = ["x", "positions", "pre_norm_g", "w_in", "q_norm_g", "w_uq", "kv_norm_g", "w_ukv", "attn_out_g",
        "s5_lam_re", "s5_lam_im", "s5_log_dt", "s5_b_re", "s5_b_im", "s5_c_re", "s5_c_im", "s5_d",
        "w_glu", "b_glu", "ssm_out_g", "w_out", "post_norm_g",
        "w_in_2", "b_nsa_gate_2", "b_forget_2", "cmp_pos_k_2", "cmp_w1_k_2", "cmp_b1_k_2", "cmp_w2_k_2", "cmp_b2_k_2",
        "cmp_pos_v_2", "cmp_w1_v_2", "cmp_b1_v_2", "cmp_w2_v_2", "cmp_b2_v_2", "w_out_2", "w_up_2", "w_down_2",
        "g_pre_mix_2", "g_post_mix_2", "g_pre_mlp_2", "g_post_mlp_2"]


def kernel(**inputs):
    import numpy as _np
    import concourse.bacc as _bacc
    from concourse import mybir as _mybir
    from concourse.bass_utils import run_bass_kernel_spmd as _run

    nc = _bacc.Bacc("TRN2", target_bir_lowering=False, num_devices=1)
    arrays, aps = {}, {}
    given = {name: _np.ascontiguousarray(inputs[name]) for name in _INS}
    given["x"] = given["x"].reshape(SEQ, D)
    given.update(constants())
    for name, value in given.items():
        arrays[f"in_{name}"] = value
        aps[name] = nc.dram_tensor(f"in_{name}", value.shape, _mybir.dt.from_np(value.dtype), kind="ExternalInput").ap()
    out = nc.dram_tensor("out", (SEQ, D), F32, kind="ExternalOutput").ap()
    build(nc, aps, out)
    r = _run(nc, [arrays], core_ids=[0])
    return r.results[0]["out"].reshape(1, SEQ, D)
```

```python
from contextlib import ExitStack
from collections import namedtuple

import numpy as np
import concourse.bass as bass
from concourse import mybir

F32 = mybir.dt.float32
F32R = mybir.dt.float32r
I32 = mybir.dt.int32
ALU = mybir.AluOpType
ACT = mybir.ActivationFunctionType
AX_X = mybir.AxisListType.X

P = 128
SEQ = 512
D = 1024
T = SEQ // P
KD = D // P
EPS = 1e-6

Q_RANK, KV_RANK, ROPE1 = 256, 128, 64
H1, NOPE, VD = 4, 128, 128
WIDE = 512
G, CH, ST = 32, 16, 64
L = 8
NC = SEQ // L
NQ, GQ = 4, 8
SCALE1 = float(NOPE + ROPE1) ** -0.5

DEPTH = 2
HD = 64
NH, KVG = 8, 2
CMP_LEN, CMP_STRIDE, CMP_HID = 32, 16, 256
NCMP = (SEQ - CMP_LEN) // CMP_STRIDE + 1
LP = CMP_LEN // 2
DFF = 4 * D
NF = DFF // P
SCALE2 = float(HD) ** -0.5
C_Q, C_KC, C_VC, C_KS, C_VS, C_KW, C_VW, C_GATE, C_FQ, C_FK, C_FV, C_FF = [
    int(v) for v in np.cumsum([0, 512, 128, 128, 128, 128, 128, 128, 24, 512, 512, 512])]
NGATE = 24
IN2 = C_FF + 8
BIG_NEG = 1e30

NS = 8
NPJ, NPM = 24, 6
FG, NG = 8, NF // 8
NSPLIT = NPJ + 2 * NF
NU = 96
ROWS = 128


def rope_table_2():
    half = HD // 4 // 2
    inv = np.float32(500000.0) ** (-np.arange(half, dtype=np.float32) * np.float32(2.0) / np.float32(HD // 4))
    ang = np.arange(SEQ, dtype=np.float32)[None, :] * inv.astype(np.float32)[:, None]
    c = np.ones((HD, SEQ), np.float32)
    s = np.zeros((HD, SEQ), np.float32)
    c[:half], c[half:2 * half] = np.cos(ang), np.cos(ang)
    s[:half], s[half:2 * half] = -np.sin(ang), np.sin(ang)
    return np.concatenate([c, c]), np.concatenate([s, s])


def swap_matrix(block, half, sign=1.0):
    m = np.zeros((P, P), np.float32)
    for b in range(0, P, block):
        for r in range(half):
            m[b + half + r, b + r] = 1.0
            m[b + r, b + half + r] = sign
    return m


def constants():
    q = np.arange(P)
    tri = np.zeros((P, SEQ), np.float32)
    tri[:, SEQ - P:] = np.where(q[None, :] <= q[:, None], 0.0, BIG_NEG)
    tok = np.arange(SEQ).reshape(T, P).T
    end = np.full(32, 10 ** 6)
    end[:NCMP] = np.arange(NCMP) * CMP_STRIDE + CMP_LEN - 1
    cmask = np.where(end[None, None, :] <= tok[:, :, None], 0.0, BIG_NEG).astype(np.float32)
    valid = (tok >= CMP_LEN - 1).astype(np.float32)
    c2, s2 = rope_table_2()
    inv1 = np.float32(10000.0) ** (-np.arange(0, ROPE1, 2, dtype=np.float32) / np.float32(ROPE1))
    col = np.zeros((P, 8), np.float32)
    col[:, 0] = np.tile(inv1, 4)
    col[:, 1] = np.tile(np.repeat([-1.0, 1.0], 32), 2)
    col[:, 2] = np.repeat([-1.0, 1.0], ST)
    return {
        "c_ident": np.eye(P, dtype=np.float32), "c_tri": tri, "c_cmask": cmask.reshape(P, T * 32),
        "c_valid": valid, "c_cos2": c2, "c_sin2": s2, "c_col": col,
        "c_swap2": swap_matrix(HD, HD // 8), "c_swap1": swap_matrix(ROPE1, ROPE1 // 2),
        "c_turn": swap_matrix(P, ST, -1.0),
    }


class Unit:

    def __init__(self, name, slots, pieces, used):
        self.name, self.slots = name, slots
        self.pieces = pieces
        self.used = used
        self.slot = self.landed = 0
        self.free = []

ONE_SEMS = (
    "par_in par_ps par dt_e par_exp par_trig amp "
    "u_ps u_sb uT_ps uT gs_ps gs za_ps za_sq za_rstd zn znT_ps znT ga_ps ga "
    "pos_in angle trig rope_ps rope_done "
    "bc_in cT_ps cT b_bar m1 m1T_ps w1T m3 tap_ps taps toep st_ps st_sb turn_ps turned state y_ps y_sb yT_ps yp "
    "ge geT_ps geT glu_ps glu_x glu_s glu_y mixer_sq mixer_rstd ssm_o "
    "qn_ps qn rq_ps rq kn_ps kn v1_ps v1 "
    "a_s_ps a_min a_exp a_pT_ps a_pT a_o_ps a_o at_o "
    "m1ix_ps m1ix").split()

TWO_PI = 2 * np.pi
PI2_A = 6.28125
PI2_B = float(np.float32(int((TWO_PI - PI2_A) * 2 ** 22) / 2 ** 22))
PI2_C = float(np.float32(TWO_PI - PI2_A - PI2_B))
ROUND = 12582912.0
PI_SAFE = 3.1415925
DG = 2 * G
DQ = 2 * GQ
NK = L + 1


def one_units(a, unit, colblock, quad, t_blocks, sem):
    w = a["w_in"][0]
    c_q, c_kr, c_ga, c_u, c_gs = 0, Q_RANK + KV_RANK, 448, 960, 1472
    quad("u", [((0, 512), t_blocks(w, (c_u, c_u + 512)))], sem.u_ps, T)
    quad("gs", [((0, 512), t_blocks(w, (c_gs, c_gs + 512)))], sem.gs_ps, T)
    quad("za", [((0, 448), t_blocks(w, (c_q, 448)))], sem.za_ps, T)
    quad("ga", [((0, 512), t_blocks(w, (c_ga, c_ga + 512)))], sem.ga_ps, T)
    quad("glu", [((0, 512), t_blocks(a["w_glu"][0], (0, 512)))], sem.glu_ps, T)
    w = a["w_uq"][0].rearrange("(k p) (h c) -> k p h c", p=P, h=H1)
    pieces = []
    for k in range(2):
        pieces.append((("q", k * 768, H1, NOPE), w[k, :, :, 0:NOPE]))
        pieces.append((("q", k * 768 + 512, H1, ROPE1), w[k, :, :, NOPE:NOPE + ROPE1]))
    unit("uq", 4, pieces, sem.rq_ps, 2)
    unit("ukv", 1, [(None, a["w_ukv"][0])], sem.v1_ps, T)
    for k in range(KD):
        unit(f"wo{k}", 1, [(None, a["w_out"][0][P * k:P * k + P, :])], sem.out_ps, 8)


def build(nc, a, out, first=True, second=True):
    names = (
        "x_in0 x_in1 x_in2 x_in3 rows_in consts_in small_in postgain_in wring0 wring1 wring2 wring3 wring4 wring5 wring6 wring7 "
        "cols_ps cols_ready const_set "
        "sq rstd xn xT x_gained x_hi hT w_hi w_lo x_new out_ps post_sq post_y post_rstd "
        "proj proj_sb perm rot rot_cos gate_e gate "
        "ff_T ff_z ff_abs ff_exp ff_ln ff_cum ff_rows aug_ones "
        "cmp_E hid_ps hid hid_rep kc_ps kc vc_ps vc "
        "cs_ps cs_exp cs_p cs_pT_ps cs_pT cs_o_ps cs_o "
        "s_ps s_masked s_exp pT_ps pT_act pT_dve o_ps o_sb "
        "mixT_ps mixT_act mixT_dve up_ps relu relu_sq down mlp_sum "
        "act_chain dve_chain pool_chain out_done").split()
    if first:
        names += ONE_SEMS
    with ExitStack() as ctx:
        sem = namedtuple("Semaphores", names)(*[ctx.enter_context(nc.semaphore("s_" + n)) for n in names])
        wring = [sem.wring0, sem.wring1, sem.wring2, sem.wring3, sem.wring4, sem.wring5, sem.wring6, sem.wring7]

        x_in = [sem.x_in0, sem.x_in1, sem.x_in2, sem.x_in3]

        def sb(name, *free, parts=P):
            return ctx.enter_context(nc.sbuf_tensor(name, [parts, *free], F32))

        ps = [ctx.enter_context(nc.psum_tensor(f"ps{b}", [P, 512], F32)) for b in range(8)]

        X = sb("X", T, D)
        at_HT = nc.sbuf_base
        HT = sb("HT", KD, SEQ)
        at_WR = nc.sbuf_base
        WR = sb("WR", NS, 1024)
        ident, swap2 = sb("ident", P), sb("swap2", P)
        tri, cos2, sin2 = sb("tri", SEQ), sb("cos2", SEQ), sb("sin2", SEQ)
        cmask, valid = sb("cmask", T, 32), sb("valid", T)
        rows, cols = sb("rows", P), sb("cols", ROWS)
        postg = sb("postg", D)
        gbias, b2v = sb("gbias", DEPTH, NGATE), sb("b2v", DEPTH, HD)
        w2k, w2v = sb("w2k", DEPTH, 2, P), sb("w2v", DEPTH, 2, HD)
        neghalf = sb("neghalf", T)
        ones = sb("ones", 1)
        ss, ms, rstd = sb("ss", T), sb("ms", T), sb("rstd", T)
        pss, pms, prstd = sb("pss", T, 2), sb("pms", T), sb("prstd", T)
        kcBD, vBD = sb("kcBD", KVG, 2, 32), sb("vBD", KVG, 4, HD)
        hidk, hidv, hidr = sb("hidk", 2, 64), sb("hidv", 2, KVG, 32), sb("hidr", 2, KVG, 4, 32)
        gf, gx, gate = sb("gf", T, 32), sb("gx", T, NGATE), sb("gate", T, NGATE)
        ffz, ffm, ffc = (sb(n, SEQ, parts=8) for n in ("ffz", "ffm", "ffc"))
        mn, rs, rg = sb("mn", 4), sb("rs", NU), sb("rg", 3, 4)
        cmn, csum = sb("cmn", NH), sb("csum", NH)

        BIGW = 28672
        at_BIG = nc.sbuf_base
        BIG = sb("BIG", BIGW)

        def parts(name, byte, *free):
            return nc.alloc_sbuf_tensor_at(name, [P, *free], F32R, offset=byte)

        HT_R, WR_R = parts("HT_R", at_HT, KD, SEQ), parts("WR_R", at_WR, NS, 1024)

        def carve(at, *shape):
            n = int(np.prod(shape))
            assert at + n <= BIGW, (at, n)
            v = BIG[:, at:at + n]
            if len(shape) == 2:
                v = v.rearrange("p (a b) -> p a b", b=shape[1])
            if len(shape) == 3:
                v = v.rearrange("p (a b c) -> p a b c", b=shape[1], c=shape[2])
            return v

        qT, qrT = carve(0, 4, SEQ), carve(2048, 4, SEQ)
        ksT, kwT = carve(4096, 2, SEQ), carve(5120, 2, SEQ)
        fq, fk = carve(6144, NH, SEQ), carve(10240, NH, SEQ)
        vn, fv = carve(14336, T, 256), carve(15360, T, 512)
        O = carve(17408, T, D)
        uT_hi, uT_lo = parts("uT_hi", at_BIG, FG, SEQ), parts("uT_lo", at_BIG + 4 * 4096, FG, SEQ)
        Y = O
        A0 = 21504
        xn = carve(A0, 2, D)
        junk = carve(A0 + 2048, D)
        relu = carve(A0 + 3072, 2, SEQ)
        HL_IN = [carve(17408, KD, SEQ), parts("HL_IN", at_BIG + 4 * 17408, KD, SEQ)]
        HL_MLP = [carve(8192, KD, SEQ), parts("HL_MLP", at_BIG + 4 * 8192, KD, SEQ)]
        WH_FIRST = parts("WH_FIRST", at_BIG + 4 * 6144, 8, 1024)
        WH_LAST = parts("WH_LAST", at_BIG + 4 * (A0 + 3072), 4, 1024)
        WH_MLP = parts("WH_MLP", at_BIG + 4 * 12288, 4, 1024)
        junk2 = carve(A0 + 4096, 512)
        kraw, rcos, rsin = carve(A0, 2, SEQ), carve(A0 + 1024, 2, SEQ), carve(A0 + 2048, 2, SEQ)
        X2 = [carve(A0 + 3072, 2, SEQ), carve(A0 + 4096, 2, SEQ)]
        E = [carve(A0 + 5120, LP, 2 * NCMP), carve(A0 + 5120 + LP * 2 * NCMP, LP, 2 * NCMP)]
        SM = carve(A0 + 3072, 3, SEQ)
        PR = carve(A0 + 4608, 2, SEQ)
        PT = carve(A0 + 5632, 2, SEQ)
        CS, CP = carve(A0, NH, 32), carve(A0 + 256, KVG, P)
        CX = carve(A0 + 512, KVG, P)
        CO = carve(A0 + 768, T, 512)

        R_PRE1, R_QN, R_KVN, R_AO, R_SO = 0, 8, 10, 11, 15
        R_NORM, R_B1, R_POS, R_B2K, R_BF = 19, 51, 59, 123, 125

        def t_blocks(w, n):
            return w.rearrange("(k p) c -> p k c", p=P)[:, :, n[0]:n[1]]

        def down_count(l, g, half, i):
            return NF * l + FG * g + FG // 2 * half + i + 1

        units = []

        def unit(name, slots, pieces, sema, value):
            units.append(Unit(name, slots, pieces, (sema, value)))

        def colblock(name, w, c, n, sema, value):
            unit(name, 1, [((0, n), t_blocks(w, (c, c + n)))], sema, value)

        def quad(name, pieces, sema, value):
            unit(name, 4, pieces, sema, value)

        if first:
            one_units(a, unit, colblock, quad, t_blocks, sem)
        B1 = int(first)
        if second:
            for l in range(DEPTH):
                w = a["w_in_2"][l]
                at = 0
                pieces = []
                for c, n in ((C_VS, P), (C_VW, P), (C_GATE, NGATE), (C_FF, 8)):
                    pieces.append(((at, n), t_blocks(w, (c, c + n))))
                    at += n
                pj = lambda n: NPJ * l + n + 1
                quad(f"n1_{l}", pieces, sem.proj, pj(3))
                for i, c in enumerate((C_KC, C_VC, C_KS, C_KW)):
                    colblock(f"t{4 + i}_{l}", w, c, P, sem.proj, pj(4 + i))
                for i, kind in enumerate("kv"):
                    w1 = a[f"cmp_w1_{kind}_2"][l]
                    unit(f"w1{kind}_{l}", 4, [(None, w1.rearrange("(k p) c -> p k c", p=P))], sem.hid_ps, 2 * l + i + 1)
                for i in range(4):
                    colblock(f"t{8 + i}_{l}", w, C_Q + P * i, P, sem.proj, pj(8 + i))
                quad(f"n2_{l}", [((0, 512), t_blocks(w, (C_FV, C_FV + 512)))], sem.proj, pj(15))
                for i in range(8):
                    colblock(f"t{16 + i}_{l}", w, C_FQ + P * i, P, sem.proj, pj(16 + i))
                for k in range(KD):
                    unit(f"wo{k}_{l}", 1, [(None, a["w_out_2"][l][P * k:P * k + P, :])], sem.out_ps,
                         8 * (B1 + l) + 8)
                for g in range(NG):
                    for f in range(FG * g, FG * g + FG):
                        colblock(f"up{f}_{l}", a["w_up_2"][l], P * f, P, sem.up_ps, NF * l + f + 1)
                    for half in range(2):
                        for i in range(FG // 2):
                            f = FG * g + 2 * i
                            wd = a["w_down_2"][l][P * f:P * f + 2 * P, 512 * half:512 * half + 512]
                            unit(f"dn{half}_{f}_{l}", 1, [(None, wd.rearrange("(k p) c -> p k c", p=P))],
                                 sem.down, down_count(l, g, half, i))

        by_name, at, owner, loads = {}, 0, [None] * NS, [0] * NS
        for u in units:
            if at % NS + u.slots > NS or (u.slots == 4 and at % 4):
                at += (-at) % 4
            u.slot = at % NS
            for s in range(u.slot, u.slot + u.slots):
                if owner[s] is not None and owner[s].used not in u.free:
                    u.free.append(owner[s].used)
                owner[s] = u
            loads[u.slot] += 16 * len(u.pieces)
            u.landed = loads[u.slot]
            by_name[u.name] = u
            at += u.slots

        def slots(u):
            return WR[:, u.slot:u.slot + u.slots, :].rearrange("p s n -> p (s n)")

        def arrived(pe, name):
            u = by_name[name]
            pe.wait_ge(wring[u.slot], u.landed)
            return slots(u)

        def block_of(name, pe, width=P):
            return arrived(pe, name).rearrange("p (k c) -> p k c", c=width)

        def split_of(j):
            if j < 4:
                return "n1", j, 288
            if 12 <= j < 16:
                return "n2", j - 12, None
            if j < NPJ:
                return f"t{j}", 0, None
            g, i = divmod(j - NPJ, 2 * FG)
            if i < FG:
                return f"up{FG * g + i}", 0, None
            half, i = divmod(i - FG, FG // 2)
            return f"dn{half}_{FG * g + 2 * i}", 0, None

        def parts_of(l, j):
            name, i, width = split_of(j)
            u = by_name[f"{name}_{l}"]
            hi = WH_FIRST[:, j % 8, :] if j < 16 else WH_LAST[:, j % 4, :] if j < NPJ else WH_MLP[:, j % 4, :]
            parts = hi, WR_R[:, u.slot + i, :], WR[:, u.slot + i, :]
            if width is not None:
                parts = [v.rearrange("p (k c) -> p k c", c=512)[:, :, 0:width] for v in parts]
            return u, *parts

        def split_hi(act, l, j):
            u, hi, lo, whole = parts_of(l, j)
            act.wait_ge(wring[u.slot], u.landed)
            if 8 <= j < 12:
                act.wait_ge(sem.proj, NPJ * l + 4)
            elif 12 <= j < 16:
                act.wait_ge(sem.proj, NPJ * l + j - 7)
            elif 20 <= j < NPJ:
                act.wait_ge(sem.proj, NPJ * l + j - 3)
            elif j >= NPJ + 4:
                g, i = divmod(j - 4 - NPJ, 2 * FG)
                if i < FG:
                    act.wait_ge(sem.up_ps, NF * l + FG * g + i + 1)
                else:
                    act.wait_ge(sem.down, down_count(l, g, (i - FG) // (FG // 2), i % (FG // 2)))
            nc.scalar.activation(hi, whole, ACT.Copy).then_inc(sem.w_hi, 1)

        def split_lo(dve, l, j):
            u, hi, lo, whole = parts_of(l, j)
            dve.wait_ge(sem.w_hi, NSPLIT * l + j + 1)
            nc.vector.tensor_tensor(lo, whole, hi.bitcast(F32), ALU.subtract).then_inc(sem.w_lo, 1)

        def split(pe, l, j):
            pe.wait_ge(sem.w_lo, NSPLIT * l + j + 1)
            _, hi, lo, _ = parts_of(l, j)
            return hi, lo

        def product(out_, w, x, start, stop):
            nc.tensor.matmul(out_, w[0], x[0], start=start, stop=False)
            nc.tensor.matmul(out_, w[0], x[1], start=False, stop=False)
            return nc.tensor.matmul(out_, w[1], x[0], start=False, stop=stop)

        def norm_squares(act, v, x_count):
            for t in range(T):
                act.wait_ge(*x_count(t))
                if v or t:
                    act.wait_ge(sem.sq, T * v + t)
                if v and t == 0:
                    act.wait_ge(sem.rstd, T * v)
                nc.scalar.activation(junk if v + V0 else BIG[:, 6144:6144 + D], X[:, t, :], ACT.Square, accum_out=ss[:, t:t + 1]).then_inc(sem.sq, 1)

        def norm_rstd(pool, v):
            for t in range(T):
                pool.wait_ge(sem.sq, T * v + t + 1)
                if v:
                    pool.wait_ge(sem.xn, T * (v - 1) + t + 1)
                pool_link(nc.gpsimd.tensor_scalar(ms[:, t:t + 1], ss[:, t:t + 1], 1.0 / D, EPS, ALU.mult, ALU.add))
                nc.gpsimd.tensor_tensor(rstd[:, t:t + 1], ms[:, t:t + 1], neghalf[:, 0:1], ALU.pow).then_inc(sem.rstd, 1)

        def norm_scale(dve, v, t):
            dve.wait_ge(sem.rstd, T * v + t + 1)
            if T * v + t >= 2:
                dve.wait_ge(sem.xT, 2 * (T * v + t - 1))
            nc.vector.tensor_scalar(xn[:, t % 2, :], X[:, t, :], rstd[:, t:t + 1], None, ALU.mult).then_inc(sem.xn, 1)

        def norm_transpose(pe, v, t):
            pe.wait_ge(sem.xn, T * v + t + 1)
            for half in range(2):
                i = 2 * t + half
                if i >= 4 and v + V0 == 0:
                    pe.wait_ge(sem.hT, 8 * v + i - 3)
                elif i >= 4:
                    pe.wait_ge(sem.x_gained, 8 * (v + V0 - 1) + i - 3)
                for k in range(4):
                    last = nc.tensor.transpose(ps[i % 4][:, P * k:P * k + P],
                                               xn[:, t % 2, 512 * half + P * k:512 * half + P * k + P], ident[:])
                last.then_inc(sem.xT, 1)

        def norm_evacuate(dve, v, t, chunked, low):
            g0 = R_PRE1 if chunked else R_NORM + 8 * (v + V0 - 1)
            for half in range(2):
                i = 2 * t + half
                dve.wait_ge(sem.xT, 8 * v + i + 1)
                gain = cols[:, g0 + 4 * half:g0 + 4 * half + 4]
                if chunked:
                    for k in range(4):
                        src = ps[i % 4][:, P * k:P * k + P].rearrange("p (c i) -> p i c", i=L)
                        dst = HT[:, 4 * half + k, :].rearrange("p (i c) -> p i c", i=L)[:, :, t * (P // L):(t + 1) * (P // L)]
                        last = nc.vector.tensor_scalar(dst, src, gain[:, k:k + 1], None, ALU.mult)
                else:
                    last = nc.vector.tensor_tensor(
                        low[0][:, 4 * half:4 * half + 4, P * t:P * t + P],
                        ps[i % 4][:].rearrange("p (k n) -> p k n", k=4),
                        gain[:, :, None].to_broadcast([P, 4, P]), ALU.mult)
                last.then_inc(sem.hT if chunked else sem.x_gained, 1)

        def norm_parts(low, i):
            k, t = 4 * (i % 2), i // 2
            return [v[:, k:k + 4, P * t:P * t + P] for v in (HT_R, low[1], low[0])]

        def norm_hi(act, v, low, i):
            hi, _, whole = norm_parts(low, i)
            act.wait_ge(sem.x_gained, 8 * (v + V0 - 1) + i + 1)
            nc.scalar.activation(hi, whole, ACT.Copy).then_inc(sem.x_hi, 1)

        def norm_lo(pool, v, low):
            for i in range(8):
                hi, lo, whole = norm_parts(low, i)
                pool.wait_ge(sem.x_hi, 8 * (v + V0 - 1) + i + 1)
                nc.gpsimd.tensor_tensor(lo, whole, hi.bitcast(F32), ALU.subtract).then_inc(sem.hT, 1)

        def norm_dve(dve, v, chunked=False, low=None):
            norm_scale(dve, v, 0)
            norm_scale(dve, v, 1)
            for t in range(T):
                norm_evacuate(dve, v, t, chunked, low)
                if t + 2 < T:
                    norm_scale(dve, v, t + 2)

        def post_squares(act, w, tile_half, ready, first_bank=0):
            for e in range(8):
                t, half = tile_half(e)
                act.wait_ge(*ready(e))
                if w or e:
                    act.wait_ge(sem.post_sq, 8 * w + e)
                if w and e == 0:
                    act.wait_ge(sem.post_rstd, T * w)
                nc.scalar.activation(junk2, ps[(e + first_bank) % 8][:], ACT.Square,
                                     accum_out=pss[:, t, half:half + 1]).then_inc(sem.post_sq, 1)

        def post_factor(pool, w, tile_half):
            last_e = {tile_half(e)[0]: e for e in range(8)}
            for t in range(T):
                pool.wait_ge(sem.post_sq, 8 * w + last_e[t] + 1)
                if w:
                    pool.wait_ge(sem.x_new, T * (w - 1) + t + 1)
                pool_link(nc.gpsimd.tensor_tensor(pms[:, t:t + 1], pss[:, t, 0:1], pss[:, t, 1:2], ALU.add))
                pool_link(nc.gpsimd.tensor_scalar(pms[:, t:t + 1], pms[:, t:t + 1], 1.0 / D, EPS, ALU.mult, ALU.add))
                nc.gpsimd.tensor_tensor(prstd[:, t:t + 1], pms[:, t:t + 1], neghalf[:, 0:1], ALU.pow)\
                    .then_inc(sem.post_rstd, 1)

        def post_add(dve, w, tile_half, first_bank=0):
            dve.wait_ge(sem.postgain_in, 16 * (w + 1))
            last_e = {tile_half(e)[0]: e for e in range(8)}

            def add(t):
                dve.wait_ge(sem.post_rstd, T * w + t + 1)
                dve.wait_ge(sem.post_y, 8 * w + last_e[t] + 1)
                nc.vector.scalar_tensor_tensor(X[:, t, :], Y[:, t, :], prstd[:, t:t + 1], X[:, t, :],
                                               ALU.mult, ALU.add).then_inc(sem.x_new, 1)

            waiting = []
            for e in range(8):
                t, half = tile_half(e)
                dve.wait_ge(sem.post_sq, 8 * w + e + 1)
                nc.vector.tensor_tensor(Y[:, t, 512 * half:512 * half + 512], ps[(e + first_bank) % 8][:],
                                        postg[:, 512 * half:512 * half + 512], ALU.mult).then_inc(sem.post_y, 1)
                if e == last_e[t]:
                    waiting.append(t)
                if len(waiting) > 1:
                    add(waiting.pop(0))
            for t in waiting:
                add(t)

        MIX = lambda e: (e // 2, e % 2)
        MLP = lambda e: (e % 4, e // 4)
        mixed = lambda w: lambda e: (sem.out_ps, 8 * w + e + 1)

        def out_projection(pe, w, weights):
            views = [arrived(pe, n) for n in weights]
            for e in range(8):
                t, half = MIX(e)
                for k in range(KD):
                    last = nc.tensor.matmul(ps[e][:], HT[:, k, P * t:P * t + P], views[k][:, 512 * half:512 * half + 512],
                                            start=(k == 0), stop=(k == KD - 1))
                last.then_inc(sem.out_ps, 1)

        chains = {"act": 0, "dve": 0, "pool": 0}

        def dve_link(ins, eng=nc.vector):
            chains["dve"] += 1
            ins.then_inc(sem.dve_chain, 1)
            eng.wait_ge(sem.dve_chain, chains["dve"])

        def pool_link(ins, eng=nc.gpsimd):
            chains["pool"] += 1
            ins.then_inc(sem.pool_chain, 1)
            eng.wait_ge(sem.pool_chain, chains["pool"])

        def act_link(ins, eng=nc.scalar):
            chains["act"] += 1
            ins.then_inc(sem.act_chain, 1)
            eng.wait_ge(sem.act_chain, chains["act"])

        if first:
            GA, GS = carve(0, T, WIDE), carve(2048, T, WIDE)
            ZT = carve(4096, 4, SEQ)
            YP = carve(6144, T, WIDE)
            ZN = carve(8192, 2, 512)
            UT = carve(9216, G, NC)
            W1 = carve(11264, DQ, P)
            M3 = carve(13312, DQ, NK * CH)
            U8 = BIG[0:NC, 11264:11264 + G * P].rearrange("p (g n) -> p g n", g=G)
            M1 = carve(15616, DQ, L * CH)
            KT = BIG[0:CH, 11264:11264 + GQ * 240].rearrange("p (g n) -> p g n", g=GQ)
            TMP = BIG[:, 17664:17664 + 1152]
            TT = carve(18816, GQ, P)
            CC, SS_ = carve(19840, DQ, NC), carve(20864, DQ, NC)
            SA, SV = carve(21888, DQ, NC), carve(22912, DQ, NC)
            B1_, B2_ = carve(23936, DQ, CH), carve(24192, DQ, CH)
            BB, BW = carve(24448, DQ, CH), carve(24704, DQ, CH)
            C1_, C2_ = carve(24960, 2, P), carve(25216, 2, P)
            CN = carve(25472, 4, P)
            AR, AI = carve(25984, NK, DG), carve(26560, NK, DG)
            WP = BIG[:, 27136:27136 + 2 * 6 * DG].rearrange("p (a n g) -> p a n g", a=2, n=6)
            YS = BIG[:, 8192:8192 + 512]
            LAM = BIG[0:DG, 27904:28160].rearrange("p (a n) -> p a n", a=2)
            DROW = BIG[0:G, 28160:28176]
            PA = BIG[:, 19840:22144].rearrange("p (n g) -> p n g", g=DG)
            LDT = BIG[:, 28176:28240]
            CRE, CIM = BIG[:, 28240:28304], BIG[:, 28304:28368]
            DT_ = BIG[0:CH, 28368:28400]
            DK = BIG[0:CH, 28400:28528].rearrange("p (g n) -> p g n", g=GQ)
            DECAY = BIG[:, 28528:28592]
            zss, zms, zrs = BIG[:, 28592:28594], BIG[:, 28594:28596], BIG[:, 28596:28604].rearrange("p (t n) -> p t n", n=2)
            QN, KN = carve(8192, H1, SEQ), carve(10240, H1, SEQ)
            QR, V1 = carve(12288, 2, SEQ), carve(13312, T, WIDE)
            COS1, SIN1 = BIG[:, 15360:15872], BIG[:, 15872:16384]
            O1 = carve(16384, T, WIDE)
            PR1, PT1 = carve(18432, 2, SEQ), carve(19456, 2, SEQ)
            YG, GT_ = carve(20480, T, WIDE), carve(22528, 4, SEQ)
            GTMP, BGLU = carve(24576, 2, WIDE), BIG[:, 25600:26112]
            ANG, ROT = carve(26112, 2, SEQ), carve(27136, 2, SEQ)
            POS = BIG[:, 24576:25088].bitcast(I32)
            JUNK1 = BIG[:, 28160:28672]
            KRT = ZT[:, 3, :]
            JUNK_Z = BIG[:, 6144:6144 + 256]
            col = sb("col", 8)
            swap1, turn = sb("swap1", P), sb("turn", P)
            ass, ams, ars = sb("ass", 2, T), sb("ams", T), sb("ars", 2, T)

        def one_small():
            return [(col[:], a["c_col"]), (swap1[:], a["c_swap1"]), (turn[:], a["c_turn"])]

        def one_params_dma(act):
            for i, n in enumerate(("s5_lam_re", "s5_lam_im")):
                for o in range(2):
                    act.dma_start(LAM[:, i, ST * o:ST * o + ST], a[n][0].rearrange("d g p -> (d g) p"))\
                        .then_inc(sem.par_in, 16)
            act.dma_start(LDT, a["s5_log_dt"].rearrange("a d g -> a (d g)").to_broadcast([P, DG])).then_inc(sem.par_in, 16)
            act.dma_start(DROW, a["s5_d"][0].rearrange("(g h) -> g h", h=CH)).then_inc(sem.par_in, 16)

        def one_bc_dma(act, q):
            if q:
                act.wait_ge(sem.b_bar, q)
                act.wait_ge(sem.cT_ps, q)
            gs_ = slice(GQ * q, GQ * q + GQ)
            for d in range(2):
                re, im = (a[n][0, d, gs_].rearrange("g p h -> p g h") for n in ("s5_b_re", "s5_b_im"))
                for dst, parts in ((B1_, (re, im)), (B2_, (im, re))):
                    for o in range(2):
                        act.dma_start(dst[ST * o:ST * o + ST, GQ * d:GQ * d + GQ, :], parts[o]).then_inc(sem.bc_in, 16)
                re, im = (a[n][0, d, gs_].rearrange("g h p -> (g h) p") for n in ("s5_c_re", "s5_c_im"))
                for order, parts in enumerate(((re, im), (im, re))):
                    for o in range(2):
                        act.dma_start(CN[:, 2 * order + d, ST * o:ST * o + ST], parts[o]).then_inc(sem.bc_in, 16)

        N_BC = 16 * 2 * 8

        def one_pe(pe):
            pe.wait_ge(sem.par_in, 16 * 6)
            for i in range(2):
                nc.tensor.transpose(ps[6][:, DG * i:DG * i + DG], LAM[:, i, :], ident[0:DG, 0:DG])
            nc.tensor.transpose(ps[6][0:CH, P:P + G], DROW, ident[0:G, 0:G]).then_inc(sem.par_ps, 1)
            for t in range(T):
                norm_transpose(pe, 0, t)
            pe.wait_ge(sem.hT, 8)

            def natural(name, n, m, width, done):
                wv = block_of(name, pe, 512)
                for k in range(KD):
                    last = nc.tensor.matmul(ps[n % 4][:, 0:width], HT[:, k, P * m:P * m + P], wv[:, k, 0:width],
                                            start=(k == 0), stop=(k == KD - 1))
                last.then_inc(done, 1)

            for m in range(T):
                natural("u", m, m, 512, sem.u_ps)
            for m in range(T):
                pe.wait_ge(sem.u_sb, m + 1)
                natural("gs", m, m, 512, sem.gs_ps)
            pe.wait_ge(sem.par, 1)
            for b in range(4):
                for g in range(8):
                    last = nc.tensor.transpose(ps[4 + b][:, NC * g:NC * g + NC], U8[:, 8 * b + g, :], ident[0:NC, 0:NC])
                last.then_inc(sem.uT_ps, 1)
            for m in range(T):
                pe.wait_ge(sem.gs, m + 1)
                natural("za", m, m, 448, sem.za_ps)
            for m in range(T):
                pe.wait_ge(sem.zn, m + 1)
                natural("ga", m, m, 512, sem.ga_ps)
                pe.wait_ge(sem.uT, m + 1)
                for k in range(4):
                    last = nc.tensor.transpose(ps[4 + m][:, P * k:P * k + P], ZN[:, m % 2, P * k:P * k + P], ident[:])
                last.then_inc(sem.znT_ps, 1)
            pe.wait_ge(sem.ga, T)
            pe.wait_ge(sem.znT, T)
            s5_pe_front(pe, 0)
            for q in range(NQ):
                s5_pe_states(pe, q)
                s5_pe_outputs(pe, q)
                if q + 1 < NQ:
                    s5_pe_front(pe, q + 1)
                s5_pe_turn(pe, q)
            glu_pe(pe)
            latent_pe(pe)
            attention_pe(pe)
            mix_pe(pe)

        def s5_pe_front(pe, q):
            pe.wait_ge(sem.bc_in, N_BC * (q + 1))
            if q:
                pe.wait_ge(sem.taps, q)
            for j in range(4):
                last = nc.tensor.transpose(ps[7][:, P * j:P * j + P], CN[:, j, :], ident[:])
            last.then_inc(sem.cT_ps, 1)
            pe.wait_ge(sem.m1, q + 1)
            if q:
                pe.wait_ge(sem.st_sb, 2 * q)
                pe.wait_ge(sem.turned, 4 * q)
            for b in range(4):
                for j in range(4):
                    last = nc.tensor.transpose(ps[b][:, P * j:P * j + P], M1[:, 4 * b + j, :], ident[:])
                last.then_inc(sem.m1T_ps, 1)

        def s5_pe_states(pe, q):
            pe.wait_ge(sem.w1T, 4 * (q + 1))
            for d in range(2):
                for g in range(GQ):
                    u = UT[:, GQ * q + g, :]
                    last = nc.tensor.matmul(ps[d][:, NC * g:NC * g + NC], W1[:, GQ * d + g, :], u[:, ::-1] if d else u,
                                            start=True, stop=True)
                last.then_inc(sem.st_ps, 1)
            def by_minus_i(r):
                for d in range(2):
                    if r == 0:
                        pe.wait_ge(sem.st_sb, 2 * q + d + 1)
                    else:
                        pe.wait_ge(sem.state, 3 * q + d + 1)
                        pe.wait_ge(sem.turned, 4 * q + d + 1)
                    nc.tensor.matmul(ps[2 + d][:], turn[:], SA[:, GQ * d:GQ * d + GQ, :].rearrange("p g c -> p (g c)"),
                                     start=True, stop=True).then_inc(sem.turn_ps, 1)

            by_minus_i(0)
            pe.wait_ge(sem.m3, q + 1)
            pe.wait_ge(sem.cT, q + 1)
            pe.wait_ge(sem.b_bar, q + 1)
            if q:
                pe.wait_ge(sem.yp, 2 * q)
                pe.wait_ge(sem.y_sb, q)
            for b in range(2):
                for j in range(4):
                    g = 4 * b + j
                    lo = ps[4 + b][0:CH, P * j:P * j + P]
                    nc.tensor.matmul(lo, BB[:, GQ + g, :], M3[:, GQ + g, CH:NK * CH], start=True, stop=True)
                    nc.tensor.matmul(lo[:, P - CH:P], BB[:, g, :], M3[:, g, 0:CH], start=False, stop=True,
                                     skip_group_check=True)
                    last = nc.tensor.matmul(ps[6 + b][0:CH, 112 * j:112 * j + 112], BB[:, g, :], M3[:, g, CH:L * CH],
                                            start=True, stop=True)
                last.then_inc(sem.tap_ps, 1)
            by_minus_i(1)

        def s5_pe_outputs(pe, q):
            pe.wait_ge(sem.toep, 128 * (q + 1))
            pe.wait_ge(sem.state, 3 * q + 3)
            for g in range(GQ):
                y = ps[6][:, NC * g:NC * g + NC]
                nc.tensor.matmul(y, TT[:, g, :], UT[:, GQ * q + g, :], start=True, stop=True)
                nc.tensor.matmul(y[:, 1:NC], M3[:, g, CH:NK * CH], SV[:, g, 0:NC - 1], start=False, stop=True,
                                 skip_group_check=True)
                last = nc.tensor.matmul(y[:, 0:NC - 1], M3[:, GQ + g, 0:L * CH], SV[:, GQ + g, 0:NC - 1][:, ::-1],
                                        start=False, stop=True, skip_group_check=True)
            last.then_inc(sem.y_ps, 1)

        def s5_pe_turn(pe, q):
            pe.wait_ge(sem.y_sb, q + 1)
            for b in range(2):
                for j in range(4):
                    g = 4 * b + j
                    last = nc.tensor.transpose(ps[4 + b][0:NC, P * j:P * j + P], YS[:, NC * g:NC * g + NC], ident[:])
                last.then_inc(sem.yT_ps, 1)

        def glu_pe(pe):
            pe.wait_ge(sem.ge, 1)
            pe.wait_ge(sem.yp, 2 * NQ)
            pe.wait_ge(sem.y_sb, NQ)
            pe.wait_ge(sem.turned, 4 * NQ)
            for m in range(T):
                for k in range(4):
                    last = nc.tensor.transpose(ps[m][:, P * k:P * k + P], YG[:, m, P * k:P * k + P], ident[:])
                last.then_inc(sem.geT_ps, 1)
            wv = block_of("glu", pe, 512)
            for m in range(T):
                pe.wait_ge(sem.geT, m + 1)
                for k in range(4):
                    last = nc.tensor.matmul(ps[4 + m][:], GT_[:, k, P * m:P * m + P], wv[:, k, :], start=(k == 0), stop=(k == 3))
                last.then_inc(sem.glu_ps, 1)

        def latent_pe(pe):
            wq = arrived(pe, "uq")
            for h in range(H1):
                pe.wait_ge(sem.geT, h + 1)
                for k in range(2):
                    last = nc.tensor.matmul(ps[h][:], wq[:, 768 * k + P * h:768 * k + P * h + P], ZT[:, k, :],
                                            start=(k == 0), stop=(k == 1))
                last.then_inc(sem.qn_ps, 1)
            for r in range(2):
                pe.wait_ge(sem.glu_x, r + 1)
                for k in range(2):
                    c = 768 * k + 512 + P * r
                    last = nc.tensor.matmul(ps[4 + r][:], wq[:, c:c + P], ZT[:, k, :], start=(k == 0), stop=(k == 1))
                last.then_inc(sem.rq_ps, 1)
            wk = arrived(pe, "ukv")
            for h in range(H1):
                pe.wait_ge(sem.qn, h + 1)
                nc.tensor.matmul(ps[h][:], wk[:, 256 * h:256 * h + P], ZT[:, 2, :], start=True, stop=True).then_inc(sem.kn_ps, 1)
            for r in range(3):
                b = 6 + r % 2
                if r == 0:
                    pe.wait_ge(sem.glu_x, 4)
                else:
                    pe.wait_ge(sem.rq, r)
                if r == 2:
                    pe.wait_ge(sem.rope_done, 1)
                nc.tensor.matmul(ps[b][:], swap1[:], KRT if r == 0 else QR[:, r - 1, :], start=True, stop=True)\
                    .then_inc(sem.rope_ps, 1)
            wvv = wk.rearrange("p (h c) -> p h c", h=H1)[:, :, NOPE:NOPE + VD]
            for m in range(T):
                pe.wait_ge(sem.kn, m + 1)
                nc.tensor.matmul(ps[m][:], ZT[:, 2, P * m:P * m + P], wvv, start=True, stop=True).then_inc(sem.v1_ps, 1)

        NU1 = H1 * T

        def attention_pe(pe):
            pe.wait_ge(sem.v1, T)
            pe.wait_ge(sem.rope_done, 3)
            pe.wait_ge(sem.rq, 2)
            pe.wait_ge(sem.qn, H1)
            pe.wait_ge(sem.kn, H1)
            for u in range(NU1 + 4):
                if u < NU1:
                    h, m = u // T, u % T
                    if u >= 3:
                        pe.wait_ge(sem.a_exp, u - 2)
                    tok = slice(P * m, P * m + P)
                    nc.tensor.matmul(ps[u % 3][:], QN[:, h, tok], KN[:, h, :], start=True, stop=False)
                    o = 64 * (h % 2)
                    nc.tensor.matmul(ps[u % 3][:], QR[o:o + 64, h // 2, tok], KRT[o:o + 64, :], start=False, stop=True)\
                        .then_inc(sem.a_s_ps, 1)
                w = u - 2
                if 0 <= w < NU1:
                    pe.wait_ge(sem.a_exp, w + 1)
                    if w >= 2:
                        pe.wait_ge(sem.a_pT, w - 1)
                    for b in range(T):
                        last = nc.tensor.transpose(ps[3 + w % 2][:, P * b:P * b + P], PR1[:, w % 2, P * b:P * b + P], ident[:])
                    last.then_inc(sem.a_pT_ps, 1)
                w = u - 3
                if 0 <= w < NU1:
                    h, m = w // T, w % T
                    pe.wait_ge(sem.a_pT, w + 1)
                    if m == 0 and h >= 2:
                        pe.wait_ge(sem.a_o, h - 1)
                    for b in range(T):
                        last = nc.tensor.matmul(ps[5 + h % 2][:, P * m:P * m + P], PT1[:, w % 2, P * b:P * b + P],
                                                V1[:, b, P * h:P * h + P], start=(b == 0), stop=(b == T - 1))
                    last.then_inc(sem.a_o_ps, 1)

        def mix_pe(pe):
            for i in range(8):
                m = i % 4
                if i < 4:
                    pe.wait_ge(sem.ssm_o, m + 1)
                    src = YG[:, m, :]
                else:
                    pe.wait_ge(sem.at_o, m + 1)
                    src = O1[:, m, :]
                if i == 0:
                    pe.wait_ge(sem.a_o, H1)
                for k in range(4):
                    last = nc.tensor.transpose(ps[i][:, P * k:P * k + P], src[:, P * k:P * k + P], ident[:])
                last.then_inc(sem.m1ix_ps, 1)
            pe.wait_ge(sem.m1ix, 8)
            out_projection(pe, 0, [f"wo{k}" for k in range(KD)])

        TT2 = nc.vector.tensor_tensor
        TS = nc.vector.tensor_scalar

        def reduce_angle(x, t1, t2):
            dve_link(TS(t1, x, 1.0 / TWO_PI, ROUND, ALU.mult, ALU.add))
            dve_link(TS(t1, t1, ROUND, None, ALU.subtract))
            for part in (PI2_A, PI2_B, PI2_C):
                dve_link(nc.vector.scalar_tensor_tensor(x, t1, -part, x, ALU.mult, ALU.add))
            dve_link(TS(t1, x, PI_SAFE, -PI_SAFE, ALU.min, ALU.max))
            dve_link(TS(t2, t1, -1.0, None, ALU.mult))
            dve_link(TT2(t2, t2, t1, ALU.max))
            return TS(t2, t2, -1.0, float(np.float32(np.pi / 2)), ALU.mult, ALU.add)

        def cmul(out_c, out_s, ac, as_, bc, bs, t1, t2):
            TT2(t1, as_, bs, ALU.mult)
            TT2(t2, as_, bc, ALU.mult)
            TT2(out_c, ac, bc, ALU.mult)
            dve_link(TT2(out_s, ac, bs, ALU.mult))
            TT2(out_c, out_c, t1, ALU.subtract)
            dve_link(TT2(out_s, out_s, t2, ALU.add))

        def one_params(dve):
            LR, LI, TH, ER, SN, CS_, DEN, T1, T2 = (PA[:, i, :] for i in range(9))
            UC, US, EA = PA[:, 9:18, :], PA[:, 18:27, :], PA[:, 27:36, :]
            dve.wait_ge(sem.par_ps, 1)
            TS(LR, ps[6][:, 0:DG], -1e-4, None, ALU.min)
            nc.vector.tensor_copy(LI, ps[6][:, DG:2 * DG])
            dve_link(nc.vector.tensor_copy(DT_, ps[6][0:CH, P:P + G]))
            dve.wait_ge(sem.dt_e, 1)
            dve_link(TT2(TH, LI, LDT, ALU.mult))
            TT2(ER, LR, LDT, ALU.mult).then_inc(sem.par_exp, 1)
            reduce_angle(TH, T1, T2).then_inc(sem.par_exp, 1)
            dve.wait_ge(sem.par_trig, 2)
            dve.wait_ge(sem.amp, NK)
            dve_link(TT2(T1, CS_, EA[:, 1, :], ALU.mult))
            TT2(T2, SN, EA[:, 1, :], ALU.mult)
            dve_link(TS(T1, T1, 1.0, None, ALU.subtract))
            TT2(CRE, T1, LR, ALU.mult)
            TT2(CIM, T2, LR, ALU.mult)
            dve_link(TT2(T1, T1, LI, ALU.mult))
            dve_link(TT2(T2, T2, LI, ALU.mult))
            dve_link(TT2(CRE, CRE, T2, ALU.add))
            dve_link(TT2(CIM, CIM, T1, ALU.subtract))
            dve_link(TT2(T1, LR, LR, ALU.mult))
            dve_link(TT2(DEN, LI, LI, ALU.mult))
            dve_link(TT2(DEN, DEN, T1, ALU.add))
            dve_link(nc.vector.reciprocal(DEN, DEN))
            dve_link(TT2(CRE, CRE, DEN, ALU.mult))
            dve_link(TT2(CIM, CIM, DEN, ALU.mult))
            dve_link(TS(CIM, CIM, col[:, 2:3], None, ALU.mult))
            nc.vector.memset(UC[:, 0, :], 1.0)
            nc.vector.memset(US[:, 0, :], 0.0)
            nc.vector.tensor_copy(UC[:, 1, :], CS_)
            dve_link(nc.vector.tensor_copy(US[:, 1, :], SN))
            n = 1
            while n < L:
                b = lambda v: v[:, n:n + 1, :].to_broadcast([P, n, DG])
                t1, t2 = TMP[:, 0:n * DG].rearrange("p (n g) -> p n g", g=DG), TMP[:, 512:512 + n * DG].rearrange("p (n g) -> p n g", g=DG)
                cmul(UC[:, n + 1:2 * n + 1, :], US[:, n + 1:2 * n + 1, :], UC[:, 1:n + 1, :], US[:, 1:n + 1, :], b(UC), b(US), t1, t2)
                n *= 2
            TT2(AR, UC, EA, ALU.mult)
            dve_link(TT2(AI, US, EA, ALU.mult))
            nc.vector.tensor_copy(DECAY, EA[:, L, :])
            nc.vector.tensor_copy(WP[:, 0, 0, :], UC[:, L, :])
            dve_link(nc.vector.tensor_copy(WP[:, 1, 0, :], US[:, L, :]))
            for n in range(5):
                c, s = WP[:, 0, n, :], WP[:, 1, n, :]
                cmul(WP[:, 0, n + 1, :], WP[:, 1, n + 1, :], c, s, c, s, TMP[:, 0:DG], TMP[:, DG:2 * DG])
            nc.vector.tensor_copy(T1, T1).then_inc(sem.par, 1)
            dve.wait_ge(sem.par, 1)

        def by_group(v, q, d):
            return v[:, :, G * d + GQ * q:G * d + GQ * q + GQ].rearrange("p k g -> p g k")

        def s5_prepare(dve, q):
            def pg(v, width):
                w = v.rearrange("p (d g) -> p d g", d=2)[:, :, GQ * q:GQ * q + GQ]
                return w[:, :, :, None].to_broadcast([P, 2, GQ, width])

            four = lambda v: v.rearrange("p (d g) n -> p d g n", d=2)
            if q:
                dve.wait_ge(sem.state, 3 * q)
            nc.vector.memset(CC[:, :, 0:1], 1.0)
            dve_link(nc.vector.memset(SS_[:, :, 0:1], 0.0))
            for s in range(6):
                n = 2 ** s
                t = TMP[:, 0:DQ * n].rearrange("p (d g n) -> p d g n", d=2, n=n)
                t2 = four(SA)[:, :, :, 0:n]
                wc, ws = pg(WP[:, 0, s, :], n), pg(WP[:, 1, s, :], n)
                cmul(four(CC)[:, :, :, n:2 * n], four(SS_)[:, :, :, n:2 * n], four(CC)[:, :, :, 0:n], four(SS_)[:, :, :, 0:n],
                     wc, ws, t, t2)
            dve.wait_ge(sem.bc_in, N_BC * (q + 1))
            if q:
                dve.wait_ge(sem.tap_ps, 2 * q)
            t = TMP[:, 0:DQ * CH].rearrange("p (d g n) -> p d g n", d=2, n=CH)
            t2 = TMP[:, 512:512 + DQ * CH].rearrange("p (d g n) -> p d g n", d=2, n=CH)
            TT2(four(BB), pg(CRE, CH), four(B1_), ALU.mult)
            TT2(t, pg(CIM, CH), four(B2_), ALU.mult)
            TT2(four(BW), pg(CRE, CH), four(B2_), ALU.mult)
            dve_link(TT2(t2, pg(CIM, CH), four(B1_), ALU.mult))
            TT2(four(BB), four(BB), t, ALU.add)
            TT2(four(BW), four(BW), t2, ALU.subtract).then_inc(sem.b_bar, 1)
            dve.wait_ge(sem.b_bar, q + 1)
            if q:
                dve.wait_ge(sem.m1T_ps, 4 * q)
            for d in range(2):
                step = slice(L - 1, None, -1) if d == 0 else slice(0, L)
                m = M1[:, GQ * d:GQ * d + GQ, :].rearrange("p g (k n) -> p g k n", n=CH)
                t = TMP[:, 0:GQ * P].rearrange("p (g k n) -> p g k n", g=GQ, n=CH)
                ar = by_group(AR, q, d)[:, :, step][:, :, :, None].to_broadcast([P, GQ, L, CH])
                ai = by_group(AI, q, d)[:, :, step][:, :, :, None].to_broadcast([P, GQ, L, CH])
                bb = BB[:, GQ * d:GQ * d + GQ, None, :].to_broadcast([P, GQ, L, CH])
                bw = BW[:, GQ * d:GQ * d + GQ, None, :].to_broadcast([P, GQ, L, CH])
                TT2(m, ar, bb, ALU.mult)
                dve_link(TT2(t, ai, bw, ALU.mult))
                last = nc.vector.scalar_tensor_tensor(
                    M1[:, GQ * d:GQ * d + GQ, :].rearrange("p g n -> p (g n)"), TMP[:, 0:GQ * P], col[:, 2:3],
                    M1[:, GQ * d:GQ * d + GQ, :].rearrange("p g n -> p (g n)"), ALU.mult, ALU.add)
                if d == 0:
                    dve_link(last)
            last.then_inc(sem.m1, 1)
            dve.wait_ge(sem.m1, q + 1)

        def s5_turn_c(dve, q):
            dve.wait_ge(sem.cT_ps, q + 1)
            TS(C1_.rearrange("p a n -> p (a n)"), ps[7][:, 0:256], col[:, 2:3], -1.0, ALU.mult, ALU.mult)
            TS(C2_.rearrange("p a n -> p (a n)"), ps[7][:, 256:512], -1.0, None, ALU.mult).then_inc(sem.cT, 1)
            dve.wait_ge(sem.cT, q + 1)

        def s5_taps_basis(dve, q):
            if q:
                dve.wait_ge(sem.y_ps, q)
            for d in range(2):
                if q and d:
                    s5_outputs(dve, q - 1)
                step = slice(0, NK) if d == 0 else slice(NK - 1, None, -1)
                m = M3[:, GQ * d:GQ * d + GQ, :].rearrange("p g (k n) -> p g k n", n=CH)
                t = TMP[:, 0:GQ * NK * CH].rearrange("p (g k n) -> p g k n", g=GQ, n=CH)
                ar = by_group(AR, q, d)[:, :, step][:, :, :, None].to_broadcast([P, GQ, NK, CH])
                ai = by_group(AI, q, d)[:, :, step][:, :, :, None].to_broadcast([P, GQ, NK, CH])
                c1 = C1_[:, d, :].rearrange("p (g n) -> p g n", g=GQ)[:, :, None, :].to_broadcast([P, GQ, NK, CH])
                c2 = C2_[:, d, :].rearrange("p (g n) -> p g n", g=GQ)[:, :, None, :].to_broadcast([P, GQ, NK, CH])
                TT2(m, ar, c1, ALU.mult)
                dve_link(TT2(t, ai, c2, ALU.mult))
                last = TT2(m, m, t, ALU.add)
                if d == 0:
                    dve_link(last)
            last.then_inc(sem.m3, 1)
            dve.wait_ge(sem.m3, q + 1)

        def s5_main(dve, q):
            flat = lambda v, d: v[:, GQ * d:GQ * d + GQ, :].rearrange("p g c -> p (g c)")

            def turn_back(d):
                dve.wait_ge(sem.st_sb, 2 * q + d + 1)
                TT2(flat(SV, d), flat(CC, d), flat(SA, d), ALU.mult)
                dve.wait_ge(sem.turn_ps, 4 * q + d + 1)
                dve_link(TT2(ps[2 + d][:], ps[2 + d][:], flat(SS_, d), ALU.mult))
                TT2(flat(SV, d), flat(SV, d), ps[2 + d][:], ALU.add).then_inc(sem.turned, 1)
                dve.wait_ge(sem.turned, 4 * q + d + 1)

            turn_back(0)
            for b in range(2):
                dve.wait_ge(sem.tap_ps, 2 * q + b + 1)
                r = slice(4 * b, 4 * b + 4)
                nc.vector.tensor_copy(KT[:, r, 0:P], ps[4 + b][0:CH, :].rearrange("p (g n) -> p g n", g=4))
                dve_link(nc.vector.tensor_copy(KT[:, r, P:P + 112], ps[6 + b][0:CH, 0:448].rearrange("p (g n) -> p g n", g=4)))
            dve_link(TT2(DK, ident[0:CH, None, 0:CH].to_broadcast([CH, GQ, CH]),
                         DT_[:, GQ * q:GQ * q + GQ, None].to_broadcast([CH, GQ, CH]), ALU.mult))
            TT2(KT[:, :, P - CH:P], KT[:, :, P - CH:P], DK, ALU.add).then_inc(sem.taps, 1)
            for d in range(2):
                if d:
                    turn_back(1)
                for g in range(GQ):
                    dg = G * d + GQ * q + g
                    last = nc.vector.tensor_tensor_scan(SA[:, GQ * d + g, :], DECAY[:, dg:dg + 1].to_broadcast([P, NC]),
                                                        SV[:, GQ * d + g, :], 0.0, ALU.mult, ALU.add)
                last.then_inc(sem.state, 1)
            for d in range(2):
                dve.wait_ge(sem.state, 3 * q + d + 1)
                dve.wait_ge(sem.turn_ps, 4 * q + d + 3)
                TT2(flat(SV, d), flat(CC, d), flat(SA, d), ALU.mult)
                dve_link(TT2(ps[2 + d][:], ps[2 + d][:], flat(SS_, d), ALU.mult))
                TT2(flat(SV, d), flat(SV, d), ps[2 + d][:], ALU.subtract).then_inc(sem.turned, 1)
                dve.wait_ge(sem.turned, 4 * q + d + 3)
            nc.vector.tensor_copy(DK[:, 0, 0:1], DK[:, 0, 0:1]).then_inc(sem.state, 1)

        def s5_outputs(dve, q):
            for b in range(2):
                dve.wait_ge(sem.yT_ps, 2 * q + b + 1)
                src = ps[4 + b][0:NC, :].rearrange("p (g m i n) -> p i m g n", g=4, m=T, i=2)
                for i in range(2):
                    c = CH * (GQ * q + 4 * b)
                    dst = YP[NC * i:NC * i + NC, :, c:c + 4 * CH].rearrange("p m (g n) -> p m g n", g=4)
                    last = nc.vector.tensor_copy(dst, src[:, i, :, :, :])
                last.then_inc(sem.yp, 1)

        def one_dve(dve):
            norm_dve(dve, 0, chunked=True)
            one_params(dve)
            s5_prepare(dve, 0)
            for b in range(4):
                dve.wait_ge(sem.uT_ps, b + 1)
                nc.vector.tensor_copy(UT[:, 8 * b:8 * b + 8, :], ps[4 + b][:].rearrange("p (g c) -> p g c", g=8)).then_inc(sem.uT, 1)
            for m in range(T):
                dve.wait_ge(sem.za_rstd, m + 1)
                if m >= 2:
                    dve.wait_ge(sem.znT_ps, m - 1)
                z = ZN[:, m % 2, :]
                TS(z[:, 0:256], ps[m][:, 0:256], zrs[:, m, 0:1], None, ALU.mult)
                TS(z[:, 256:384], ps[m][:, 256:384], zrs[:, m, 1:2], None, ALU.mult)
                nc.vector.tensor_copy(z[:, 384:448], ps[m][:, 384:448])
                nc.vector.tensor_copy(z[:, 448:512], ps[m][:, 384:448]).then_inc(sem.zn, 1)
                if m >= 1:
                    znT_copy(dve, m - 1)
            znT_copy(dve, T - 1)
            s5_turn_c(dve, 0)
            s5_taps_basis(dve, 0)
            for q in range(NQ):
                s5_main(dve, q)
                if q + 1 < NQ:
                    s5_prepare(dve, q + 1)
                    s5_turn_c(dve, q + 1)
                    s5_taps_basis(dve, q + 1)
            s5_outputs(dve, NQ - 1)
            for m in range(T):
                dve.wait_ge(sem.geT_ps, m + 1)
                nc.vector.tensor_copy(GT_[:, :, P * m:P * m + P], ps[m][:].rearrange("p (k n) -> p k n", k=4)).then_inc(sem.geT, 1)
            dve.wait_ge(sem.pos_in, 32)
            ang = ANG[:, 0, :]
            dve_link(nc.vector.tensor_copy(ANG[:, 1, :].rearrange("p (i c) -> p i c", i=L), POS.rearrange("p (c i) -> p i c", i=L)))
            dve_link(TS(ang, ANG[:, 1, :], col[:, 0:1], None, ALU.mult))
            reduce_angle(ang, ROT[:, 0, :], ROT[:, 1, :]).then_inc(sem.angle, 1)
            dve.wait_ge(sem.trig, 2)
            TS(SIN1, SIN1, col[:, 1:2], None, ALU.mult).then_inc(sem.angle, 1)
            dve.wait_ge(sem.angle, 2)
            for m in range(T):
                dve.wait_ge(sem.glu_ps, m + 1)
                if m >= 2:
                    dve.wait_ge(sem.glu_y, m - 1)
                TT2(GTMP[:, m % 2, :], ps[4 + m][:], BGLU, ALU.add).then_inc(sem.glu_x, 1)
                if m >= 1:
                    glu_gate(dve, m - 1)
            glu_gate(dve, T - 1)
            for r in range(3):
                raw = KRT if r == 0 else QR[:, r - 1, :]
                b = 6 + r % 2
                dve.wait_ge(sem.rope_ps, r + 1)
                TT2(ROT[:, r % 2, :], raw, COS1, ALU.mult)
                dve_link(TT2(ps[b][:], ps[b][:], SIN1, ALU.mult))
                TT2(raw, ROT[:, r % 2, :], ps[b][:], ALU.add).then_inc(sem.rope_done, 1)
            for m in range(T):
                dve.wait_ge(sem.mixer_rstd, m + 1)
                nc.vector.scalar_tensor_tensor(YG[:, m, :], YG[:, m, :], ars[:, 0, m:m + 1], GS[:, m, :], ALU.mult, ALU.mult)\
                    .then_inc(sem.ssm_o, 1)
            for u in range(NU1 + 4):
                if u < NU1:
                    dve.wait_ge(sem.a_s_ps, u + 1)
                    if u >= 4:
                        dve.wait_ge(sem.a_exp, u - 3)
                    nc.vector.tensor_reduce(mn[:, u % 4:u % 4 + 1], ps[u % 3][:], AX_X, ALU.min).then_inc(sem.a_min, 1)
                z = u - 2
                if 0 <= z < NU1:
                    dve.wait_ge(sem.a_pT_ps, z + 1)
                    if z >= 2:
                        dve.wait_ge(sem.a_o_ps, z - 1)
                    nc.vector.tensor_copy(PT1[:, z % 2, :], ps[3 + z % 2][:]).then_inc(sem.a_pT, 1)
                z = u - 4
                if z >= 0 and z % 4 == 3:
                    h = z // 4
                    dve.wait_ge(sem.a_exp, z + 1)
                    r = rg[:, h % 3, :]
                    dve_link(nc.vector.reciprocal(r, rs[:, 4 * h:4 * h + 4]))
                    dve.wait_ge(sem.a_o_ps, z + 1)
                    for m in range(T):
                        last = TS(O1[:, m, P * h:P * h + P], ps[5 + h % 2][:, P * m:P * m + P], r[:, m:m + 1], None, ALU.mult)
                    last.then_inc(sem.a_o, 1)
            for m in range(T):
                mix1_copy(dve, m, m, R_SO, 4)
            for m in range(T):
                dve.wait_ge(sem.mixer_rstd, T + m + 1)
                nc.vector.scalar_tensor_tensor(O1[:, m, :], O1[:, m, :], ars[:, 1, m:m + 1], GA[:, m, :], ALU.mult, ALU.mult)\
                    .then_inc(sem.at_o, 1)
            for m in range(T):
                mix1_copy(dve, 4 + m, m, R_AO, 0)
            post_add(dve, 0, MIX)

        def mix1_copy(dve, i, m, row, k0):
            dve.wait_ge(sem.m1ix_ps, i + 1)
            dst = HT[:, k0:k0 + 4, :].rearrange("p k (c i) -> p k i c", i=L)[:, :, 2 * m:2 * m + 2, :]
            for k in range(4):
                last = TS(dst[:, k, :, :], ps[i][:, P * k:P * k + P].rearrange("p (i c) -> p i c", i=2),
                          cols[:, row + k:row + k + 1], None, ALU.mult)
            last.then_inc(sem.m1ix, 1)

        def znT_copy(dve, m):
            dve.wait_ge(sem.znT_ps, m + 1)
            src = ps[4 + m][:].rearrange("p (k n) -> p k n", k=4)
            TT2(ZT[:, 0:3, P * m:P * m + P], src[:, 0:3, :], cols[:, R_QN:R_QN + 3, None].to_broadcast([P, 3, P]), ALU.mult)
            nc.vector.tensor_copy(ZT[:, 3, P * m:P * m + P], src[:, 3, :]).then_inc(sem.znT, 1)

        def glu_gate(dve, m):
            dve.wait_ge(sem.glu_s, m + 1)
            TT2(YG[:, m, :], YG[:, m, :], GTMP[:, m % 2, :], ALU.mult).then_inc(sem.glu_y, 1)

        def one_act(act, post_gain):
            one_params_dma(act)
            one_bc_dma(act, 0)
            norm_squares(act, 0, lambda t: x_tile(-1, t))
            act.wait_ge(sem.par_in, 16 * 6)
            nc.scalar.activation(LDT, LDT, ACT.Exp).then_inc(sem.dt_e, 1)
            EA, CS_, SN, T1, T2, ER = PA[:, 27:36, :], PA[:, 5, :], PA[:, 4, :], PA[:, 7, :], PA[:, 8, :], PA[:, 3, :]
            act.wait_ge(sem.par_exp, 1)
            for k in range(NK):
                nc.scalar.activation(EA[:, k, :], ER, ACT.Exp, scale=float(k)).then_inc(sem.amp, 1)
            act.wait_ge(sem.par_exp, 2)
            nc.scalar.activation(SN, T1, ACT.Sin).then_inc(sem.par_trig, 1)
            nc.scalar.activation(CS_, T2, ACT.Sin).then_inc(sem.par_trig, 1)
            post_gain(0, a["post_norm_g"])
            for m in range(T):
                act.wait_ge(sem.u_ps, m + 1)
                for i in range(2):
                    dst = U8[:, :, CH * (2 * m + i):CH * (2 * m + i) + CH]
                    last = nc.scalar.activation(dst, ps[m][NC * i:NC * i + NC, :].rearrange("p (g n) -> p g n", g=G), ACT.Copy)
                last.then_inc(sem.u_sb, 1)
            for m in range(T):
                act.wait_ge(sem.gs_ps, m + 1)
                nc.scalar.activation(GS[:, m, :], ps[m][:], ACT.Silu).then_inc(sem.gs, 1)
            for m in range(T):
                act.wait_ge(sem.za_ps, m + 1)
                if m:
                    act.wait_ge(sem.za_rstd, m)
                act_link(nc.scalar.activation(JUNK_Z[:, 0:256], ps[m][:, 0:256], ACT.Square, accum_out=zss[:, 0:1]))
                nc.scalar.activation(JUNK_Z[:, 0:128], ps[m][:, 256:384], ACT.Square, accum_out=zss[:, 1:2]).then_inc(sem.za_sq, 1)
                if m < T - 1:
                    act.wait_ge(sem.za_sq, m + 1)
            for m in range(T):
                act.wait_ge(sem.ga_ps, m + 1)
                nc.scalar.activation(GA[:, m, :], ps[m][:], ACT.Silu).then_inc(sem.ga, 1)
            def turn_outputs(q):
                act.wait_ge(sem.y_ps, q + 1)
                nc.scalar.activation(YS, ps[6][:], ACT.Copy).then_inc(sem.y_sb, 1)

            for q in range(NQ):
                for b in range(4):
                    act.wait_ge(sem.m1T_ps, 4 * q + b + 1)
                    if b == 0:
                        act.wait_ge(sem.uT_ps, 4)
                        if q:
                            act.wait_ge(sem.st_ps, 2 * q)
                            act.wait_ge(sem.toep, 128 * q)
                    nc.scalar.activation(W1[:, 4 * b:4 * b + 4, :], ps[b][:].rearrange("p (g n) -> p g n", g=4), ACT.Copy)\
                        .then_inc(sem.w1T, 1)
                if q:
                    turn_outputs(q - 1)
                for d in range(2):
                    act.wait_ge(sem.st_ps, 2 * q + d + 1)
                    nc.scalar.activation(SA[:, GQ * d:GQ * d + GQ, :], ps[d][:].rearrange("p (g c) -> p g c", g=GQ), ACT.Copy)\
                        .then_inc(sem.st_sb, 1)
                act.wait_ge(sem.taps, q + 1)
                if q:
                    act.wait_ge(sem.y_ps, q)
                for i in range(L):
                    c = CH * (L - 1 - i)
                    act.dma_start(TT[CH * i:CH * i + CH, :, :], KT[:, :, c:c + P]).then_inc(sem.toep, 16)
            turn_outputs(NQ - 1)
            act.wait_ge(sem.yp, 2 * NQ)
            nc.scalar.activation(YG, YP, ACT.Gelu_apprx_tanh).then_inc(sem.ge, 1)
            act.wait_ge(sem.state, 3 * NQ)
            act.dma_start(POS, a["positions"].to_broadcast([P, SEQ])).then_inc(sem.pos_in, 16)
            act.dma_start(BGLU, a["b_glu"].to_broadcast([P, WIDE])).then_inc(sem.pos_in, 16)
            act.wait_ge(sem.angle, 1)
            nc.scalar.activation(SIN1, ROT[:, 0, :], ACT.Sin).then_inc(sem.trig, 1)
            nc.scalar.activation(COS1, ROT[:, 1, :], ACT.Sin).then_inc(sem.trig, 1)
            for m in range(T):
                act.wait_ge(sem.glu_x, m + 1)
                nc.scalar.activation(GTMP[:, m % 2, :], GTMP[:, m % 2, :], ACT.Sigmoid).then_inc(sem.glu_s, 1)
            for h in range(H1):
                act.wait_ge(sem.qn_ps, h + 1)
                nc.scalar.activation(QN[:, h, :], ps[h][:], ACT.Copy, scale=-SCALE1).then_inc(sem.qn, 1)
            for r in range(2):
                act.wait_ge(sem.rq_ps, r + 1)
                nc.scalar.activation(QR[:, r, :], ps[4 + r][:], ACT.Copy, scale=-SCALE1).then_inc(sem.rq, 1)
            for h in range(H1):
                act.wait_ge(sem.kn_ps, h + 1)
                nc.scalar.activation(KN[:, h, :], ps[h][:], ACT.Copy).then_inc(sem.kn, 1)
            for m in range(T):
                act.wait_ge(sem.v1_ps, m + 1)
                nc.scalar.activation(V1[:, m, :], ps[m][:], ACT.Copy).then_inc(sem.v1, 1)
            for m in range(T):
                act.wait_ge(sem.glu_y, m + 1)
                if m:
                    act.wait_ge(sem.mixer_sq, m)
                nc.scalar.activation(JUNK1, YG[:, m, :], ACT.Square, accum_out=ass[:, 0, m:m + 1]).then_inc(sem.mixer_sq, 1)
            for u in range(NU1):
                act.wait_ge(sem.a_min, u + 1)
                if u >= 2:
                    act.wait_ge(sem.a_pT_ps, u - 1)
                nc.scalar.activation(PR1[:, u % 2, :], ps[u % 3][:], ACT.Exp, bias=mn[:, u % 4:u % 4 + 1], scale=-1.0,
                                     accum_out=rs[:, u:u + 1]).then_inc(sem.a_exp, 1)
            for m in range(T):
                act.wait_ge(sem.a_o, H1)
                act.wait_ge(sem.mixer_sq, T + m)
                nc.scalar.activation(JUNK1, O1[:, m, :], ACT.Square, accum_out=ass[:, 1, m:m + 1]).then_inc(sem.mixer_sq, 1)
            post_squares(act, 0, MIX, mixed(0))

        def one_pool(pool):
            norm_rstd(pool, 0)
            for m in range(T):
                pool.wait_ge(sem.za_sq, m + 1)
                pool_link(nc.gpsimd.tensor_scalar(zms[:, 0:1], zss[:, 0:1], 1.0 / Q_RANK, EPS, ALU.mult, ALU.add))
                pool_link(nc.gpsimd.tensor_scalar(zms[:, 1:2], zss[:, 1:2], 1.0 / KV_RANK, EPS, ALU.mult, ALU.add))
                nc.gpsimd.tensor_tensor(zrs[:, m, :], zms, neghalf[:, 0:2], ALU.pow).then_inc(sem.za_rstd, 1)
            for o in range(2):
                for m in range(T):
                    pool.wait_ge(sem.mixer_sq, T * o + m + 1)
                    pool_link(nc.gpsimd.tensor_scalar(ams[:, m:m + 1], ass[:, o, m:m + 1], 1.0 / WIDE, EPS, ALU.mult, ALU.add))
                    nc.gpsimd.tensor_tensor(ars[:, o, m:m + 1], ams[:, m:m + 1], neghalf[:, 0:1], ALU.pow).then_inc(sem.mixer_rstd, 1)
            post_factor(pool, 0, MIX)

        HEADS = [("sel", h) for h in range(NH)] + [("win", h) for h in range(NH)] + [("fox", h) for h in range(NH)]

        def q_of(kind, h, t):
            tok = slice(P * t, P * t + P)
            if kind == "fox":
                return fq[0:HD + 2, h, tok]
            o = HD * (h % 2)
            return qrT[o:o + HD, h // 2, tok]

        def k_of(kind, h, n):
            if kind == "fox":
                return fk[0:HD + 2, h, 0:n]
            o = HD * (h % 2)
            return {"sel": ksT, "win": kwT}[kind][o:o + HD, h // 4, 0:n]

        def v_of(kind, h, b):
            if kind == "fox":
                return fv[:, b, HD * h:HD * h + HD]
            o = {"sel": 0, "win": P}[kind] + HD * (h // 4)
            return vn[:, b, o:o + HD]

        def o_of(kind, h, t):
            c = HD * h + (512 if kind == "fox" else 0)
            return O[:, t, c:c + HD]

        def two_pe(pe, l):
            v = 1 + 2 * l
            w0 = B1 + 2 * l
            if w0:
                pe.wait_ge(sem.post_y, 8 * w0)
            for t in range(T):
                norm_transpose(pe, v - V0, t)
            pe.wait_ge(sem.hT, 8 * (v - V0) + 8)

            def bank_free(n):
                if n >= 4:
                    pe.wait_ge(sem.proj_sb, NPJ * l + n - 3)

            def wide_product(bank, j, low):
                w = split(pe, l, j)
                for k in range(KD):
                    last = product(bank[:], [v[:, P * k:P * k + P] for v in w],
                                   [v[:, k, :] for v in (HT_R, low[1])], k == 0, k == KD - 1)
                return last

            def natural(n, t, name, width):
                bank_free(n)
                for k in range(KD):
                    w = split(pe, l, (0 if name == "n1" else 12) + k // 2)
                    if name != "n1":
                        w = [v.rearrange("p (k c) -> p k c", c=512) for v in w]
                    x = [v[:, k, P * t:P * t + P] for v in (HT_R, HL_IN[1])]
                    last = product(ps[n % 4][:, 0:width], x, [v[:, k % 2, :] for v in w], k == 0, k == KD - 1)
                last.then_inc(sem.proj, 1)

            def transposed(n):
                bank_free(n)
                wide_product(ps[n % 4], n, HL_IN).then_inc(sem.proj, 1)

            def permute(m):
                n = 6 + m
                pe.wait_ge(sem.proj_sb, NPJ * l + n + 1)
                if m >= 2:
                    pe.wait_ge(sem.rot, NPM * l + m - 1)
                src = kraw[:, m, :] if m < 2 else qT[:, m - 2, :]
                nc.tensor.matmul(ps[4 + m % 2][:], swap2[:], src, start=True, stop=True).then_inc(sem.perm, 1)

            def hidden(i):
                pe.wait_ge(sem.cmp_E, 2 * l + i + 1)
                if l:
                    pe.wait_ge(sem.cs_o, T * l)
                wv = block_of(f"w1{'kv'[i]}_{l}", pe, CMP_HID)
                for j in range(2):
                    for k in range(LP):
                        last = nc.tensor.matmul(ps[6 + i][:, 64 * j:64 * j + 2 * NCMP], wv[:, k, P * j:P * j + P],
                                                E[i][:, k, :], start=(k == 0), stop=(k == LP - 1))
                last.then_inc(sem.hid_ps, 1)

            def compressed():
                pe.wait_ge(sem.hid, 4 * l + 2)
                for j in range(2):
                    last = nc.tensor.matmul(ps[6][:, 0:2 * NCMP], w2k[:, l, j, :], hidk[:, j, 0:2 * NCMP],
                                            start=(j == 0), stop=(j == 1))
                last.then_inc(sem.kc_ps, 1)
                pe.wait_ge(sem.hid_rep, l + 1)
                for g in range(KVG):
                    for j in range(2):
                        last = nc.tensor.matmul(ps[7][:, HD * g:HD * g + HD], hidr[:, j, g, :, :].rearrange("p r n -> p (r n)"),
                                                w2v[:, l, j, :], start=(j == 0), stop=(j == 1))
                last.then_inc(sem.vc_ps, 1)

            def forget_transpose():
                pe.wait_ge(sem.proj_sb, NPJ * l + 4)
                if l:
                    pe.wait_ge(sem.vc, l)
                for t in range(T):
                    last = nc.tensor.transpose(ps[7][0:8, P * t:P * t + P], gf[:, t, NGATE:NGATE + 8], ident[:])
                last.then_inc(sem.ff_T, 1)

            def cmp_scores(t):
                if t == 0:
                    pe.wait_ge(sem.kc, l + 1)
                    pe.wait_ge(sem.rot, NPM * (l + 1))
                else:
                    pe.wait_ge(sem.cs_p, T * l + t)
                for j in range(4):
                    last = nc.tensor.matmul(ps[4][:, HD * j:HD * j + HD], qT[:, j, P * t:P * t + P],
                                            kcBD[:, j // 2, :, :].rearrange("p o n -> p (o n)"), start=True, stop=True)
                last.then_inc(sem.cs_ps, 1)

            def cmp_transpose(t):
                pe.wait_ge(sem.cs_p, T * l + t + 1)
                if t:
                    pe.wait_ge(sem.cs_pT, T * l + t)
                for g in range(KVG):
                    last = nc.tensor.transpose(ps[5][:, P * g:P * g + P], CP[:, g, :], ident[:])
                last.then_inc(sem.cs_pT_ps, 1)

            def cmp_values(t):
                pe.wait_ge(sem.cs_pT, T * l + t + 1)
                if t == 0:
                    pe.wait_ge(sem.vc, l + 1)
                    pe.wait_ge(sem.kc, l + 1)
                else:
                    pe.wait_ge(sem.cs_o, T * l + t)
                for g in range(KVG):
                    last = nc.tensor.matmul(ps[6][:, 256 * g:256 * g + 256], CX[:, g, :],
                                            vBD[:, g, :, :].rearrange("p h d -> p (h d)"), start=True, stop=True)
                last.then_inc(sem.cs_o_ps, 1)

            for n in range(4):
                natural(n, n, "n1", 288)
            transposed(4)
            transposed(5)
            forget_transpose()
            transposed(6)
            transposed(7)
            permute(0)
            hidden(0)
            pe.wait_ge(sem.ff_z, l + 1)
            hidden(1)
            permute(1)
            transposed(8)
            transposed(9)
            permute(2)
            compressed()
            transposed(10)
            permute(3)
            transposed(11)
            permute(4)
            for n in range(12, 16):
                natural(n, n - 12, "n2", 512)
                if n == 12:
                    permute(5)
            for n in range(16, 24):
                transposed(n)
                t = n - 16
                if t < T:
                    cmp_scores(t)
                if 1 <= t <= T:
                    cmp_transpose(t - 1)
                if 2 <= t <= T + 1:
                    cmp_values(t - 2)

            pe.wait_ge(sem.proj_sb, NPJ * (l + 1))
            pe.wait_ge(sem.aug_ones, l + 1)
            pe.wait_ge(sem.ff_rows, 32 * (l + 1))
            pe.wait_ge(sem.cs_o, T * (l + 1))
            for u in range(NU + 4):
                if u < NU:
                    kind, h = HEADS[u // 4]
                    t = u % 4
                    if u >= 3:
                        pe.wait_ge(sem.s_masked, NU * l + u - 2)
                    nc.tensor.matmul(ps[u % 3][:, 0:P * (t + 1)], q_of(kind, h, t), k_of(kind, h, P * (t + 1)),
                                     start=True, stop=True).then_inc(sem.s_ps, 1)
                w = u - 2
                if 0 <= w < NU:
                    pe.wait_ge(sem.s_exp, NU * l + w + 1)
                    if w >= 2:
                        pt_wait(pe, l, w - 2)
                    for b in range(w % 4 + 1):
                        last = nc.tensor.transpose(ps[3 + w % 2][:, P * b:P * b + P], PR[:, w % 2, P * b:P * b + P], ident[:])
                    last.then_inc(sem.pT_ps, 1)
                w = u - 3
                if 0 <= w < NU:
                    kind, h = HEADS[w // 4]
                    t, gr = w % 4, w // 4
                    pt_wait(pe, l, w)
                    if t == 0 and gr >= 2:
                        pe.wait_ge(sem.o_sb, NU // 4 * l + gr - 1)
                    for b in range(t + 1):
                        last = nc.tensor.matmul(ps[5 + gr % 2][:, HD * t:HD * t + HD], PT[:, w % 2, P * b:P * b + P],
                                                v_of(kind, h, b), start=(b == 0), stop=(b == t))
                    last.then_inc(sem.o_ps, 1)

            pe.wait_ge(sem.o_sb, NU // 4 * (l + 1))
            for i in range(8):
                t, half = i // 2, i % 2
                for k in range(4):
                    c = 512 * half + P * k
                    last = nc.tensor.transpose(ps[i][:, P * k:P * k + P], O[:, t, c:c + P], ident[:])
                last.then_inc(sem.mixT_ps, 1)
            pe.wait_ge(sem.mixT_act, 4 * (l + 1))
            pe.wait_ge(sem.mixT_dve, 4 * (l + 1))
            out_projection(pe, B1 + l, [f"wo{k}_{l}" for k in range(KD)])

            pe.wait_ge(sem.post_y, 8 * (w0 + 1))
            for t in range(T):
                norm_transpose(pe, v + 1 - V0, t)
            pe.wait_ge(sem.hT, 8 * (v + 1 - V0) + 8)
            for g in range(NG):
                for i in range(FG):
                    f = FG * g + i
                    if i >= 4:
                        pe.wait_ge(sem.relu, NF * l + f - 3)
                    elif g:
                        pe.wait_ge(sem.mlp_sum, mlp_count(l, g - 1, 0))
                    wide_product(ps[up_bank(g) + f % 4], NPJ + 2 * FG * g + i, HL_MLP).then_inc(sem.up_ps, 1)
                for half in range(2):
                    if half:
                        pe.wait_ge(sem.relu, NF * l + FG * (g + 1))
                    elif g:
                        pe.wait_ge(sem.mlp_sum, mlp_count(l, g - 1, 1))
                    for i in range(FG):
                        pe.wait_ge(sem.relu_sq, NF * l + FG * g + i + 1)
                        w = split(pe, l, NPJ + 2 * FG * g + FG + FG // 2 * half + i // 2)
                        w = [v[:, 512 * (i % 2):512 * (i % 2) + 512] for v in w]
                        for t in range(T):
                            x = [v[:, i, P * t:P * t + P] for v in (uT_hi, uT_lo)]
                            last = product(ps[down_bank(g, half) + t][:], x, w, i == 0, i == FG - 1)
                        if i % 2:
                            last.then_inc(sem.down, 1)

        def up_bank(g):
            return 4 * ((g + 1) % 2)

        def down_bank(g, half):
            return 4 * ((g + half) % 2)

        def mlp_count(l, g, half):
            return 8 * NG * l + 8 * g + 4 * half + 4

        MLP_BANK = down_bank(NG - 1, 0)

        def pt_wait(eng, l, u):
            if on_act(u):
                eng.wait_ge(sem.pT_act, N_ACT * l + ACT_BEFORE[u] + 1)
            else:
                eng.wait_ge(sem.pT_dve, (NU - N_ACT) * l + u - ACT_BEFORE[u] + 1)

        def two_act(act, l, post_gain):
            v = 1 + 2 * l - V0
            w0 = B1 + 2 * l
            norm_squares(act, v, lambda t: x_tile(2 * l, t))
            for i in range(8):
                norm_hi(act, v, HL_IN, i)
                split_hi(act, l, i)
            post_gain(w0, a["g_post_mix_2"][l:l + 1, :])

            def copy(dst, src, scale=1.0):
                return nc.scalar.activation(dst, src, ACT.Copy, scale=scale)

            def evacuate(n):
                act.wait_ge(sem.proj, NPJ * l + n + 1)
                src = ps[n % 4]
                if n < 4:
                    copy(vn[:, n, :], src[:, 0:256])
                    last = copy(gf[:, n, :], src[:, 256:288])
                elif n < 6:
                    for g in range(KVG):
                        mine = src[HD * g:HD * g + HD, :]
                        copy(X2[n - 4][0:HD, g, :], mine)
                        last = copy(X2[n - 4][HD:P, g, 0:SEQ - 1], mine[:, 1:SEQ])
                elif n < 8:
                    last = copy(kraw[:, n - 6, :], src[:])
                elif n < 12:
                    last = copy(qT[:, n - 8, :], src[:], -SCALE2)
                elif n < 16:
                    last = copy(fv[:, n - 12, :], src[:])
                else:
                    dst, scale = (fq, -SCALE2) if n < 20 else (fk, 1.0)
                    for o in range(2):
                        last = copy(dst[0:HD, 2 * (n % 4) + o, :], src[HD * o:HD * o + HD, :], scale)
                last.then_inc(sem.proj_sb, 1)

            def gelu_hidden(i):
                act.wait_ge(sem.hid_ps, 2 * l + i + 1)
                for j in range(2):
                    bias = cols[:, R_B1 + 4 * i + 2 * l + j:R_B1 + 4 * i + 2 * l + j + 1]
                    src = ps[6 + i][:, 64 * j:64 * j + 2 * NCMP]
                    if i == 0:
                        dst = hidk[:, j, 0:2 * NCMP]
                    else:
                        dst = hidv[:, j, :, 0:NCMP]
                        src = src.rearrange("p (g n) -> p g n", g=KVG)
                    nc.scalar.activation(dst, src, ACT.Gelu_apprx_tanh, bias=bias).then_inc(sem.hid, 1)

            def cmp_exp(t):
                act.wait_ge(sem.cs_exp, 2 * (T * l + t) + 1)
                nc.scalar.activation(CP.rearrange("p g n -> p (g n)"), CS.rearrange("p h n -> p (h n)"), ACT.Exp)\
                    .then_inc(sem.cs_exp, 1)

            act.wait_ge(sem.hT, 8 * v + 8)
            for n in range(4):
                evacuate(n)
            act.wait_ge(sem.gate, 2 * l + 1)
            nc.scalar.activation(gx[:], gx[:], ACT.Exp, scale=-1.0).then_inc(sem.gate_e, 1)
            evacuate(4)
            evacuate(5)
            act.wait_ge(sem.ff_z, l + 1)
            nc.scalar.activation(ffm[:], ffz[:], ACT.Abs).then_inc(sem.ff_abs, 1)
            act.wait_ge(sem.ff_abs, l + 1)
            nc.scalar.activation(ffm[:], ffm[:], ACT.Exp, scale=-1.0).then_inc(sem.ff_exp, 1)
            act.wait_ge(sem.ff_exp, l + 1)
            nc.scalar.activation(ffm[:], ffm[:], ACT.Ln, bias=1.0).then_inc(sem.ff_ln, 1)
            evacuate(6)
            evacuate(7)
            gelu_hidden(0)
            gelu_hidden(1)
            for j in range(8, 16):
                split_hi(act, l, j)
            for n in range(8, 16):
                evacuate(n)
                if n >= 12:
                    split_hi(act, l, n + 4)
            act.wait_ge(sem.ff_cum, 2 * (l + 1))
            act.wait_ge(sem.aug_ones, l + 1)
            act.dma_start(fk[HD:HD + 1, :, :], ffc[:]).then_inc(sem.ff_rows, 16)
            act.dma_start(fq[HD + 1:HD + 2, :, :], ffz[:]).then_inc(sem.ff_rows, 16)
            for n in range(16, 24):
                evacuate(n)
                if n < 20:
                    split_hi(act, l, n + 4)
                if n - 16 < T:
                    cmp_exp(n - 16)

            for u in range(NU + 2):
                if u < NU:
                    act.wait_ge(sem.s_masked, NU * l + u + 1)
                    if u >= 2:
                        act.wait_ge(sem.pT_ps, NU * l + u - 1)
                    w = P * (u % 4 + 1)
                    nc.scalar.activation(PR[:, u % 2, 0:w], SM[:, u % 3, 0:w], ACT.Exp, bias=mn[:, u % 4:u % 4 + 1],
                                         scale=-1.0, accum_out=rs[:, u:u + 1]).then_inc(sem.s_exp, 1)
                z = u - 2
                if z >= 0 and on_act(z):
                    act.wait_ge(sem.pT_ps, NU * l + z + 1)
                    if z >= 2:
                        act.wait_ge(sem.o_ps, NU * l + z - 1)
                    w = P * (z % 4 + 1)
                    copy(PT[:, z % 2, 0:w], ps[3 + z % 2][:, 0:w]).then_inc(sem.pT_act, 1)

            for i in range(0, 8, 2):
                mixT_copy(act, l, i, lambda d, s: copy(d, s), sem.mixT_act)
            post_squares(act, w0, MIX, mixed(B1 + l))
            norm_squares(act, v + 1, lambda t: x_tile(2 * l + 1, t))
            for i in range(8):
                norm_hi(act, v + 1, HL_MLP, i)
                if i < AHEAD:
                    split_hi(act, l, NPJ + i)
            post_gain(w0 + 1, a["g_post_mlp_2"][l:l + 1, :])
            for j in range(2 * NF):
                if j + AHEAD < 2 * NF:
                    split_hi(act, l, NPJ + j + AHEAD)
                g, i = divmod(j, 2 * FG)
                if i < FG:
                    f = FG * g + i
                    act.wait_ge(sem.up_ps, NF * l + f + 1)
                    if f >= 2:
                        act.wait_ge(sem.relu_sq, NF * l + f - 1)
                    nc.scalar.activation(relu[:, f % 2, :], ps[up_bank(g) + f % 4][:], ACT.Relu).then_inc(sem.relu, 1)
            post_squares(act, w0 + 1, MLP, lambda e: (sem.mlp_sum, mlp_count(l, NG - 1, 0) - 3 + e), MLP_BANK)

        AHEAD = 3

        def mixT_copy(eng, l, i, copy, done):
            t, half = i // 2, i % 2
            eng.wait_ge(sem.mixT_ps, 8 * l + i + 1)
            copy(HT[:, 4 * half:4 * half + 4, P * t:P * t + P], ps[i][:].rearrange("p (k n) -> p k n", k=4))\
                .then_inc(done, 1)

        def x_tile(i, t):
            n = B1 + i
            return (sem.x_new, T * (n - 1) + t + 1) if n else (x_in[t], 16)

        def two_dve(dve, l):
            v = 1 + 2 * l - V0
            w0 = B1 + 2 * l
            norm_dve(dve, v, low=HL_IN)
            for j in range(8):
                split_lo(dve, l, j)

            def rotate(m):
                dve.wait_ge(sem.perm, NPM * l + m + 1)
                dve_link(nc.vector.tensor_tensor(rsin[:, m % 2, :], ps[4 + m % 2][:], sin2[:], ALU.mult))
                dve.wait_ge(sem.rot_cos, NPM * l + m + 1)
                if m < 2:
                    dst = (ksT, kwT)[m]
                    for g in range(KVG):
                        for o in range(2):
                            a_, b_ = slice(HD * g, HD * g + HD), slice(HD * o, HD * o + HD)
                            last = nc.vector.tensor_tensor(dst[b_, g, :], rcos[a_, m % 2, :], rsin[a_, m % 2, :], ALU.add)
                else:
                    last = nc.vector.tensor_tensor(qrT[:, m - 2, :], rcos[:, m % 2, :], rsin[:, m % 2, :], ALU.add)
                last.then_inc(sem.rot, 1)

            def compressed():
                dve.wait_ge(sem.hid, 4 * l + 4)
                for j in range(2):
                    last = nc.vector.tensor_copy(hidr[:, j, :, :, :], hidv[:, j, :, None, :].to_broadcast([P, KVG, 4, 32]))
                last.then_inc(sem.hid_rep, 1)
                dve.wait_ge(sem.kc_ps, l + 1)
                for o in range(2):
                    r = slice(HD * o, HD * o + HD)
                    last = nc.vector.tensor_scalar(kcBD[r, :, o, 0:NCMP], ps[6][r, 0:2 * NCMP].rearrange("p (g n) -> p g n", g=KVG),
                                                   cols[r, R_B2K + l:R_B2K + l + 1], None, ALU.add)
                last.then_inc(sem.kc, 1)
                dve.wait_ge(sem.vc_ps, l + 1)
                for i in range(4):
                    r = slice(32 * i, 32 * i + 32)
                    last = nc.vector.tensor_tensor(vBD[r, :, i, :], ps[7][r, 0:P].rearrange("p (g d) -> p g d", g=KVG),
                                                   b2v[r, l, None, :].to_broadcast([32, KVG, HD]), ALU.add)
                last.then_inc(sem.vc, 1)

            def cmp_softmax(t):
                dve.wait_ge(sem.cs_ps, T * l + t + 1)
                if t:
                    dve.wait_ge(sem.cs_pT_ps, T * l + t)
                dve_link(nc.vector.tensor_tensor(CS, ps[4][:, 0:256].rearrange("p (h n) -> p h n", n=32),
                                                 cmask[:, t, None, :].to_broadcast([P, NH, 32]), ALU.add))
                dve_link(nc.vector.tensor_reduce(cmn[:], CS, AX_X, ALU.min))
                nc.vector.tensor_tensor(CS, cmn[:, :, None].to_broadcast([P, NH, 32]), CS, ALU.subtract)\
                    .then_inc(sem.cs_exp, 1)
                dve.wait_ge(sem.cs_exp, 2 * (T * l + t) + 2)
                pv = CP.rearrange("p g (h n) -> p (g h) n", n=32)
                dve_link(nc.vector.tensor_reduce(csum[:], pv, AX_X, ALU.add))
                dve_link(nc.vector.reciprocal(csum[:], csum[:]))
                dve_link(nc.vector.scalar_tensor_tensor(csum[:], gate[:, t, :].rearrange("p (h b) -> p b h", b=3)[:, 0, :],
                                                        valid[:, t:t + 1], csum[:], ALU.mult, ALU.mult))
                nc.vector.tensor_tensor(pv, pv, csum[:, :, None].to_broadcast([P, NH, 32]), ALU.mult).then_inc(sem.cs_p, 1)

            def cmp_pT(t):
                dve.wait_ge(sem.cs_pT_ps, T * l + t + 1)
                if t:
                    dve.wait_ge(sem.cs_o_ps, T * l + t)
                nc.vector.tensor_copy(CX, ps[5][:, 0:256].rearrange("p (g n) -> p g n", g=KVG)).then_inc(sem.cs_pT, 1)

            def cmp_out(t):
                dve.wait_ge(sem.cs_o_ps, T * l + t + 1)
                nc.vector.tensor_copy(CO[:, t, :], ps[6][:]).then_inc(sem.cs_o, 1)

            dve.wait_ge(sem.proj_sb, NPJ * l + 4)
            nc.vector.tensor_tensor(gx[:], gf[:, :, 0:NGATE], gbias[:, l, None, :].to_broadcast([P, T, NGATE]), ALU.add)\
                .then_inc(sem.gate, 1)
            dve.wait_ge(sem.ff_T, l + 1)
            if l:
                dve.wait_ge(sem.ff_rows, 32 * l)
            nc.vector.tensor_scalar(ffz[:], ps[7][0:8, :], cols[0:8, R_BF + l:R_BF + l + 1], None, ALU.add)\
                .then_inc(sem.ff_z, 1)
            dve.wait_ge(sem.gate_e, l + 1)
            dve_link(nc.vector.tensor_scalar(gx[:], gx[:], 1.0, None, ALU.add))
            nc.vector.reciprocal(gate[:], gx[:]).then_inc(sem.gate, 1)
            dve.wait_ge(sem.ff_ln, l + 1)
            dve_link(nc.vector.scalar_tensor_tensor(ffz[:], ffz[:], 0.0, ffm[:], ALU.min, ALU.subtract))
            nc.vector.tensor_tensor_scan(ffc[:], ones[0:8, 0:1].to_broadcast([8, SEQ]), ffz[:], 0.0, ALU.mult, ALU.add).then_inc(sem.ff_cum, 1)
            dve.wait_ge(sem.ff_cum, 2 * l + 1)
            nc.vector.tensor_scalar(ffz[:], ffc[:], -1.0, None, ALU.mult).then_inc(sem.ff_cum, 1)
            dve.wait_ge(sem.gate, 2 * l + 2)
            rotate(0)
            rotate(1)
            for j in range(8, 16):
                split_lo(dve, l, j)
            compressed()
            for m in range(2, 6):
                rotate(m)
            for j in range(16, 20):
                split_lo(dve, l, j)
            for t in range(T + 2):
                if 1 <= t <= 4:
                    split_lo(dve, l, 19 + t)
                if t < T:
                    cmp_softmax(t)
                if 1 <= t <= T:
                    cmp_pT(t - 1)
                if t >= 2:
                    cmp_out(t - 2)

            for u in range(NU + 4):
                if u < NU:
                    dve.wait_ge(sem.s_ps, NU * l + u + 1)
                    if u >= 3:
                        dve.wait_ge(sem.s_exp, NU * l + u - 2)
                    if u >= 4:
                        dve.wait_ge(sem.s_exp, NU * l + u - 3)
                    t = u % 4
                    w = P * (t + 1)
                    nc.vector.tensor_tensor_reduce(SM[:, u % 3, 0:w], ps[u % 3][:, 0:w], tri[:, SEQ - w:SEQ], 1.0,
                                                   3.0e38, ALU.add, ALU.min, mn[:, t:t + 1]).then_inc(sem.s_masked, 1)
                z = u - 2
                if 0 <= z < NU and not on_act(z):
                    dve.wait_ge(sem.pT_ps, NU * l + z + 1)
                    if z >= 2:
                        dve.wait_ge(sem.o_ps, NU * l + z - 1)
                    w = P * (z % 4 + 1)
                    nc.vector.tensor_copy(PT[:, z % 2, 0:w], ps[3 + z % 2][:, 0:w]).then_inc(sem.pT_dve, 1)
                z = u - 4
                if z >= 0 and z % 4 == 3:
                    gr = z // 4
                    kind, h = HEADS[gr]
                    dve.wait_ge(sem.s_exp, NU * l + z + 1)
                    r = rg[:, gr % 3, :]
                    dve_link(nc.vector.reciprocal(r, rs[:, 4 * gr:4 * gr + 4]))
                    if kind != "fox":
                        b = 1 if kind == "sel" else 2
                        dve_link(nc.vector.tensor_tensor(r, r, gate[:, :, 3 * h + b], ALU.mult))
                    dve.wait_ge(sem.o_ps, NU * l + z + 1)
                    for t in range(T):
                        src = ps[5 + gr % 2][:, HD * t:HD * t + HD]
                        dst = o_of(kind, h, t)
                        if kind == "fox":
                            last = nc.vector.tensor_scalar(dst, src, r[:, t:t + 1], None, ALU.mult)
                        else:
                            base = CO[:, t, HD * h:HD * h + HD] if kind == "sel" else dst
                            last = nc.vector.scalar_tensor_tensor(dst, src, r[:, t:t + 1], base, ALU.mult, ALU.add)
                    last.then_inc(sem.o_sb, 1)

            for i in range(1, 8, 2):
                mixT_copy(dve, l, i, lambda d, s: nc.vector.tensor_copy(d, s), sem.mixT_dve)
            post_add(dve, w0, MIX)
            norm_dve(dve, v + 1, low=HL_MLP)
            for j in range(AHEAD):
                split_lo(dve, l, NPJ + j)
            for j in range(2 * NF):
                if j + AHEAD < 2 * NF:
                    split_lo(dve, l, NPJ + j + AHEAD)
                g, i = divmod(j, 2 * FG)
                if i in (2 * FG - FG // 2 - 1, 2 * FG - 1):
                    add_outputs(dve, l, g, (i - FG) // (FG // 2))
            post_add(dve, w0 + 1, MLP, MLP_BANK)

        def add_outputs(dve, l, g, half):
            dve.wait_ge(sem.down, down_count(l, g, half, FG // 2 - 1))
            if g:
                dve.wait_ge(sem.mlp_sum, mlp_count(l, g - 1, half))
            for t in range(T):
                bank, y = ps[down_bank(g, half) + t][:], Y[:, t, 512 * half:512 * half + 512]
                if g == 0:
                    last = nc.vector.tensor_copy(y, bank)
                else:
                    last = nc.vector.tensor_tensor(bank if g == NG - 1 else y, bank, y, ALU.add)
                last.then_inc(sem.mlp_sum, 1)

        def two_pool(pool, l):
            v = 1 + 2 * l - V0
            w0 = B1 + 2 * l
            norm_rstd(pool, v)
            norm_lo(pool, v, HL_IN)
            for i in range(2):
                pool.wait_ge(sem.proj_sb, NPJ * l + 5 + i)
                r0 = R_POS + 32 * i + LP * l
                for g in range(KVG):
                    src = window(X2[i], g)
                    last = nc.gpsimd.tensor_tensor(E[i][:, :, NCMP * g:NCMP * g + NCMP], src,
                                                   cols[:, r0:r0 + LP, None].to_broadcast([P, LP, NCMP]), ALU.add)
                last.then_inc(sem.cmp_E, 1)
            for m in range(NPM):
                pool.wait_ge(sem.proj_sb, NPJ * l + 7 + m)
                if m >= 2:
                    pool.wait_ge(sem.rot, NPM * l + m - 1)
                src = kraw[:, m, :] if m < 2 else qT[:, m - 2, :]
                nc.gpsimd.tensor_tensor(rcos[:, m % 2, :], src, cos2[:], ALU.mult).then_inc(sem.rot_cos, 1)
            pool.wait_ge(sem.proj, NPJ * l + 16)
            pool.wait_ge(sem.rot_cos, NPM * (l + 1))
            nc.gpsimd.memset(fq[HD:HD + 2, :, :], 1.0)
            nc.gpsimd.memset(fk[HD:HD + 2, :, :], 1.0).then_inc(sem.aug_ones, 1)
            pool.wait_ge(sem.aug_ones, l + 1)
            post_factor(pool, w0, MIX)
            norm_rstd(pool, v + 1)
            norm_lo(pool, v + 1, HL_MLP)
            for f in range(NF):
                pool.wait_ge(sem.relu, NF * l + f + 1)
                r, i = relu[:, f % 2, :], f % FG
                pool_link(nc.gpsimd.tensor_tensor(r, r, r, ALU.mult))
                if f >= FG:
                    pool.wait_ge(sem.down, down_count(l, f // FG - 1, 1, i // 2))
                pool_link(nc.gpsimd.tensor_copy(uT_hi[:, i, :], r))
                nc.gpsimd.tensor_tensor(uT_lo[:, i, :], r, uT_hi[:, i, :].bitcast(F32), ALU.subtract).then_inc(sem.relu_sq, 1)
            post_factor(pool, w0 + 1, MLP)

        def window(x2, g):
            v = x2[:, g, 0:SEQ]
            ap = [list(d) for d in v.ap]
            return bass.AP(v.tensor, v.offset, [ap[0], [2, LP], [CMP_STRIDE, NCMP]])

        V0 = 0 if first else 1
        on_act = lambda u: u % 5 in (1, 3)
        ACT_BEFORE = [sum(on_act(x) for x in range(u)) for u in range(NU)]
        N_ACT = sum(on_act(u) for u in range(NU))

        vectors = []
        if first:
            vectors += [(R_PRE1, a["pre_norm_g"][0]), (R_QN, a["q_norm_g"][0]), (R_KVN, a["kv_norm_g"][0]),
                        (R_AO, a["attn_out_g"][0]), (R_SO, a["ssm_out_g"][0])]
        for l in range(DEPTH):
            vectors += [(R_NORM + 16 * l, a["g_pre_mix_2"][l]), (R_NORM + 16 * l + 8, a["g_pre_mlp_2"][l]),
                        (R_B1 + 2 * l, a["cmp_b1_k_2"][l]), (R_B1 + 4 + 2 * l, a["cmp_b1_v_2"][l]),
                        (R_POS + LP * l, a["cmp_pos_k_2"][l].rearrange("(k o) d -> (k o d)", o=2)),
                        (R_POS + 32 + LP * l, a["cmp_pos_v_2"][l].rearrange("(k o) d -> (k o d)", o=2))]
        small = [(swap2[:], a["c_swap2"]), (tri[:], a["c_tri"]), (cos2[:], a["c_cos2"]), (sin2[:], a["c_sin2"]),
                 (cmask[:], a["c_cmask"].rearrange("p (t n) -> p t n", t=T)), (valid[:], a["c_valid"])]
        for l in range(DEPTH):
            small += [(gbias[:, l, :], a["b_nsa_gate_2"][l:l + 1, :].to_broadcast([P, NGATE])),
                      (b2v[:, l, :], a["cmp_b2_v_2"][l:l + 1, :].to_broadcast([P, HD])),
                      (w2k[:, l, :, 0:HD], a["cmp_w2_k_2"][l].rearrange("(j p) d -> p j d", p=P)),
                      (w2k[:, l, :, HD:P], a["cmp_w2_k_2"][l].rearrange("(j p) d -> p j d", p=P)),
                      (w2v[:, l, :, :], a["cmp_w2_v_2"][l].rearrange("(j p) d -> p j d", p=P))]
        if first:
            small += one_small()
        N_ROWS, N_SMALL = 16 * (len(vectors) + 3), 16 * len(small)

        block = ctx.enter_context(nc.Block())

        @block.sync
        def _(sp):
            for u in units:
                for s, n in u.free:
                    sp.wait_ge(s, n)
                for where, src in u.pieces:
                    dst = slots(u)
                    if where is not None:
                        width = 512 if u.slots == 4 else P
                    if where is not None and where[0] == "q":
                        _, c, h, n = where
                        dst = dst[:, c:c + h * n].rearrange("p (h n) -> p h n", h=h)
                    elif where is not None:
                        dst = dst.rearrange("p (k c) -> p k c", c=width)[:, 0:src.shape[1], where[0]:where[0] + where[1]]
                    elif len(src.shape) == 3:
                        dst = dst.rearrange("p (k c) -> p k c", c=src.shape[2])[:, 0:src.shape[1], :]
                    else:
                        dst = dst[:, 0:src.shape[1]]
                    sp.dma_start(dst, src).then_inc(wring[u.slot], 16)
                if u.name == "uq":
                    for q in range(1, NQ):
                        one_bc_dma(sp, q)
            sp.wait_ge(sem.out_done, 16 * T)

        @block.gpsimd
        def _(pool):
            nc.gpsimd.memset(neghalf[:], -0.5).then_inc(sem.const_set, 1)
            nc.gpsimd.memset(rows[:], 0.0).then_inc(sem.const_set, 1)
            nc.gpsimd.memset(ones[:], 1.0).then_inc(sem.const_set, 1)
            nc.gpsimd.memset(kcBD[:], 0.0).then_inc(sem.const_set, 1)
            nc.gpsimd.memset(vBD[:], 0.0).then_inc(sem.const_set, 1)
            nc.gpsimd.memset(hidv[:], 0.0).then_inc(sem.const_set, 1)
            pool.wait_ge(sem.const_set, 6)
            if first:
                one_pool(pool)
            if second:
                pool.wait_ge(sem.cols_ready, 1)
                for l in range(DEPTH):
                    two_pool(pool, l)

        @block.scalar
        def _(act):
            act.dma_start(ident[:], a["c_ident"]).then_inc(sem.consts_in, 16)
            for t in range(T):
                act.dma_start(X[:, t, :], a["x"][P * t:P * t + P, :]).then_inc(x_in[t], 16)
            act.wait_ge(sem.const_set, 6)
            for r, src in vectors:
                k = src.shape[0] // P
                act.dma_start(rows[r:r + k, :], src.rearrange("(k p) -> k p", p=P)).then_inc(sem.rows_in, 16)
            for o in range(2):
                act.dma_start(rows[R_B2K:R_B2K + DEPTH, HD * o:HD * o + HD], a["cmp_b2_k_2"][0:DEPTH, :]).then_inc(sem.rows_in, 16)
            act.dma_start(rows[R_BF:R_BF + DEPTH, 0:8], a["b_forget_2"][0:DEPTH, :]).then_inc(sem.rows_in, 16)
            for dst, src in small:
                act.dma_start(dst, src).then_inc(sem.small_in, 16)
            act.wait_ge(sem.cols_ready, 1)
            act.wait_ge(sem.small_in, N_SMALL)
            act.wait_ge(sem.const_set, 6)

            def post_gain(w, src):
                if w:
                    act.wait_ge(sem.post_y, 8 * w)
                act.dma_start(postg[:], src.to_broadcast([P, D])).then_inc(sem.postgain_in, 16)

            if first:
                one_act(act, post_gain)
            if second:
                for l in range(DEPTH):
                    two_act(act, l, post_gain)
            n = (B1 + 2 * DEPTH if second else 1)
            for t in range(T):
                act.wait_ge(sem.x_new, T * (n - 1) + t + 1)
                act.dma_start(out[P * t:P * t + P, :], X[:, t, :]).then_inc(sem.out_done, 16)

        @block.tensor
        def _(pe):
            pe.wait_ge(sem.consts_in, 16)
            pe.wait_ge(sem.rows_in, N_ROWS)
            nc.tensor.transpose(ps[7][:, 0:ROWS], rows[:], ident[:]).then_inc(sem.cols_ps, 1)
            pe.wait_ge(sem.small_in, N_SMALL)
            pe.wait_ge(sem.const_set, 6)
            if first:
                one_pe(pe)
            if second:
                for l in range(DEPTH):
                    two_pe(pe, l)

        @block.vector
        def _(dve):
            dve.wait_ge(sem.cols_ps, 1)
            nc.vector.tensor_copy(cols[:], ps[7][:, 0:ROWS]).then_inc(sem.cols_ready, 1)
            dve.wait_ge(sem.cols_ready, 1)
            dve.wait_ge(sem.small_in, N_SMALL)
            dve.wait_ge(sem.const_set, 6)
            if first:
                one_dve(dve)
            if second:
                for l in range(DEPTH):
                    two_dve(dve, l)


_INS = ["x", "positions", "pre_norm_g", "w_in", "q_norm_g", "w_uq", "kv_norm_g", "w_ukv", "attn_out_g",
        "s5_lam_re", "s5_lam_im", "s5_log_dt", "s5_b_re", "s5_b_im", "s5_c_re", "s5_c_im", "s5_d",
        "w_glu", "b_glu", "ssm_out_g", "w_out", "post_norm_g",
        "w_in_2", "b_nsa_gate_2", "b_forget_2", "cmp_pos_k_2", "cmp_w1_k_2", "cmp_b1_k_2", "cmp_w2_k_2", "cmp_b2_k_2",
        "cmp_pos_v_2", "cmp_w1_v_2", "cmp_b1_v_2", "cmp_w2_v_2", "cmp_b2_v_2", "w_out_2", "w_up_2", "w_down_2",
        "g_pre_mix_2", "g_post_mix_2", "g_pre_mlp_2", "g_post_mlp_2"]


def kernel(**inputs):
    import numpy as _np
    import concourse.bacc as _bacc
    from concourse import mybir as _mybir
    from concourse.bass_utils import run_bass_kernel_spmd as _run

    nc = _bacc.Bacc("TRN2", target_bir_lowering=False, num_devices=1)
    arrays, aps = {}, {}
    given = {name: _np.ascontiguousarray(inputs[name]) for name in _INS}
    given["x"] = given["x"].reshape(SEQ, D)
    given.update(constants())
    for name, value in given.items():
        arrays[f"in_{name}"] = value
        aps[name] = nc.dram_tensor(f"in_{name}", value.shape, _mybir.dt.from_np(value.dtype), kind="ExternalInput").ap()
    out = nc.dram_tensor("out", (SEQ, D), F32, kind="ExternalOutput").ap()
    build(nc, aps, out)
    r = _run(nc, [arrays], core_ids=[0])
    return r.results[0]["out"].reshape(1, SEQ, D)
```

```python
from contextlib import ExitStack
from collections import namedtuple

import numpy as np
import concourse.bass as bass
from concourse import mybir

F32 = mybir.dt.float32
F32R = mybir.dt.float32r
I32 = mybir.dt.int32
ALU = mybir.AluOpType
ACT = mybir.ActivationFunctionType
AX_X = mybir.AxisListType.X

P = 128
SEQ = 512
D = 1024
T = SEQ // P
KD = D // P
EPS = 1e-6

Q_RANK, KV_RANK, ROPE1 = 256, 128, 64
H1, NOPE, VD = 4, 128, 128
WIDE = 512
G, CH, ST = 32, 16, 64
L = 8
NC = SEQ // L
NQ, GQ = 4, 8
SCALE1 = float(NOPE + ROPE1) ** -0.5

DEPTH = 2
HD = 64
NH, KVG = 8, 2
CMP_LEN, CMP_STRIDE, CMP_HID = 32, 16, 256
NCMP = (SEQ - CMP_LEN) // CMP_STRIDE + 1
LP = CMP_LEN // 2
DFF = 4 * D
NF = DFF // P
SCALE2 = float(HD) ** -0.5
C_Q, C_KC, C_VC, C_KS, C_VS, C_KW, C_VW, C_GATE, C_FQ, C_FK, C_FV, C_FF = [
    int(v) for v in np.cumsum([0, 512, 128, 128, 128, 128, 128, 128, 24, 512, 512, 512])]
NGATE = 24
IN2 = C_FF + 8
BIG_NEG = 1e30

NS = 8
NPJ, NPM = 24, 6
FG, NG = 8, NF // 8
J_OUT, J_MLP = NPJ, NPJ + KD
NSPLIT = J_MLP + 2 * NF
NU = 96
ROWS = 128


def rope_table_2():
    half = HD // 4 // 2
    inv = np.float32(500000.0) ** (-np.arange(half, dtype=np.float32) * np.float32(2.0) / np.float32(HD // 4))
    ang = np.arange(SEQ, dtype=np.float32)[None, :] * inv.astype(np.float32)[:, None]
    c = np.ones((HD, SEQ), np.float32)
    s = np.zeros((HD, SEQ), np.float32)
    c[:half], c[half:2 * half] = np.cos(ang), np.cos(ang)
    s[:half], s[half:2 * half] = -np.sin(ang), np.sin(ang)
    return np.concatenate([c, c]), np.concatenate([s, s])


def swap_matrix(block, half, sign=1.0):
    m = np.zeros((P, P), np.float32)
    for b in range(0, P, block):
        for r in range(half):
            m[b + half + r, b + r] = 1.0
            m[b + r, b + half + r] = sign
    return m


def constants():
    q = np.arange(P)
    tri = np.zeros((P, SEQ), np.float32)
    tri[:, SEQ - P:] = np.where(q[None, :] <= q[:, None], 0.0, BIG_NEG)
    tok = np.arange(SEQ).reshape(T, P).T
    end = np.full(32, 10 ** 6)
    end[:NCMP] = np.arange(NCMP) * CMP_STRIDE + CMP_LEN - 1
    cmask = np.where(end[None, None, :] <= tok[:, :, None], 0.0, BIG_NEG).astype(np.float32)
    valid = (tok >= CMP_LEN - 1).astype(np.float32)
    c2, s2 = rope_table_2()
    inv1 = np.float32(10000.0) ** (-np.arange(0, ROPE1, 2, dtype=np.float32) / np.float32(ROPE1))
    col = np.zeros((P, 8), np.float32)
    col[:, 0] = np.tile(inv1, 4)
    col[:, 1] = np.tile(np.repeat([-1.0, 1.0], 32), 2)
    col[:, 2] = np.repeat([-1.0, 1.0], ST)
    return {
        "c_ident": np.eye(P, dtype=np.float32), "c_tri": tri, "c_cmask": cmask.reshape(P, T * 32),
        "c_valid": valid, "c_cos2": c2, "c_sin2": s2, "c_col": col,
        "c_swap2": swap_matrix(HD, HD // 8), "c_swap1": swap_matrix(ROPE1, ROPE1 // 2),
        "c_turn": swap_matrix(P, ST, -1.0),
    }


class Unit:

    def __init__(self, name, slots, pieces, used):
        self.name, self.slots = name, slots
        self.pieces = pieces
        self.used = used
        self.slot = self.landed = 0
        self.free = []

ONE_SEMS = (
    "par_in par_ps par dt_e par_exp par_trig amp "
    "u_ps u_sb uT_ps uT gs_ps gs za_ps za_sq za_rstd zn znT_ps znT ga_ps ga "
    "pos_in angle trig rope_ps rope_done "
    "bc_in cT_ps cT b_bar m1 m1T_ps w1T m3 tap_ps taps toep st_ps st_sb turn_ps turned state y_ps y_sb yT_ps yp "
    "ge geT_ps geT glu_ps glu_x glu_s glu_y mixer_sq mixer_rstd ssm_o "
    "qn_ps qn rq_ps rq kn_ps kn v1_ps v1 "
    "a_s_ps a_min a_exp a_pT_ps a_pT a_o_ps a_o at_o "
    "m1ix_ps m1ix").split()

TWO_PI = 2 * np.pi
PI2_A = 6.28125
PI2_B = float(np.float32(int((TWO_PI - PI2_A) * 2 ** 22) / 2 ** 22))
PI2_C = float(np.float32(TWO_PI - PI2_A - PI2_B))
ROUND = 12582912.0
PI_SAFE = 3.1415925
DG = 2 * G
DQ = 2 * GQ
NK = L + 1


def one_units(a, unit, colblock, quad, t_blocks, sem):
    w = a["w_in"][0]
    c_q, c_kr, c_ga, c_u, c_gs = 0, Q_RANK + KV_RANK, 448, 960, 1472
    quad("u", [((0, 512), t_blocks(w, (c_u, c_u + 512)))], sem.u_ps, T)
    quad("gs", [((0, 512), t_blocks(w, (c_gs, c_gs + 512)))], sem.gs_ps, T)
    quad("za", [((0, 448), t_blocks(w, (c_q, 448)))], sem.za_ps, T)
    quad("ga", [((0, 512), t_blocks(w, (c_ga, c_ga + 512)))], sem.ga_ps, T)
    w = a["w_uq"][0].rearrange("(k p) (h c) -> k p h c", p=P, h=H1)
    pieces = []
    for k in range(2):
        pieces.append((("q", k * 768, H1, NOPE), w[k, :, :, 0:NOPE]))
        pieces.append((("q", k * 768 + 512, H1, ROPE1), w[k, :, :, NOPE:NOPE + ROPE1]))
    unit("uq", 4, pieces, sem.rq_ps, 2)
    unit("ukv", 1, [(None, a["w_ukv"][0])], sem.v1_ps, T)
    quad("glu", [((0, 512), t_blocks(a["w_glu"][0], (0, 512)))], sem.glu_ps, T)
    for k in range(KD):
        unit(f"wo{k}", 1, [(None, a["w_out"][0][P * k:P * k + P, :])], sem.out_ps, 8)


def build(nc, a, out, first=True, second=True):
    names = (
        "x_in0 x_in1 x_in2 x_in3 rows_in consts_in small_in postgain_in wring0 wring1 wring2 wring3 wring4 wring5 wring6 wring7 "
        "cols_ps cols_ready const_set "
        "sq rstd xn xT x_gained x_hi hT w_hi w_lo x_new out_ps post_sq post_y post_rstd "
        "proj proj_sb perm rot rot_cos gate_e gate "
        "ff_T ff_z ff_part ff_cum ff_rows aug_ones "
        "cmp_E hid_ps hid hid_rep kc_ps kc vc_ps vc "
        "cs_ps cs_exp cs_p cs_pT_ps cs_pT cs_o_ps cs_o "
        "s_ps s_masked s_exp pT_ps pT_act pT_dve o_ps o_sb "
        "mixT_ps mixT mixT_hi mixT_lo up_ps relu relu_sq down mlp_sum "
        "act_chain dve_chain pool_chain out_done").split()
    if first:
        names += ONE_SEMS
    with ExitStack() as ctx:
        sem = namedtuple("Semaphores", names)(*[ctx.enter_context(nc.semaphore("s_" + n)) for n in names])
        wring = [sem.wring0, sem.wring1, sem.wring2, sem.wring3, sem.wring4, sem.wring5, sem.wring6, sem.wring7]

        x_in = [sem.x_in0, sem.x_in1, sem.x_in2, sem.x_in3]

        def sb(name, *free, parts=P):
            return ctx.enter_context(nc.sbuf_tensor(name, [parts, *free], F32))

        ps = [ctx.enter_context(nc.psum_tensor(f"ps{b}", [P, 512], F32)) for b in range(8)]

        X = sb("X", T, D)
        at_HT = nc.sbuf_base
        HT = sb("HT", KD, SEQ)
        at_WR = nc.sbuf_base
        WR = sb("WR", NS, 1024)
        ident, swap2 = sb("ident", P), sb("swap2", P)
        tri, cos2, sin2 = sb("tri", SEQ), sb("cos2", SEQ), sb("sin2", SEQ)
        cmask, valid = sb("cmask", T, 32), sb("valid", T)
        rows, cols = sb("rows", P), sb("cols", ROWS)
        postg = sb("postg", D)
        gbias, b2v = sb("gbias", DEPTH, NGATE), sb("b2v", DEPTH, HD)
        w2k, w2v = sb("w2k", DEPTH, 2, P), sb("w2v", DEPTH, 2, HD)
        neghalf = sb("neghalf", T)
        ones = sb("ones", 1)
        ss, ms, rstd = sb("ss", T), sb("ms", T), sb("rstd", T)
        pss, pms, prstd = sb("pss", T, 2), sb("pms", T), sb("prstd", T)
        kcBD, vBD = sb("kcBD", KVG, 2, 32), sb("vBD", KVG, 4, HD)
        hidk, hidv, hidr = sb("hidk", 2, 64), sb("hidv", 2, KVG, 32), sb("hidr", 2, KVG, 4, 32)
        gf, gx, gate = sb("gf", T, 32), sb("gx", T, NGATE), sb("gate", T, NGATE)
        ffz, ffm, ffc = (sb(n, SEQ, parts=8) for n in ("ffz", "ffm", "ffc"))
        mn, rs, rg = sb("mn", 4), sb("rs", NU), sb("rg", 3, 4)
        cmn, csum = sb("cmn", NH), sb("csum", NH)

        BIGW = 28672
        at_BIG = nc.sbuf_base
        BIG = sb("BIG", BIGW)

        def parts(name, byte, *free):
            return nc.alloc_sbuf_tensor_at(name, [P, *free], F32R, offset=byte)

        HT_R, WR_R = parts("HT_R", at_HT, KD, SEQ), parts("WR_R", at_WR, NS, 1024)

        def carve(at, *shape):
            n = int(np.prod(shape))
            assert at + n <= BIGW, (at, n)
            v = BIG[:, at:at + n]
            if len(shape) == 2:
                v = v.rearrange("p (a b) -> p a b", b=shape[1])
            if len(shape) == 3:
                v = v.rearrange("p (a b c) -> p a b c", b=shape[1], c=shape[2])
            return v

        qT, qrT = carve(0, 4, SEQ), carve(2048, 4, SEQ)
        ksT, kwT = carve(4096, 2, SEQ), carve(5120, 2, SEQ)
        fq, fk = carve(6144, NH, SEQ), carve(10240, NH, SEQ)
        vn, fv = carve(14336, T, 256), carve(15360, T, 512)
        O = carve(17408, T, D)
        uT_hi, uT_lo = parts("uT_hi", at_BIG, FG, SEQ), parts("uT_lo", at_BIG + 4 * 4096, FG, SEQ)
        Y = O
        A0 = 21504
        xn = carve(A0, 2, D)
        junk = carve(A0 + 2048, D)
        relu = carve(A0 + 3072, 2, SEQ)
        HL_IN = [carve(17408, KD, SEQ), parts("HL_IN", at_BIG + 4 * 17408, KD, SEQ)]
        HL_MLP = [carve(8192, KD, SEQ), parts("HL_MLP", at_BIG + 4 * 8192, KD, SEQ)]
        WH_FIRST = parts("WH_FIRST", at_BIG + 4 * 6144, 8, 1024)
        WH_LAST = parts("WH_LAST", at_BIG + 4 * (A0 + 3072), 4, 1024)
        WH_MLP = parts("WH_MLP", at_BIG + 4 * 12288, 4, 1024)
        WH_OUT = parts("WH_OUT", at_BIG, 6, 1024)
        WH_OUT6, WH_OUT7 = parts("WH_OUT6", at_BIG + 4 * 14336, 1024), parts("WH_OUT7", at_BIG + 4 * 6144, 1024)
        HL_MIX = [carve(10240, KD, SEQ), parts("HL_MIX", at_BIG + 4 * 10240, KD, SEQ)]
        junk2 = carve(A0 + 4096, 512)
        kraw, rcos, rsin = carve(A0, 2, SEQ), carve(A0 + 1024, 2, SEQ), carve(A0 + 2048, 2, SEQ)
        X2 = [carve(A0 + 3072, 2, SEQ), carve(A0 + 4096, 2, SEQ)]
        E = [carve(A0 + 5120, LP, 2 * NCMP), carve(A0 + 5120 + LP * 2 * NCMP, LP, 2 * NCMP)]
        PR = carve(A0 + 3072, 4, SEQ)
        PT = carve(A0 + 5120, 2, SEQ)
        CS, CP = carve(A0, NH, 32), carve(A0 + 256, KVG, P)
        CX = carve(A0 + 512, KVG, P)
        CO = carve(A0 + 768, T, 512)

        R_PRE1, R_QN, R_KVN, R_AO, R_SO = 0, 8, 10, 11, 15
        R_NORM, R_B1, R_POS, R_B2K, R_BF = 19, 51, 59, 123, 125

        def t_blocks(w, n):
            return w.rearrange("(k p) c -> p k c", p=P)[:, :, n[0]:n[1]]

        LAST_HALF = (NG - 1, 1)

        def down_count(l, g, half, i):
            return NF * l + FG * g + FG // 2 * half + i + 1

        units = []

        def unit(name, slots, pieces, sema, value):
            units.append(Unit(name, slots, pieces, (sema, value)))

        def colblock(name, w, c, n, sema, value):
            unit(name, 1, [((0, n), t_blocks(w, (c, c + n)))], sema, value)

        def quad(name, pieces, sema, value):
            unit(name, 4, pieces, sema, value)

        if first:
            one_units(a, unit, colblock, quad, t_blocks, sem)
        B1 = int(first)
        if second:
            for l in range(DEPTH):
                w = a["w_in_2"][l]
                at = 0
                pieces = []
                for c, n in ((C_VS, P), (C_VW, P), (C_GATE, NGATE), (C_FF, 8)):
                    pieces.append(((at, n), t_blocks(w, (c, c + n))))
                    at += n
                pj = lambda n: NPJ * l + n + 1
                quad(f"n1_{l}", pieces, sem.proj, pj(3))
                for i, c in enumerate((C_KC, C_VC, C_KS, C_KW)):
                    colblock(f"t{4 + i}_{l}", w, c, P, sem.proj, pj(4 + i))
                for i, kind in enumerate("kv"):
                    w1 = a[f"cmp_w1_{kind}_2"][l]
                    unit(f"w1{kind}_{l}", 4, [(None, w1.rearrange("(k p) c -> p k c", p=P))], sem.hid_ps, 2 * l + i + 1)
                for i in range(4):
                    colblock(f"t{8 + i}_{l}", w, C_Q + P * i, P, sem.proj, pj(8 + i))
                quad(f"n2_{l}", [((0, 512), t_blocks(w, (C_FV, C_FV + 512)))], sem.proj, pj(15))
                for i in range(8):
                    colblock(f"t{16 + i}_{l}", w, C_FQ + P * i, P, sem.proj, pj(16 + i))
                for k in range(KD):
                    unit(f"wo{k}_{l}", 1, [(None, a["w_out_2"][l][P * k:P * k + P, :])], sem.out_ps,
                         8 * (B1 + l) + 8)
                for g in range(NG):
                    for f in range(FG * g, FG * g + FG):
                        colblock(f"up{f}_{l}", a["w_up_2"][l], P * f, P, sem.up_ps, NF * l + f + 1)
                    for half in range(2):
                        for i in range(FG // 2):
                            f = FG * g + 2 * i
                            wd = a["w_down_2"][l][P * f:P * f + 2 * P, 512 * half:512 * half + 512]
                            if (g, half) == LAST_HALF:
                                i = FG // 2 - 1
                            unit(f"dn{half}_{f}_{l}", 1, [(None, wd.rearrange("(k p) c -> p k c", p=P))],
                                 sem.down, down_count(l, g, half, i))

        by_name, at, owner, loads = {}, 0, [None] * NS, [0] * NS
        for u in units:
            if at % NS + u.slots > NS or (u.slots == 4 and at % 4):
                at += (-at) % 4
            u.slot = at % NS
            for s in range(u.slot, u.slot + u.slots):
                if owner[s] is not None and owner[s].used not in u.free:
                    u.free.append(owner[s].used)
                owner[s] = u
            loads[u.slot] += 16 * len(u.pieces)
            u.landed = loads[u.slot]
            by_name[u.name] = u
            at += u.slots

        def slots(u):
            return WR[:, u.slot:u.slot + u.slots, :].rearrange("p s n -> p (s n)")

        def arrived(pe, name):
            u = by_name[name]
            pe.wait_ge(wring[u.slot], u.landed)
            return slots(u)

        def block_of(name, pe, width=P):
            return arrived(pe, name).rearrange("p (k c) -> p k c", c=width)

        def split_of(j):
            if j < 4:
                return "n1", j, 288
            if 12 <= j < 16:
                return "n2", j - 12, None
            if j < NPJ:
                return f"t{j}", 0, None
            if j < J_MLP:
                return f"wo{j - J_OUT}", 0, None
            g, i = divmod(j - J_MLP, 2 * FG)
            if i < FG:
                return f"up{FG * g + i}", 0, None
            half, i = divmod(i - FG, FG // 2)
            return f"dn{half}_{FG * g + 2 * i}", 0, None

        def parts_of(l, j):
            name, i, width = split_of(j)
            u = by_name[f"{name}_{l}"]
            if j < NPJ:
                hi = WH_FIRST[:, j % 8, :] if j < 16 else WH_LAST[:, j % 4, :]
            elif j < J_MLP:
                hi = (*(WH_OUT[:, k, :] for k in range(6)), WH_OUT6[:], WH_OUT7[:])[j - J_OUT]
            else:
                hi = WH_MLP[:, j % 4, :]
            parts = hi, WR_R[:, u.slot + i, :], WR[:, u.slot + i, :]
            if width is not None:
                parts = [v.rearrange("p (k c) -> p k c", c=512)[:, :, 0:width] for v in parts]
            return u, *parts

        def split_hi(act, l, j):
            u, hi, lo, whole = parts_of(l, j)
            act.wait_ge(wring[u.slot], u.landed)
            if 8 <= j < 12:
                act.wait_ge(sem.proj, NPJ * l + 4)
            elif 12 <= j < 16:
                act.wait_ge(sem.proj, NPJ * l + j - 7)
            elif 20 <= j < NPJ:
                act.wait_ge(sem.proj, NPJ * l + j - 3)
            elif j >= J_MLP + 4:
                g, i = divmod(j - 4 - J_MLP, 2 * FG)
                if i < FG:
                    act.wait_ge(sem.up_ps, NF * l + FG * g + i + 1)
                else:
                    act.wait_ge(sem.down, down_count(l, g, (i - FG) // (FG // 2), i % (FG // 2)))
            nc.scalar.activation(hi, whole, ACT.Copy).then_inc(sem.w_hi, 1)

        def split_lo(eng, l, j):
            u, hi, lo, whole = parts_of(l, j)
            eng.wait_ge(sem.w_hi, NSPLIT * l + j + 1)
            if j == J_MLP or J_OUT <= j < J_MLP or l and j == 0:
                eng.wait_ge(sem.w_lo, NSPLIT * l + j)
            (nc.gpsimd if J_OUT <= j < J_MLP else nc.vector).tensor_tensor(lo, whole, hi.bitcast(F32), ALU.subtract).then_inc(sem.w_lo, 1)

        def split(pe, l, j):
            pe.wait_ge(sem.w_lo, NSPLIT * l + j + 1)
            _, hi, lo, _ = parts_of(l, j)
            return hi, lo

        def product(out_, w, x, start, stop):
            nc.tensor.matmul(out_, w[0], x[0], start=start, stop=False)
            nc.tensor.matmul(out_, w[0], x[1], start=False, stop=False)
            return nc.tensor.matmul(out_, w[1], x[0], start=False, stop=stop)

        def norm_squares(act, v, x_count):
            for t in range(T):
                act.wait_ge(*x_count(t))
                if v or t:
                    act.wait_ge(sem.sq, T * v + t)
                if v and t == 0:
                    act.wait_ge(sem.rstd, T * v)
                nc.scalar.activation(junk if v + V0 else BIG[:, 6144:6144 + D], X[:, t, :], ACT.Square, accum_out=ss[:, t:t + 1]).then_inc(sem.sq, 1)

        def norm_rstd(pool, v):
            for t in range(T):
                pool.wait_ge(sem.sq, T * v + t + 1)
                if v:
                    pool.wait_ge(sem.xn, T * (v - 1) + t + 1)
                pool_link(nc.gpsimd.tensor_scalar(ms[:, t:t + 1], ss[:, t:t + 1], 1.0 / D, EPS, ALU.mult, ALU.add))
                nc.gpsimd.tensor_tensor(rstd[:, t:t + 1], ms[:, t:t + 1], neghalf[:, 0:1], ALU.pow).then_inc(sem.rstd, 1)

        def norm_scale(dve, v, t):
            dve.wait_ge(sem.rstd, T * v + t + 1)
            if T * v + t >= 2:
                dve.wait_ge(sem.xT, 2 * (T * v + t - 1))
            nc.vector.tensor_scalar(xn[:, t % 2, :], X[:, t, :], rstd[:, t:t + 1], None, ALU.mult).then_inc(sem.xn, 1)

        def norm_transpose(pe, v, t):
            pe.wait_ge(sem.xn, T * v + t + 1)
            for half in range(2):
                i = 2 * t + half
                if i >= 4 and v + V0 == 0:
                    pe.wait_ge(sem.hT, 8 * v + i - 3)
                elif i >= 4:
                    pe.wait_ge(sem.x_gained, 8 * (v + V0 - 1) + i - 3)
                for k in range(4):
                    last = nc.tensor.transpose(ps[i % 4][:, P * k:P * k + P],
                                               xn[:, t % 2, 512 * half + P * k:512 * half + P * k + P], ident[:])
                last.then_inc(sem.xT, 1)

        def norm_evacuate(dve, v, t, chunked, low):
            g0 = R_PRE1 if chunked else R_NORM + 8 * (v + V0 - 1)
            for half in range(2):
                i = 2 * t + half
                dve.wait_ge(sem.xT, 8 * v + i + 1)
                gain = cols[:, g0 + 4 * half:g0 + 4 * half + 4]
                if chunked:
                    for k in range(4):
                        src = ps[i % 4][:, P * k:P * k + P].rearrange("p (c i) -> p i c", i=L)
                        dst = HT[:, 4 * half + k, :].rearrange("p (i c) -> p i c", i=L)[:, :, t * (P // L):(t + 1) * (P // L)]
                        last = nc.vector.tensor_scalar(dst, src, gain[:, k:k + 1], None, ALU.mult)
                else:
                    last = nc.vector.tensor_tensor(
                        low[0][:, 4 * half:4 * half + 4, P * t:P * t + P],
                        ps[i % 4][:].rearrange("p (k n) -> p k n", k=4),
                        gain[:, :, None].to_broadcast([P, 4, P]), ALU.mult)
                last.then_inc(sem.hT if chunked else sem.x_gained, 1)

        def norm_parts(low, i):
            k, t = 4 * (i % 2), i // 2
            return [v[:, k:k + 4, P * t:P * t + P] for v in (HT_R, low[1], low[0])]

        def norm_hi(act, v, low, i):
            hi, _, whole = norm_parts(low, i)
            act.wait_ge(sem.x_gained, 8 * (v + V0 - 1) + i + 1)
            nc.scalar.activation(hi, whole, ACT.Copy).then_inc(sem.x_hi, 1)

        def norm_lo(pool, v, low):
            for i in range(8):
                hi, lo, whole = norm_parts(low, i)
                pool.wait_ge(sem.x_hi, 8 * (v + V0 - 1) + i + 1)
                nc.gpsimd.tensor_tensor(lo, whole, hi.bitcast(F32), ALU.subtract).then_inc(sem.hT, 1)

        def norm_dve(dve, v, chunked=False, low=None, behind_two=None):
            norm_scale(dve, v, 0)
            norm_scale(dve, v, 1)
            for t in range(T):
                norm_evacuate(dve, v, t, chunked, low)
                if t == 1 and behind_two:
                    behind_two()
                if t + 2 < T:
                    norm_scale(dve, v, t + 2)

        def post_squares(act, w, tile_half, ready, first_bank=0):
            for e in range(8):
                t, half = tile_half(e)
                act.wait_ge(*ready(e))
                if w or e:
                    act.wait_ge(sem.post_sq, 8 * w + e)
                if w and e == 0:
                    act.wait_ge(sem.post_rstd, T * w)
                nc.scalar.activation(junk2, ps[(e + first_bank) % 8][:], ACT.Square,
                                     accum_out=pss[:, t, half:half + 1]).then_inc(sem.post_sq, 1)

        def post_factor(pool, w, tile_half):
            last_e = {tile_half(e)[0]: e for e in range(8)}
            for t in range(T):
                pool.wait_ge(sem.post_sq, 8 * w + last_e[t] + 1)
                if w:
                    pool.wait_ge(sem.x_new, T * (w - 1) + t + 1)
                pool_link(nc.gpsimd.tensor_tensor(pms[:, t:t + 1], pss[:, t, 0:1], pss[:, t, 1:2], ALU.add))
                pool_link(nc.gpsimd.tensor_scalar(pms[:, t:t + 1], pms[:, t:t + 1], 1.0 / D, EPS, ALU.mult, ALU.add))
                nc.gpsimd.tensor_tensor(prstd[:, t:t + 1], pms[:, t:t + 1], neghalf[:, 0:1], ALU.pow)\
                    .then_inc(sem.post_rstd, 1)

        def post_add(dve, w, tile_half, first_bank=0, before=None):
            dve.wait_ge(sem.postgain_in, 16 * (w + 1))
            last_e = {tile_half(e)[0]: e for e in range(8)}

            def add(t):
                dve.wait_ge(sem.post_rstd, T * w + t + 1)
                dve.wait_ge(sem.post_y, 8 * w + last_e[t] + 1)
                nc.vector.scalar_tensor_tensor(X[:, t, :], Y[:, t, :], prstd[:, t:t + 1], X[:, t, :],
                                               ALU.mult, ALU.add).then_inc(sem.x_new, 1)

            waiting = []
            for e in range(8):
                t, half = tile_half(e)
                if before:
                    before(e)
                dve.wait_ge(sem.post_sq, 8 * w + e + 1)
                nc.vector.tensor_tensor(Y[:, t, 512 * half:512 * half + 512], ps[(e + first_bank) % 8][:],
                                        postg[:, 512 * half:512 * half + 512], ALU.mult).then_inc(sem.post_y, 1)
                if e == last_e[t]:
                    waiting.append(t)
                if len(waiting) > 1 or waiting and before:
                    add(waiting.pop(0))
            for t in waiting:
                add(t)

        MIX = lambda e: (e // 2, e % 2)
        MLP = lambda e: (e % 4, e // 4)
        mixed = lambda w: lambda e: (sem.out_ps, 8 * w + e + 1)

        def out_projection(pe, w, weights):
            views = [arrived(pe, n) for n in weights]
            for e in range(8):
                t, half = MIX(e)
                for k in range(KD):
                    last = nc.tensor.matmul(ps[e][:], HT[:, k, P * t:P * t + P], views[k][:, 512 * half:512 * half + 512],
                                            start=(k == 0), stop=(k == KD - 1))
                last.then_inc(sem.out_ps, 1)

        chains = {"act": 0, "dve": 0, "pool": 0}

        def dve_link(ins, eng=nc.vector):
            chains["dve"] += 1
            ins.then_inc(sem.dve_chain, 1)
            eng.wait_ge(sem.dve_chain, chains["dve"])

        def pool_link(ins, eng=nc.gpsimd):
            chains["pool"] += 1
            ins.then_inc(sem.pool_chain, 1)
            eng.wait_ge(sem.pool_chain, chains["pool"])

        def act_link(ins, eng=nc.scalar):
            chains["act"] += 1
            ins.then_inc(sem.act_chain, 1)
            eng.wait_ge(sem.act_chain, chains["act"])

        if first:
            GA, GS = carve(0, T, WIDE), carve(2048, T, WIDE)
            ZT = carve(4096, 4, SEQ)
            YP = carve(6144, T, WIDE)
            ZN = carve(8192, 2, 512)
            UT = carve(9216, G, NC)
            W1 = carve(11264, DQ, P)
            M3 = carve(13312, DQ, NK * CH)
            U8 = BIG[0:NC, 11264:11264 + G * P].rearrange("p (g n) -> p g n", g=G)
            M1 = carve(15616, DQ, L * CH)
            KT = BIG[0:CH, 11264:11264 + GQ * 240].rearrange("p (g n) -> p g n", g=GQ)
            TMP = BIG[:, 17664:17664 + 1152]
            TT = carve(18816, GQ, P)
            CC, SS_ = carve(19840, DQ, NC), carve(20864, DQ, NC)
            SA, SV = carve(21888, DQ, NC), carve(22912, DQ, NC)
            B1_, B2_ = carve(23936, DQ, CH), carve(24192, DQ, CH)
            BB, BW = carve(24448, DQ, CH), carve(24704, DQ, CH)
            C1_, C2_ = carve(24960, 2, P), carve(25216, 2, P)
            CN = carve(25472, 4, P)
            AR, AI = carve(25984, NK, DG), carve(26560, NK, DG)
            WP = BIG[:, 27136:27136 + 2 * 6 * DG].rearrange("p (a n g) -> p a n g", a=2, n=6)
            YS = BIG[:, 8192:8192 + 512]
            TMP_P = BIG[:, 8704:8704 + 512]
            LAM = BIG[0:DG, 27904:28160].rearrange("p (a n) -> p a n", a=2)
            DROW = BIG[0:G, 28160:28176]
            PA = BIG[:, 19840:22144].rearrange("p (n g) -> p n g", g=DG)
            LDT = BIG[:, 28176:28240]
            CRE, CIM = BIG[:, 28240:28304], BIG[:, 28304:28368]
            DT_ = BIG[0:CH, 28368:28400]
            DK = BIG[0:CH, 28400:28528].rearrange("p (g n) -> p g n", g=GQ)
            DECAY = BIG[:, 28528:28592]
            zss, zms, zrs = BIG[:, 28592:28594], BIG[:, 28594:28596], BIG[:, 28596:28604].rearrange("p (t n) -> p t n", n=2)
            QN, KN = carve(8192, H1, SEQ), carve(10240, H1, SEQ)
            QR, V1 = carve(12288, 2, SEQ), carve(13312, T, WIDE)
            COS1, SIN1 = BIG[:, 15360:15872], BIG[:, 15872:16384]
            O1 = carve(16384, T, WIDE)
            PR1, PT1 = carve(18432, 2, SEQ), carve(19456, 2, SEQ)
            YG, GT_ = carve(20480, T, WIDE), carve(22528, 4, SEQ)
            GTMP, BGLU = carve(24576, 2, WIDE), BIG[:, 25600:26112]
            ANG, ROT = carve(26112, 2, SEQ), carve(27136, 2, SEQ)
            POS = BIG[:, 24576:25088].bitcast(I32)
            JUNK1 = BIG[:, 28160:28672]
            KRT = ZT[:, 3, :]
            JUNK_Z = BIG[:, 6144:6144 + 256]
            col = sb("col", 8)
            rows1 = sb("rows1", P, parts=R_NORM)
            swap1, turn = sb("swap1", P), sb("turn", P)
            ass, ams, ars = sb("ass", 2, T), sb("ams", T), sb("ars", 2, T)

        def one_params_dma(act):
            for i, n in enumerate(("s5_lam_re", "s5_lam_im")):
                for o in range(2):
                    act.dma_start(LAM[:, i, ST * o:ST * o + ST], a[n][0].rearrange("d g p -> (d g) p"))\
                        .then_inc(sem.par_in, 16)
            act.dma_start(LDT, a["s5_log_dt"].rearrange("a d g -> a (d g)").to_broadcast([P, DG])).then_inc(sem.par_in, 16)
            for dst, n in ((col, "c_col"), (swap1, "c_swap1"), (turn, "c_turn")):
                act.dma_start(dst[:], a[n]).then_inc(sem.par_in, 16)
            act.dma_start(DROW, a["s5_d"][0].rearrange("(g h) -> g h", h=CH)).then_inc(sem.par_in, 16)

        def one_bc_dma(act, q):
            if q:
                act.wait_ge(sem.b_bar, q)
                act.wait_ge(sem.cT_ps, q)
            gs_ = slice(GQ * q, GQ * q + GQ)
            for d in range(2):
                re, im = (a[n][0, d, gs_].rearrange("g p h -> p g h") for n in ("s5_b_re", "s5_b_im"))
                for dst, parts in ((B1_, (re, im)), (B2_, (im, re))):
                    for o in range(2):
                        act.dma_start(dst[ST * o:ST * o + ST, GQ * d:GQ * d + GQ, :], parts[o]).then_inc(sem.bc_in, 16)
                re, im = (a[n][0, d, gs_].rearrange("g h p -> (g h) p") for n in ("s5_c_re", "s5_c_im"))
                for order, parts in enumerate(((re, im), (im, re))):
                    for o in range(2):
                        act.dma_start(CN[:, 2 * order + d, ST * o:ST * o + ST], parts[o]).then_inc(sem.bc_in, 16)

        N_BC, N_PAR = 16 * 2 * 8, 16 * 9

        def one_pe(pe):
            for t in range(T):
                norm_transpose(pe, 0, t)
            pe.wait_ge(sem.par_in, N_PAR)
            for i in range(2):
                nc.tensor.transpose(ps[6][:, DG * i:DG * i + DG], LAM[:, i, :], ident[0:DG, 0:DG])
            nc.tensor.transpose(ps[6][0:CH, P:P + G], DROW, ident[0:G, 0:G]).then_inc(sem.par_ps, 1)
            pe.wait_ge(sem.hT, 8)

            def natural(name, n, m, width, done):
                wv = block_of(name, pe, 512)
                for k in range(KD):
                    last = nc.tensor.matmul(ps[n % 4][:, 0:width], HT[:, k, P * m:P * m + P], wv[:, k, 0:width],
                                            start=(k == 0), stop=(k == KD - 1))
                last.then_inc(done, 1)

            for m in range(T):
                natural("u", m, m, 512, sem.u_ps)
            for m in range(T):
                pe.wait_ge(sem.u_sb, m + 1)
                natural("gs", m, m, 512, sem.gs_ps)
            turn_rows(pe)
            pe.wait_ge(sem.cols_ready, 1)
            s5_pe_c(pe, 0)
            pe.wait_ge(sem.par, 1)
            pe.wait_ge(sem.cols_ready, 2)
            pe.wait_ge(sem.cT, 1)
            for b in range(4):
                for g in range(8):
                    last = nc.tensor.transpose(ps[4 + b][:, NC * g:NC * g + NC], U8[:, 8 * b + g, :], ident[0:NC, 0:NC])
                last.then_inc(sem.uT_ps, 1)
            for m in range(T):
                pe.wait_ge(sem.gs, m + 1)
                natural("za", m, m, 448, sem.za_ps)
            for m in range(T):
                pe.wait_ge(sem.zn, m + 1)
                natural("ga", m, m, 512, sem.ga_ps)
                pe.wait_ge(sem.uT, m + 1)
                for k in range(4):
                    last = nc.tensor.transpose(ps[4 + m][:, P * k:P * k + P], ZN[:, m % 2, P * k:P * k + P], ident[:])
                last.then_inc(sem.znT_ps, 1)
            pe.wait_ge(sem.ga, T)
            pe.wait_ge(sem.znT, T)
            s5_pe_front(pe, 0)
            for q in range(NQ):
                s5_pe_states(pe, q)
                s5_pe_outputs(pe, q)
                if q + 1 < NQ:
                    s5_pe_c(pe, q + 1)
                    s5_pe_front(pe, q + 1)
                s5_pe_turn(pe, q)
            latent_pe(pe)
            glu_pe(pe)
            attention_pe(pe)
            mix_pe(pe)

        def s5_pe_c(pe, q):
            pe.wait_ge(sem.bc_in, N_BC * (q + 1))
            if q:
                pe.wait_ge(sem.taps, q)
            for j in range(4):
                last = nc.tensor.transpose(ps[7][:, P * j:P * j + P], CN[:, j, :], ident[:])
            last.then_inc(sem.cT_ps, 1)

        def s5_pe_front(pe, q):
            pe.wait_ge(sem.m1, 2 * q + 2)
            if q:
                pe.wait_ge(sem.st_sb, 2 * q)
                pe.wait_ge(sem.turned, 4 * q)
            for b in range(4):
                for j in range(4):
                    last = nc.tensor.transpose(ps[b][:, P * j:P * j + P], M1[:, 4 * b + j, :], ident[:])
                last.then_inc(sem.m1T_ps, 1)

        def s5_pe_states(pe, q):
            pe.wait_ge(sem.w1T, 4 * (q + 1))
            for d in range(2):
                for g in range(GQ):
                    u = UT[:, GQ * q + g, :]
                    last = nc.tensor.matmul(ps[d][:, NC * g:NC * g + NC], W1[:, GQ * d + g, :], u[:, ::-1] if d else u,
                                            start=True, stop=True)
                last.then_inc(sem.st_ps, 1)
            def by_minus_i(r):
                for d in range(2):
                    if r == 0:
                        pe.wait_ge(sem.st_sb, 2 * q + d + 1)
                    else:
                        pe.wait_ge(sem.state, 3 * q + d + 1)
                        pe.wait_ge(sem.turned, 4 * q + d + 1)
                    nc.tensor.matmul(ps[2 + d][:], turn[:], SA[:, GQ * d:GQ * d + GQ, :].rearrange("p g c -> p (g c)"),
                                     start=True, stop=True).then_inc(sem.turn_ps, 1)

            by_minus_i(0)
            pe.wait_ge(sem.m3, 2 * q + 2)
            pe.wait_ge(sem.cT, q + 1)
            pe.wait_ge(sem.b_bar, q + 1)
            if q:
                pe.wait_ge(sem.yp, 2 * q)
                pe.wait_ge(sem.y_sb, q)
            for b in range(2):
                for j in range(4):
                    g = 4 * b + j
                    lo = ps[4 + b][0:CH, P * j:P * j + P]
                    nc.tensor.matmul(lo, BB[:, GQ + g, :], M3[:, GQ + g, CH:NK * CH], start=True, stop=True)
                    nc.tensor.matmul(lo[:, P - CH:P], BB[:, g, :], M3[:, g, 0:CH], start=False, stop=True,
                                     skip_group_check=True)
                    last = nc.tensor.matmul(ps[6 + b][0:CH, 112 * j:112 * j + 112], BB[:, g, :], M3[:, g, CH:L * CH],
                                            start=True, stop=True)
                last.then_inc(sem.tap_ps, 1)
            by_minus_i(1)

        def s5_pe_outputs(pe, q):
            pe.wait_ge(sem.toep, 128 * (q + 1))
            pe.wait_ge(sem.state, 3 * q + 3)
            for g in range(GQ):
                y = ps[6][:, NC * g:NC * g + NC]
                nc.tensor.matmul(y, TT[:, g, :], UT[:, GQ * q + g, :], start=True, stop=True)
                nc.tensor.matmul(y[:, 1:NC], M3[:, g, CH:NK * CH], SV[:, g, 0:NC - 1], start=False, stop=True,
                                 skip_group_check=True)
                last = nc.tensor.matmul(y[:, 0:NC - 1], M3[:, GQ + g, 0:L * CH], SV[:, GQ + g, 0:NC - 1][:, ::-1],
                                        start=False, stop=True, skip_group_check=True)
            last.then_inc(sem.y_ps, 1)

        def s5_pe_turn(pe, q):
            pe.wait_ge(sem.y_sb, q + 1)
            for b in range(2):
                for j in range(4):
                    g = 4 * b + j
                    last = nc.tensor.transpose(ps[4 + b][0:NC, P * j:P * j + P], YS[:, NC * g:NC * g + NC], ident[:])
                last.then_inc(sem.yT_ps, 1)

        def glu_pe(pe):
            pe.wait_ge(sem.ge, 1)
            for m in range(T):
                pe.wait_ge(sem.v1, m + 1)
                for k in range(4):
                    last = nc.tensor.transpose(ps[m][:, P * k:P * k + P], YG[:, m, P * k:P * k + P], ident[:])
                last.then_inc(sem.geT_ps, 1)
            wv = block_of("glu", pe, 512)
            for m in range(T):
                pe.wait_ge(sem.geT, m + 1)
                if m == 0:
                    pe.wait_ge(sem.rq, 2)
                    pe.wait_ge(sem.rope_done, 3)
                for k in range(4):
                    last = nc.tensor.matmul(ps[4 + m][:], GT_[:, k, P * m:P * m + P], wv[:, k, :], start=(k == 0), stop=(k == 3))
                last.then_inc(sem.glu_ps, 1)

        def latent_pe(pe):
            wq = arrived(pe, "uq")
            pe.wait_ge(sem.turned, 4 * NQ)
            for h in range(H1):
                for k in range(2):
                    last = nc.tensor.matmul(ps[h][:], wq[:, 768 * k + P * h:768 * k + P * h + P], ZT[:, k, :],
                                            start=(k == 0), stop=(k == 1))
                last.then_inc(sem.qn_ps, 1)
            pe.wait_ge(sem.yp, 2 * NQ)
            for r in range(2):
                for k in range(2):
                    c = 768 * k + 512 + P * r
                    last = nc.tensor.matmul(ps[4 + r][:], wq[:, c:c + P], ZT[:, k, :], start=(k == 0), stop=(k == 1))
                last.then_inc(sem.rq_ps, 1)
            wk = arrived(pe, "ukv")
            for h in range(H1):
                pe.wait_ge(sem.qn, h + 1)
                nc.tensor.matmul(ps[h][:], wk[:, 256 * h:256 * h + P], ZT[:, 2, :], start=True, stop=True).then_inc(sem.kn_ps, 1)
            for r in range(3):
                b = 6 + r % 2
                if r == 0:
                    pe.wait_ge(sem.y_sb, NQ)
                    pe.wait_ge(sem.taps, NQ)
                else:
                    pe.wait_ge(sem.rq, r)
                if r == 2:
                    pe.wait_ge(sem.rope_done, 1)
                nc.tensor.matmul(ps[b][:], swap1[:], KRT if r == 0 else QR[:, r - 1, :], start=True, stop=True)\
                    .then_inc(sem.rope_ps, 1)
            wvv = wk.rearrange("p (h c) -> p h c", h=H1)[:, :, NOPE:NOPE + VD]
            for m in range(T):
                pe.wait_ge(sem.kn, m + 1)
                nc.tensor.matmul(ps[m][:], ZT[:, 2, P * m:P * m + P], wvv, start=True, stop=True).then_inc(sem.v1_ps, 1)

        NU1 = H1 * T

        def attention_pe(pe):
            pe.wait_ge(sem.geT, T)
            pe.wait_ge(sem.v1, T)
            pe.wait_ge(sem.rope_done, 3)
            pe.wait_ge(sem.rq, 2)
            pe.wait_ge(sem.qn, H1)
            pe.wait_ge(sem.kn, H1)
            for u in range(NU1 + 4):
                if u < NU1:
                    h, m = u // T, u % T
                    if u >= 3:
                        pe.wait_ge(sem.a_exp, u - 2)
                    tok = slice(P * m, P * m + P)
                    nc.tensor.matmul(ps[u % 3][:], QN[:, h, tok], KN[:, h, :], start=True, stop=False)
                    o = 64 * (h % 2)
                    nc.tensor.matmul(ps[u % 3][:], QR[o:o + 64, h // 2, tok], KRT[o:o + 64, :], start=False, stop=True)\
                        .then_inc(sem.a_s_ps, 1)
                w = u - 2
                if 0 <= w < NU1:
                    if w == 0:
                        pe.wait_ge(sem.glu_x, T)
                    pe.wait_ge(sem.a_exp, w + 1)
                    if w >= 2:
                        pe.wait_ge(sem.a_pT, w - 1)
                    for b in range(T):
                        last = nc.tensor.transpose(ps[3 + w % 2][:, P * b:P * b + P], PR1[:, w % 2, P * b:P * b + P], ident[:])
                    last.then_inc(sem.a_pT_ps, 1)
                w = u - 3
                if 0 <= w < NU1:
                    h, m = w // T, w % T
                    pe.wait_ge(sem.a_pT, w + 1)
                    if m == 0 and h >= 2:
                        pe.wait_ge(sem.a_o, h - 1)
                    for b in range(T):
                        last = nc.tensor.matmul(ps[5 + h % 2][:, P * m:P * m + P], PT1[:, w % 2, P * b:P * b + P],
                                                V1[:, b, P * h:P * h + P], start=(b == 0), stop=(b == T - 1))
                    last.then_inc(sem.a_o_ps, 1)

        def mix_pe(pe):
            for i in range(8):
                m = i % 4
                if i < 4:
                    pe.wait_ge(sem.ssm_o, m + 1)
                    src = YG[:, m, :]
                else:
                    pe.wait_ge(sem.at_o, m + 1)
                    src = O1[:, m, :]
                if i == 0:
                    pe.wait_ge(sem.a_o, H1)
                for k in range(4):
                    last = nc.tensor.transpose(ps[i][:, P * k:P * k + P], src[:, P * k:P * k + P], ident[:])
                last.then_inc(sem.m1ix_ps, 1)
            pe.wait_ge(sem.m1ix, 8)
            out_projection(pe, 0, [f"wo{k}" for k in range(KD)])

        TT2 = nc.vector.tensor_tensor
        TS = nc.vector.tensor_scalar

        def reduce_angle(x, t1, t2):
            dve_link(TS(t1, x, 1.0 / TWO_PI, ROUND, ALU.mult, ALU.add))
            dve_link(TS(t1, t1, ROUND, None, ALU.subtract))
            for part in (PI2_A, PI2_B, PI2_C):
                dve_link(nc.vector.scalar_tensor_tensor(x, t1, -part, x, ALU.mult, ALU.add))
            dve_link(TS(t1, x, PI_SAFE, -PI_SAFE, ALU.min, ALU.max))
            dve_link(TS(t2, t1, -1.0, None, ALU.mult))
            dve_link(TT2(t2, t2, t1, ALU.max))
            return TS(t2, t2, -1.0, float(np.float32(np.pi / 2)), ALU.mult, ALU.add)

        def cmul(out_c, out_s, ac, as_, bc, bs, t1, t2):
            TT2(t1, as_, bs, ALU.mult)
            TT2(t2, as_, bc, ALU.mult)
            TT2(out_c, ac, bc, ALU.mult)
            dve_link(TT2(out_s, ac, bs, ALU.mult))
            TT2(out_c, out_c, t1, ALU.subtract)
            dve_link(TT2(out_s, out_s, t2, ALU.add))

        def one_params(dve):
            LR, LI, TH, ER, SN, CS_, DEN, T1, T2 = (PA[:, i, :] for i in range(9))
            UC, US, EA = PA[:, 9:18, :], PA[:, 18:27, :], PA[:, 27:36, :]
            dve.wait_ge(sem.par_ps, 1)
            TS(LR, ps[6][:, 0:DG], -1e-4, None, ALU.min)
            nc.vector.tensor_copy(LI, ps[6][:, DG:2 * DG])
            dve_link(nc.vector.tensor_copy(DT_, ps[6][0:CH, P:P + G]))
            dve.wait_ge(sem.dt_e, 1)
            dve_link(TT2(TH, LI, LDT, ALU.mult))
            TT2(ER, LR, LDT, ALU.mult).then_inc(sem.par_exp, 1)
            reduce_angle(TH, T1, T2).then_inc(sem.par_exp, 1)
            dve.wait_ge(sem.par_trig, 2)
            dve.wait_ge(sem.amp, NK)
            dve_link(TT2(T1, CS_, EA[:, 1, :], ALU.mult))
            TT2(T2, SN, EA[:, 1, :], ALU.mult)
            dve_link(TS(T1, T1, 1.0, None, ALU.subtract))
            TT2(CRE, T1, LR, ALU.mult)
            TT2(CIM, T2, LR, ALU.mult)
            dve_link(TT2(T1, T1, LI, ALU.mult))
            dve_link(TT2(T2, T2, LI, ALU.mult))
            dve_link(TT2(CRE, CRE, T2, ALU.add))
            dve_link(TT2(CIM, CIM, T1, ALU.subtract))
            dve_link(TT2(T1, LR, LR, ALU.mult))
            dve_link(TT2(DEN, LI, LI, ALU.mult))
            dve_link(TT2(DEN, DEN, T1, ALU.add))
            dve_link(nc.vector.reciprocal(DEN, DEN))
            dve_link(TT2(CRE, CRE, DEN, ALU.mult))
            dve_link(TT2(CIM, CIM, DEN, ALU.mult))
            dve_link(TS(CIM, CIM, col[:, 2:3], None, ALU.mult))
            nc.vector.memset(UC[:, 0, :], 1.0)
            nc.vector.memset(US[:, 0, :], 0.0)
            nc.vector.tensor_copy(UC[:, 1, :], CS_)
            dve_link(nc.vector.tensor_copy(US[:, 1, :], SN))
            n = 1
            while n < L:
                b = lambda v: v[:, n:n + 1, :].to_broadcast([P, n, DG])
                t1, t2 = TMP[:, 0:n * DG].rearrange("p (n g) -> p n g", g=DG), TMP[:, 512:512 + n * DG].rearrange("p (n g) -> p n g", g=DG)
                cmul(UC[:, n + 1:2 * n + 1, :], US[:, n + 1:2 * n + 1, :], UC[:, 1:n + 1, :], US[:, 1:n + 1, :], b(UC), b(US), t1, t2)
                n *= 2
            TT2(AR, UC, EA, ALU.mult)
            dve_link(TT2(AI, US, EA, ALU.mult))
            nc.vector.tensor_copy(DECAY, EA[:, L, :])
            nc.vector.tensor_copy(WP[:, 0, 0, :], UC[:, L, :])
            dve_link(nc.vector.tensor_copy(WP[:, 1, 0, :], US[:, L, :]))
            for n in range(5):
                c, s = WP[:, 0, n, :], WP[:, 1, n, :]
                cmul(WP[:, 0, n + 1, :], WP[:, 1, n + 1, :], c, s, c, s, TMP[:, 0:DG], TMP[:, DG:2 * DG])
            nc.vector.tensor_copy(T1, T1).then_inc(sem.par, 1)
            dve.wait_ge(sem.par, 1)

        def by_group(v, q, d):
            return v[:, :, G * d + GQ * q:G * d + GQ * q + GQ].rearrange("p k g -> p g k")

        def s5_prepare(dve, q):
            def pg(v, width):
                w = v.rearrange("p (d g) -> p d g", d=2)[:, :, GQ * q:GQ * q + GQ]
                return w[:, :, :, None].to_broadcast([P, 2, GQ, width])

            four = lambda v: v.rearrange("p (d g) n -> p d g n", d=2)
            if q:
                dve.wait_ge(sem.state, 3 * q)
            nc.vector.memset(CC[:, :, 0:1], 1.0)
            dve_link(nc.vector.memset(SS_[:, :, 0:1], 0.0))
            for s in range(6):
                n = 2 ** s
                t = TMP[:, 0:DQ * n].rearrange("p (d g n) -> p d g n", d=2, n=n)
                t2 = four(SA)[:, :, :, 0:n]
                wc, ws = pg(WP[:, 0, s, :], n), pg(WP[:, 1, s, :], n)
                cmul(four(CC)[:, :, :, n:2 * n], four(SS_)[:, :, :, n:2 * n], four(CC)[:, :, :, 0:n], four(SS_)[:, :, :, 0:n],
                     wc, ws, t, t2)
            dve.wait_ge(sem.bc_in, N_BC * (q + 1))
            if q:
                dve.wait_ge(sem.tap_ps, 2 * q)
            t = TMP[:, 0:DQ * CH].rearrange("p (d g n) -> p d g n", d=2, n=CH)
            t2 = TMP[:, 512:512 + DQ * CH].rearrange("p (d g n) -> p d g n", d=2, n=CH)
            TT2(four(BB), pg(CRE, CH), four(B1_), ALU.mult)
            TT2(t, pg(CIM, CH), four(B2_), ALU.mult)
            TT2(four(BW), pg(CRE, CH), four(B2_), ALU.mult)
            dve_link(TT2(t2, pg(CIM, CH), four(B1_), ALU.mult))
            TT2(four(BB), four(BB), t, ALU.add)
            dve_link(TT2(four(BW), four(BW), t2, ALU.subtract))
            TS(BW.rearrange("p g n -> p (g n)"), BW.rearrange("p g n -> p (g n)"), col[:, 2:3], None, ALU.mult)\
                .then_inc(sem.b_bar, 1)
            dve.wait_ge(sem.b_bar, q + 1)
            if q:
                dve.wait_ge(sem.m1T_ps, 4 * q)
            dve_link(s5_inputs(nc.vector, dve_link, q, 0, TMP[:, 0:GQ * P], GQ))
            s5_inputs(nc.vector, dve_link, q, 1, TMP[:, 0:GQ // 2 * P], GQ // 2).then_inc(sem.m1, 1)
            dve.wait_ge(sem.m1, 2 * q + 2)

        def s5_inputs(eng, link, q, d, temp, n, first_group=0):
            step = slice(L - 1, None, -1) if d == 0 else slice(0, L)
            b_ = slice(GQ * d + first_group, GQ * d + first_group + n)
            m = M1[:, b_, :].rearrange("p g (k n) -> p g k n", n=CH)
            t = temp.rearrange("p (g k n) -> p g k n", g=n, n=CH)
            ar, ai = (by_group(v, q, d)[:, first_group:first_group + n, step][:, :, :, None].to_broadcast([P, n, L, CH]) for v in (AR, AI))
            bb, bw = (v[:, b_, None, :].to_broadcast([P, n, L, CH]) for v in (BB, BW))
            eng.tensor_tensor(m, ar, bb, ALU.mult)
            link(eng.tensor_tensor(t, ai, bw, ALU.mult))
            last = eng.tensor_tensor(M1[:, b_, :].rearrange("p g n -> p (g n)"), M1[:, b_, :].rearrange("p g n -> p (g n)"),
                                     temp, ALU.add)
            return last

        def s5_turn_c(dve, q):
            dve.wait_ge(sem.cT_ps, q + 1)
            TS(C1_.rearrange("p a n -> p (a n)"), ps[7][:, 0:256], col[:, 2:3], -1.0, ALU.mult, ALU.mult)
            TS(C2_.rearrange("p a n -> p (a n)"), ps[7][:, 256:512], -1.0, None, ALU.mult).then_inc(sem.cT, 1)
            dve.wait_ge(sem.cT, q + 1)

        def s5_taps_basis(dve, q):
            if q:
                dve.wait_ge(sem.y_ps, q)
            dve_link(s5_powers(nc.vector, dve_link, q, 0, TMP[:, 0:GQ * NK * CH], GQ))
            if q:
                s5_outputs(dve, q - 1)
            s5_powers(nc.vector, dve_link, q, 1, TMP[:, 0:GQ // 2 * NK * CH], GQ // 2).then_inc(sem.m3, 1)
            dve.wait_ge(sem.m3, 2 * q + 2)

        def s5_powers(eng, link, q, d, temp, n, first_group=0):
            step = slice(0, NK) if d == 0 else slice(NK - 1, None, -1)
            b_ = slice(GQ * d + first_group, GQ * d + first_group + n)
            m = M3[:, b_, :].rearrange("p g (k n) -> p g k n", n=CH)
            t = temp.rearrange("p (g k n) -> p g k n", g=n, n=CH)
            ar, ai = (by_group(v, q, d)[:, first_group:first_group + n, step][:, :, :, None].to_broadcast([P, n, NK, CH]) for v in (AR, AI))
            c1, c2 = (v[:, d, :].rearrange("p (g n) -> p g n", g=GQ)[:, first_group:first_group + n, None, :].to_broadcast([P, n, NK, CH])
                      for v in (C1_, C2_))
            eng.tensor_tensor(m, ar, c1, ALU.mult)
            link(eng.tensor_tensor(t, ai, c2, ALU.mult))
            last = eng.tensor_tensor(M3[:, b_, :].rearrange("p g n -> p (g n)"), M3[:, b_, :].rearrange("p g n -> p (g n)"),
                                     temp, ALU.add)
            return last

        def s5_pool_inputs(pool, q):
            pool.wait_ge(sem.b_bar, q + 1)
            if q:
                pool.wait_ge(sem.m1T_ps, 4 * q)
            s5_inputs(nc.gpsimd, pool_link, q, 1, TMP_P, GQ // 2, GQ // 2).then_inc(sem.m1, 1)

        def s5_pool_powers(pool, q):
            pool.wait_ge(sem.cT, q + 1)
            pool.wait_ge(sem.uT_ps, 4)
            if q:
                pool.wait_ge(sem.y_ps, q)
            s5_powers(nc.gpsimd, pool_link, q, 1, SV.rearrange("p g c -> p (g c)")[:, 0:GQ // 2 * NK * CH], GQ // 2, GQ // 2)\
                .then_inc(sem.m3, 1)

        def s5_main(dve, q):
            flat = lambda v, d: v[:, GQ * d:GQ * d + GQ, :].rearrange("p g c -> p (g c)")

            def turn_back(d):
                dve.wait_ge(sem.st_sb, 2 * q + d + 1)
                TT2(flat(SV, d), flat(CC, d), flat(SA, d), ALU.mult)
                dve.wait_ge(sem.turn_ps, 4 * q + d + 1)
                dve_link(TT2(ps[2 + d][:], ps[2 + d][:], flat(SS_, d), ALU.mult))
                TT2(flat(SV, d), flat(SV, d), ps[2 + d][:], ALU.add).then_inc(sem.turned, 1)
                dve.wait_ge(sem.turned, 4 * q + d + 1)

            turn_back(0)
            for b in range(2):
                dve.wait_ge(sem.tap_ps, 2 * q + b + 1)
                r = slice(4 * b, 4 * b + 4)
                nc.vector.tensor_copy(KT[:, r, 0:P], ps[4 + b][0:CH, :].rearrange("p (g n) -> p g n", g=4))
                dve_link(nc.vector.tensor_copy(KT[:, r, P:P + 112], ps[6 + b][0:CH, 0:448].rearrange("p (g n) -> p g n", g=4)))
            dve_link(TT2(DK, ident[0:CH, None, 0:CH].to_broadcast([CH, GQ, CH]),
                         DT_[:, GQ * q:GQ * q + GQ, None].to_broadcast([CH, GQ, CH]), ALU.mult))
            TT2(KT[:, :, P - CH:P], KT[:, :, P - CH:P], DK, ALU.add).then_inc(sem.taps, 1)
            for d in range(2):
                if d:
                    turn_back(1)
                for g in range(GQ):
                    dg = G * d + GQ * q + g
                    last = nc.vector.tensor_tensor_scan(SA[:, GQ * d + g, :], DECAY[:, dg:dg + 1].to_broadcast([P, NC]),
                                                        SV[:, GQ * d + g, :], 0.0, ALU.mult, ALU.add)
                last.then_inc(sem.state, 1)
            for d in range(2):
                dve.wait_ge(sem.state, 3 * q + d + 1)
                dve.wait_ge(sem.turn_ps, 4 * q + d + 3)
                TT2(flat(SV, d), flat(CC, d), flat(SA, d), ALU.mult)
                dve_link(TT2(ps[2 + d][:], ps[2 + d][:], flat(SS_, d), ALU.mult))
                TT2(flat(SV, d), flat(SV, d), ps[2 + d][:], ALU.subtract).then_inc(sem.turned, 1)
                dve.wait_ge(sem.turned, 4 * q + d + 3)
            nc.vector.tensor_copy(DK[:, 0, 0:1], DK[:, 0, 0:1]).then_inc(sem.state, 1)

        def s5_outputs(dve, q):
            for b in range(2):
                dve.wait_ge(sem.yT_ps, 2 * q + b + 1)
                src = ps[4 + b][0:NC, :].rearrange("p (g m i n) -> p i m g n", g=4, m=T, i=2)
                for i in range(2):
                    c = CH * (GQ * q + 4 * b)
                    dst = YP[NC * i:NC * i + NC, :, c:c + 4 * CH].rearrange("p m (g n) -> p m g n", g=4)
                    last = nc.vector.tensor_copy(dst, src[:, i, :, :, :])
                last.then_inc(sem.yp, 1)

        def one_dve(dve):
            norm_dve(dve, 0, chunked=True)
            one_params(dve)
            s5_prepare(dve, 0)
            copy_cols(dve)
            s5_turn_c(dve, 0)
            for b in range(4):
                dve.wait_ge(sem.uT_ps, b + 1)
                nc.vector.tensor_copy(UT[:, 8 * b:8 * b + 8, :], ps[4 + b][:].rearrange("p (g c) -> p g c", g=8)).then_inc(sem.uT, 1)
            s5_taps_basis(dve, 0)
            for m in range(T):
                dve.wait_ge(sem.za_rstd, m + 1)
                if m >= 2:
                    dve.wait_ge(sem.znT_ps, m - 1)
                z = ZN[:, m % 2, :]
                TS(z[:, 0:256], ps[m][:, 0:256], zrs[:, m, 0:1], None, ALU.mult)
                TS(z[:, 256:384], ps[m][:, 256:384], zrs[:, m, 1:2], None, ALU.mult)
                nc.vector.tensor_copy(z[:, 384:448], ps[m][:, 384:448])
                nc.vector.tensor_copy(z[:, 448:512], ps[m][:, 384:448]).then_inc(sem.zn, 1)
                if m >= 1:
                    znT_copy(dve, m - 1)
            znT_copy(dve, T - 1)
            for q in range(NQ):
                s5_main(dve, q)
                if q + 1 < NQ:
                    s5_prepare(dve, q + 1)
                    s5_turn_c(dve, q + 1)
                    s5_taps_basis(dve, q + 1)
            s5_outputs(dve, NQ - 1)
            dve.wait_ge(sem.pos_in, 32)
            ang = ANG[:, 0, :]
            dve_link(nc.vector.tensor_copy(ANG[:, 1, :].rearrange("p (i c) -> p i c", i=L), POS.rearrange("p (c i) -> p i c", i=L)))
            dve_link(TS(ang, ANG[:, 1, :], col[:, 0:1], None, ALU.mult))
            reduce_angle(ang, ROT[:, 0, :], ROT[:, 1, :]).then_inc(sem.angle, 1)
            dve.wait_ge(sem.trig, 2)
            TS(SIN1, SIN1, col[:, 1:2], None, ALU.mult).then_inc(sem.angle, 1)
            dve.wait_ge(sem.angle, 2)
            for r in range(3):
                raw = KRT if r == 0 else QR[:, r - 1, :]
                b = 6 + r % 2
                dve.wait_ge(sem.rope_ps, r + 1)
                TT2(ROT[:, r % 2, :], raw, COS1, ALU.mult)
                dve_link(TT2(ps[b][:], ps[b][:], SIN1, ALU.mult))
                TT2(raw, ROT[:, r % 2, :], ps[b][:], ALU.add).then_inc(sem.rope_done, 1)
            for m in range(T):
                dve.wait_ge(sem.geT_ps, m + 1)
                nc.vector.tensor_copy(GT_[:, :, P * m:P * m + P], ps[m][:].rearrange("p (k n) -> p k n", k=4)).then_inc(sem.geT, 1)
            for m in range(T):
                dve.wait_ge(sem.glu_ps, m + 1)
                if m >= 2:
                    dve.wait_ge(sem.glu_y, m - 1)
                TT2(GTMP[:, m % 2, :], ps[4 + m][:], BGLU, ALU.add).then_inc(sem.glu_x, 1)
                if m >= 1:
                    glu_gate(dve, m - 1)
            glu_gate(dve, T - 1)
            for m in range(T):
                dve.wait_ge(sem.mixer_rstd, m + 1)
                nc.vector.scalar_tensor_tensor(YG[:, m, :], YG[:, m, :], ars[:, 0, m:m + 1], GS[:, m, :], ALU.mult, ALU.mult)\
                    .then_inc(sem.ssm_o, 1)
            for u in range(NU1 + 4):
                if u < NU1:
                    dve.wait_ge(sem.a_s_ps, u + 1)
                    if u >= 4:
                        dve.wait_ge(sem.a_exp, u - 3)
                    nc.vector.tensor_reduce(mn[:, u % 4:u % 4 + 1], ps[u % 3][:], AX_X, ALU.min).then_inc(sem.a_min, 1)
                z = u - 2
                if 0 <= z < NU1:
                    dve.wait_ge(sem.a_pT_ps, z + 1)
                    if z >= 2:
                        dve.wait_ge(sem.a_o_ps, z - 1)
                    nc.vector.tensor_copy(PT1[:, z % 2, :], ps[3 + z % 2][:]).then_inc(sem.a_pT, 1)
                z = u - 4
                if z >= 0 and z % 4 == 3:
                    h = z // 4
                    dve.wait_ge(sem.a_exp, z + 1)
                    r = rg[:, h % 3, :]
                    dve_link(nc.vector.reciprocal(r, rs[:, 4 * h:4 * h + 4]))
                    dve.wait_ge(sem.a_o_ps, z + 1)
                    for m in range(T):
                        last = TS(O1[:, m, P * h:P * h + P], ps[5 + h % 2][:, P * m:P * m + P], r[:, m:m + 1], None, ALU.mult)
                    last.then_inc(sem.a_o, 1)
            for m in range(T):
                mix1_copy(dve, m, m, R_SO, 4)
            for m in range(T):
                dve.wait_ge(sem.mixer_rstd, T + m + 1)
                nc.vector.scalar_tensor_tensor(O1[:, m, :], O1[:, m, :], ars[:, 1, m:m + 1], GA[:, m, :], ALU.mult, ALU.mult)\
                    .then_inc(sem.at_o, 1)
            for m in range(T):
                mix1_copy(dve, 4 + m, m, R_AO, 0)
            post_add(dve, 0, MIX)

        def mix1_copy(dve, i, m, row, k0):
            dve.wait_ge(sem.m1ix_ps, i + 1)
            dst = HT[:, k0:k0 + 4, :].rearrange("p k (c i) -> p k i c", i=L)[:, :, 2 * m:2 * m + 2, :]
            for k in range(4):
                last = TS(dst[:, k, :, :], ps[i][:, P * k:P * k + P].rearrange("p (i c) -> p i c", i=2),
                          cols[:, row + k:row + k + 1], None, ALU.mult)
            last.then_inc(sem.m1ix, 1)

        def znT_copy(dve, m):
            dve.wait_ge(sem.znT_ps, m + 1)
            src = ps[4 + m][:].rearrange("p (k n) -> p k n", k=4)
            TT2(ZT[:, 0:3, P * m:P * m + P], src[:, 0:3, :], cols[:, R_QN:R_QN + 3, None].to_broadcast([P, 3, P]), ALU.mult)
            nc.vector.tensor_copy(ZT[:, 3, P * m:P * m + P], src[:, 3, :]).then_inc(sem.znT, 1)

        def glu_gate(dve, m):
            dve.wait_ge(sem.glu_s, m + 1)
            TT2(YG[:, m, :], YG[:, m, :], GTMP[:, m % 2, :], ALU.mult).then_inc(sem.glu_y, 1)

        def one_act(act, post_gain, load_small):
            one_params_dma(act)
            norm_squares(act, 0, lambda t: x_tile(-1, t))
            act.wait_ge(sem.par_in, N_PAR)
            nc.scalar.activation(LDT, LDT, ACT.Exp).then_inc(sem.dt_e, 1)
            EA, CS_, SN, T1, T2, ER = PA[:, 27:36, :], PA[:, 5, :], PA[:, 4, :], PA[:, 7, :], PA[:, 8, :], PA[:, 3, :]
            act.wait_ge(sem.par_exp, 1)
            for k in range(NK):
                nc.scalar.activation(EA[:, k, :], ER, ACT.Exp, scale=float(k)).then_inc(sem.amp, 1)
            act.wait_ge(sem.par_exp, 2)
            nc.scalar.activation(SN, T1, ACT.Sin).then_inc(sem.par_trig, 1)
            nc.scalar.activation(CS_, T2, ACT.Sin).then_inc(sem.par_trig, 1)
            one_bc_dma(act, 0)
            for m in range(T):
                act.wait_ge(sem.u_ps, m + 1)
                for i in range(2):
                    dst = U8[:, :, CH * (2 * m + i):CH * (2 * m + i) + CH]
                    last = nc.scalar.activation(dst, ps[m][NC * i:NC * i + NC, :].rearrange("p (g n) -> p g n", g=G), ACT.Copy)
                last.then_inc(sem.u_sb, 1)
            load_small()
            post_gain(0, a["post_norm_g"])
            for m in range(T):
                act.wait_ge(sem.gs_ps, m + 1)
                nc.scalar.activation(GS[:, m, :], ps[m][:], ACT.Silu).then_inc(sem.gs, 1)
            for m in range(T):
                act.wait_ge(sem.za_ps, m + 1)
                if m:
                    act.wait_ge(sem.za_rstd, m)
                act_link(nc.scalar.activation(JUNK_Z[:, 0:256], ps[m][:, 0:256], ACT.Square, accum_out=zss[:, 0:1]))
                nc.scalar.activation(JUNK_Z[:, 0:128], ps[m][:, 256:384], ACT.Square, accum_out=zss[:, 1:2]).then_inc(sem.za_sq, 1)
                if m < T - 1:
                    act.wait_ge(sem.za_sq, m + 1)
            for m in range(T):
                act.wait_ge(sem.ga_ps, m + 1)
                nc.scalar.activation(GA[:, m, :], ps[m][:], ACT.Silu).then_inc(sem.ga, 1)
            def turn_outputs(q):
                act.wait_ge(sem.y_ps, q + 1)
                nc.scalar.activation(YS, ps[6][:], ACT.Copy).then_inc(sem.y_sb, 1)

            for q in range(NQ):
                for b in range(4):
                    act.wait_ge(sem.m1T_ps, 4 * q + b + 1)
                    if b == 0:
                        act.wait_ge(sem.uT_ps, 4)
                        if q:
                            act.wait_ge(sem.st_ps, 2 * q)
                            act.wait_ge(sem.toep, 128 * q)
                    nc.scalar.activation(W1[:, 4 * b:4 * b + 4, :], ps[b][:].rearrange("p (g n) -> p g n", g=4), ACT.Copy)\
                        .then_inc(sem.w1T, 1)
                if q:
                    turn_outputs(q - 1)
                for d in range(2):
                    act.wait_ge(sem.st_ps, 2 * q + d + 1)
                    nc.scalar.activation(SA[:, GQ * d:GQ * d + GQ, :], ps[d][:].rearrange("p (g c) -> p g c", g=GQ), ACT.Copy)\
                        .then_inc(sem.st_sb, 1)
                act.wait_ge(sem.taps, q + 1)
                if q:
                    act.wait_ge(sem.y_ps, q)
                for i in range(L):
                    c = CH * (L - 1 - i)
                    act.dma_start(TT[CH * i:CH * i + CH, :, :], KT[:, :, c:c + P]).then_inc(sem.toep, 16)
            turn_outputs(NQ - 1)
            act.wait_ge(sem.state, 3 * NQ)
            act.dma_start(POS, a["positions"].to_broadcast([P, SEQ])).then_inc(sem.pos_in, 16)
            act.dma_start(BGLU, a["b_glu"].to_broadcast([P, WIDE])).then_inc(sem.pos_in, 16)
            act.wait_ge(sem.yp, 2 * NQ)
            nc.scalar.activation(YG, YP, ACT.Gelu_apprx_tanh).then_inc(sem.ge, 1)
            for h in range(H1):
                act.wait_ge(sem.qn_ps, h + 1)
                nc.scalar.activation(QN[:, h, :], ps[h][:], ACT.Copy, scale=-SCALE1).then_inc(sem.qn, 1)
            for r in range(2):
                act.wait_ge(sem.rq_ps, r + 1)
                nc.scalar.activation(QR[:, r, :], ps[4 + r][:], ACT.Copy, scale=-SCALE1).then_inc(sem.rq, 1)
            act.wait_ge(sem.angle, 1)
            nc.scalar.activation(SIN1, ROT[:, 0, :], ACT.Sin).then_inc(sem.trig, 1)
            nc.scalar.activation(COS1, ROT[:, 1, :], ACT.Sin).then_inc(sem.trig, 1)
            for h in range(H1):
                act.wait_ge(sem.kn_ps, h + 1)
                nc.scalar.activation(KN[:, h, :], ps[h][:], ACT.Copy).then_inc(sem.kn, 1)
            for m in range(T):
                act.wait_ge(sem.v1_ps, m + 1)
                nc.scalar.activation(V1[:, m, :], ps[m][:], ACT.Copy).then_inc(sem.v1, 1)
            for m in range(T):
                act.wait_ge(sem.glu_x, m + 1)
                nc.scalar.activation(GTMP[:, m % 2, :], GTMP[:, m % 2, :], ACT.Sigmoid).then_inc(sem.glu_s, 1)
            for m in range(T):
                act.wait_ge(sem.glu_y, m + 1)
                if m:
                    act.wait_ge(sem.mixer_sq, m)
                nc.scalar.activation(JUNK1, YG[:, m, :], ACT.Square, accum_out=ass[:, 0, m:m + 1]).then_inc(sem.mixer_sq, 1)
            for u in range(NU1):
                act.wait_ge(sem.a_min, u + 1)
                if u >= 2:
                    act.wait_ge(sem.a_pT_ps, u - 1)
                nc.scalar.activation(PR1[:, u % 2, :], ps[u % 3][:], ACT.Exp, bias=mn[:, u % 4:u % 4 + 1], scale=-1.0,
                                     accum_out=rs[:, u:u + 1]).then_inc(sem.a_exp, 1)
            for m in range(T):
                act.wait_ge(sem.a_o, H1)
                act.wait_ge(sem.mixer_sq, T + m)
                nc.scalar.activation(JUNK1, O1[:, m, :], ACT.Square, accum_out=ass[:, 1, m:m + 1]).then_inc(sem.mixer_sq, 1)
            post_squares(act, 0, MIX, mixed(0))

        def one_pool(pool):
            norm_rstd(pool, 0)
            s5_pool_inputs(pool, 0)
            s5_pool_powers(pool, 0)
            for m in range(T):
                pool.wait_ge(sem.za_sq, m + 1)
                pool_link(nc.gpsimd.tensor_scalar(zms[:, 0:1], zss[:, 0:1], 1.0 / Q_RANK, EPS, ALU.mult, ALU.add))
                pool_link(nc.gpsimd.tensor_scalar(zms[:, 1:2], zss[:, 1:2], 1.0 / KV_RANK, EPS, ALU.mult, ALU.add))
                nc.gpsimd.tensor_tensor(zrs[:, m, :], zms, neghalf[:, 0:2], ALU.pow).then_inc(sem.za_rstd, 1)
            for q in range(1, NQ):
                s5_pool_inputs(pool, q)
                s5_pool_powers(pool, q)
            for o in range(2):
                for m in range(T):
                    pool.wait_ge(sem.mixer_sq, T * o + m + 1)
                    pool_link(nc.gpsimd.tensor_scalar(ams[:, m:m + 1], ass[:, o, m:m + 1], 1.0 / WIDE, EPS, ALU.mult, ALU.add))
                    nc.gpsimd.tensor_tensor(ars[:, o, m:m + 1], ams[:, m:m + 1], neghalf[:, 0:1], ALU.pow).then_inc(sem.mixer_rstd, 1)
            post_factor(pool, 0, MIX)

        HEADS = [("sel", h) for h in range(NH)] + [("win", h) for h in range(NH)] + [("fox", h) for h in range(NH)]

        def q_of(kind, h, t):
            tok = slice(P * t, P * t + P)
            if kind == "fox":
                return fq[0:HD + 2, h, tok]
            o = HD * (h % 2)
            return qrT[o:o + HD, h // 2, tok]

        def k_of(kind, h, n):
            if kind == "fox":
                return fk[0:HD + 2, h, 0:n]
            o = HD * (h % 2)
            return {"sel": ksT, "win": kwT}[kind][o:o + HD, h // 4, 0:n]

        def v_of(kind, h, b):
            if kind == "fox":
                return fv[:, b, HD * h:HD * h + HD]
            o = {"sel": 0, "win": P}[kind] + HD * (h // 4)
            return vn[:, b, o:o + HD]

        def o_of(kind, h, t):
            c = HD * h + (512 if kind == "fox" else 0)
            return O[:, t, c:c + HD]

        def two_pe(pe, l):
            v = 1 + 2 * l
            w0 = B1 + 2 * l
            if w0:
                pe.wait_ge(sem.post_y, 8 * w0)
            def bank_free(n):
                if n >= 8:
                    pe.wait_ge(sem.proj_sb, NPJ * l + n - 3)

            def wide_product(bank, j, low, tok=slice(0, SEQ)):
                w = split(pe, l, j)
                for k in range(KD):
                    last = product(bank[:, tok], [v[:, P * k:P * k + P] for v in w],
                                   [v[:, k, tok] for v in (HT_R, low[1])], k == 0, k == KD - 1)
                return last

            def natural(n, t, name, width):
                bank_free(n)
                for k in range(KD):
                    w = split(pe, l, (0 if name == "n1" else 12) + k // 2)
                    if name != "n1":
                        w = [v.rearrange("p (k c) -> p k c", c=512) for v in w]
                    x = [v[:, k, P * t:P * t + P] for v in (HT_R, HL_IN[1])]
                    last = product(proj_bank(n)[:, 0:width], x, [v[:, k % 2, :] for v in w], k == 0, k == KD - 1)
                last.then_inc(sem.proj, 1)

            def transposed(n):
                bank_free(n)
                wide_product(proj_bank(n), n, HL_IN).then_inc(sem.proj, 1)

            def permute(m):
                n = 6 + m
                pe.wait_ge(sem.proj_sb, NPJ * l + n + 1)
                if m >= 2:
                    pe.wait_ge(sem.rot, NPM * l + m - 1)
                src = kraw[:, m, :] if m < 2 else qT[:, m - 2, :]
                nc.tensor.matmul(ps[4 + m % 2][:], swap2[:], src, start=True, stop=True).then_inc(sem.perm, 1)

            def hidden(i):
                pe.wait_ge(sem.cmp_E, 2 * l + i + 1)
                if l:
                    pe.wait_ge(sem.cs_o, T * l)
                wv = block_of(f"w1{'kv'[i]}_{l}", pe, CMP_HID)
                for j in range(2):
                    for k in range(LP):
                        last = nc.tensor.matmul(ps[6 + i][:, 64 * j:64 * j + 2 * NCMP], wv[:, k, P * j:P * j + P],
                                                E[i][:, k, :], start=(k == 0), stop=(k == LP - 1))
                last.then_inc(sem.hid_ps, 1)

            def compressed():
                pe.wait_ge(sem.hid, 4 * l + 2)
                for j in range(2):
                    last = nc.tensor.matmul(ps[6][:, 0:2 * NCMP], w2k[:, l, j, :], hidk[:, j, 0:2 * NCMP],
                                            start=(j == 0), stop=(j == 1))
                last.then_inc(sem.kc_ps, 1)
                pe.wait_ge(sem.hid_rep, l + 1)
                for g in range(KVG):
                    for j in range(2):
                        last = nc.tensor.matmul(ps[7][:, HD * g:HD * g + HD], hidr[:, j, g, :, :].rearrange("p r n -> p (r n)"),
                                                w2v[:, l, j, :], start=(j == 0), stop=(j == 1))
                last.then_inc(sem.vc_ps, 1)

            def forget_transpose():
                pe.wait_ge(sem.proj_sb, NPJ * l + 4)
                if l:
                    pe.wait_ge(sem.vc, l)
                for t in range(T):
                    last = nc.tensor.transpose(ps[7][0:8, P * t:P * t + P], gf[:, t, NGATE:NGATE + 8], ident[:])
                last.then_inc(sem.ff_T, 1)

            def cmp_scores(t):
                if t == 0:
                    pe.wait_ge(sem.kc, l + 1)
                    pe.wait_ge(sem.rot, NPM * (l + 1))
                else:
                    pe.wait_ge(sem.cs_p, T * l + t)
                for j in range(4):
                    last = nc.tensor.matmul(ps[4][:, HD * j:HD * j + HD], qT[:, j, P * t:P * t + P],
                                            kcBD[:, j // 2, :, :].rearrange("p o n -> p (o n)"), start=True, stop=True)
                last.then_inc(sem.cs_ps, 1)

            def cmp_transpose(t):
                pe.wait_ge(sem.cs_p, T * l + t + 1)
                if t:
                    pe.wait_ge(sem.cs_pT, T * l + t)
                for g in range(KVG):
                    last = nc.tensor.transpose(ps[5][:, P * g:P * g + P], CP[:, g, :], ident[:])
                last.then_inc(sem.cs_pT_ps, 1)

            def cmp_values(t):
                pe.wait_ge(sem.cs_pT, T * l + t + 1)
                if t == 0:
                    pe.wait_ge(sem.vc, l + 1)
                    pe.wait_ge(sem.kc, l + 1)
                else:
                    pe.wait_ge(sem.cs_o, T * l + t)
                for g in range(KVG):
                    last = nc.tensor.matmul(ps[6][:, 256 * g:256 * g + 256], CX[:, g, :],
                                            vBD[:, g, :, :].rearrange("p h d -> p (h d)"), start=True, stop=True)
                last.then_inc(sem.cs_o_ps, 1)

            norm_transpose(pe, v - V0, 0)
            for n in range(4):
                if n + 1 < T:
                    norm_transpose(pe, v - V0, n + 1)
                pe.wait_ge(sem.hT, 8 * (v - V0) + 2 * n + 2)
                natural(n, n, "n1", 288)
            transposed(4)
            transposed(5)
            forget_transpose()
            transposed(6)
            transposed(7)
            permute(0)
            hidden(0)
            pe.wait_ge(sem.ff_z, l + 1)
            hidden(1)
            permute(1)
            transposed(8)
            transposed(9)
            permute(2)
            compressed()
            transposed(10)
            permute(3)
            transposed(11)
            permute(4)
            for n in range(12, 16):
                natural(n, n - 12, "n2", 512)
                if n == 12:
                    permute(5)
            for n in range(16, 24):
                transposed(n)
                t = n - 16
                if t < T:
                    cmp_scores(t)
                if 1 <= t <= T:
                    cmp_transpose(t - 1)
                if 2 <= t <= T + 1:
                    cmp_values(t - 2)

            for u in range(NU + LAG + 1):
                if u < NU:
                    kind, h = HEADS[u // 4]
                    t = u % 4
                    if u == 0:
                        pe.wait_ge(sem.rot, NPM * (l + 1))
                        pe.wait_ge(sem.vc, l + 1)
                    elif u < 4:
                        pe.wait_ge(sem.proj_sb, NPJ * l + 20 + u)
                    elif u == LAG + 1:
                        pe.wait_ge(sem.proj_sb, NPJ * (l + 1))
                        pe.wait_ge(sem.aug_ones, l + 1)
                        pe.wait_ge(sem.ff_rows, 32 * (l + 1))
                        pe.wait_ge(sem.cs_o, T * (l + 1))
                    if u >= 4:
                        pe.wait_ge(sem.s_exp, NU * l + u - 3)
                    nc.tensor.matmul(s_bank(u)[:, 0:P * (t + 1)], q_of(kind, h, t), k_of(kind, h, P * (t + 1)),
                                     start=True, stop=True).then_inc(sem.s_ps, 1)
                w = u - LAG
                if 0 <= w < NU:
                    if w == 0:
                        pe.wait_ge(sem.proj_sb, NPJ * (l + 1))
                    pe.wait_ge(sem.s_exp, NU * l + w + 1)
                    if w >= 2:
                        pt_wait(pe, l, w - 2)
                    for b in range(w % 4 + 1):
                        last = nc.tensor.transpose(ps[3 + w % 2][:, P * b:P * b + P], PR[:, w % 4, P * b:P * b + P], ident[:])
                    last.then_inc(sem.pT_ps, 1)
                w = u - LAG - 1
                if 0 <= w < NU:
                    kind, h = HEADS[w // 4]
                    t, gr = w % 4, w // 4
                    pt_wait(pe, l, w)
                    if t == 0 and gr >= 2:
                        pe.wait_ge(sem.o_sb, NU // 4 * l + gr - 1)
                    for b in range(t + 1):
                        last = nc.tensor.matmul(ps[5 + gr % 2][:, HD * t:HD * t + HD], PT[:, w % 2, P * b:P * b + P],
                                                v_of(kind, h, b), start=(b == 0), stop=(b == t))
                    last.then_inc(sem.o_ps, 1)

            pe.wait_ge(sem.o_sb, NU // 4 * (l + 1))
            for i in range(8):
                t, half = i // 2, i % 2
                for k in range(4):
                    c = 512 * half + P * k
                    last = nc.tensor.transpose(ps[i][:, P * k:P * k + P], O[:, t, c:c + P], ident[:])
                last.then_inc(sem.mixT_ps, 1)
            for e in range(8):
                t, half = MIX(e)
                pe.wait_ge(sem.mixT_lo, 8 * l + 2 * t + 2)
                for k in range(KD):
                    w = [v[:, 512 * half:512 * half + 512] for v in split(pe, l, J_OUT + k)]
                    x = [v[:, k, P * t:P * t + P] for v in (HT_R, HL_MIX[1])]
                    last = product(ps[e][:], x, w, k == 0, k == KD - 1)
                last.then_inc(sem.out_ps, 1)

            pe.wait_ge(sem.post_y, 8 * (w0 + 1))
            for t in range(3):
                norm_transpose(pe, v + 1 - V0, t)
            for step in range(8):
                half, i = divmod(step, 4)
                if step == 2:
                    norm_transpose(pe, v + 1 - V0, 3)
                pe.wait_ge(sem.hT, 8 * (v + 1 - V0) + 4 * half + 4)
                last = wide_product(ps[up_bank(0) + i], J_MLP + i, HL_MLP, slice(256 * half, 256 * half + 256))
                if half:
                    last.then_inc(sem.up_ps, 1)
            for g in range(NG):
                for i in range(FG):
                    f = FG * g + i
                    if f < 4:
                        continue
                    if i >= 4:
                        pe.wait_ge(sem.relu, NF * l + f - 3)
                    elif g:
                        pe.wait_ge(sem.mlp_sum, mlp_count(l, g - 1, 0))
                    wide_product(ps[up_bank(g) + f % 4], J_MLP + 2 * FG * g + i, HL_MLP).then_inc(sem.up_ps, 1)
                for half in range(2):
                    if half:
                        pe.wait_ge(sem.relu, NF * l + FG * (g + 1))
                    elif g:
                        pe.wait_ge(sem.mlp_sum, mlp_count(l, g - 1, 1))
                    if (g, half) == LAST_HALF:
                        for t in range(T):
                            for i in range(FG):
                                w = split(pe, l, J_MLP + 2 * FG * g + FG + FG // 2 * half + i // 2)
                                w = [v[:, 512 * (i % 2):512 * (i % 2) + 512] for v in w]
                                x = [v[:, i, P * t:P * t + P] for v in (uT_hi, uT_lo)]
                                last = product(ps[down_bank(g, half) + t][:], x, w, i == 0, i == FG - 1)
                            last.then_inc(sem.down, 1)
                        continue
                    for i in range(FG):
                        pe.wait_ge(sem.relu_sq, NF * l + FG * g + i + 1)
                        w = split(pe, l, J_MLP + 2 * FG * g + FG + FG // 2 * half + i // 2)
                        w = [v[:, 512 * (i % 2):512 * (i % 2) + 512] for v in w]
                        for t in range(T):
                            x = [v[:, i, P * t:P * t + P] for v in (uT_hi, uT_lo)]
                            last = product(ps[down_bank(g, half) + t][:], x, w, i == 0, i == FG - 1)
                        if i % 2:
                            last.then_inc(sem.down, 1)

        def up_bank(g):
            return 4 * ((g + 1) % 2)

        def down_bank(g, half):
            return 4 * ((g + half) % 2)

        def mlp_count(l, g, half):
            return 8 * NG * l + 8 * g + 4 * half + 4

        MLP_BANK = down_bank(NG - 1, 0)

        def pt_wait(eng, l, u):
            if on_act(u):
                eng.wait_ge(sem.pT_act, N_ACT * l + ACT_BEFORE[u] + 1)
            else:
                eng.wait_ge(sem.pT_dve, (NU - N_ACT) * l + u - ACT_BEFORE[u] + 1)

        def two_act(act, l, post_gain):
            v = 1 + 2 * l - V0
            w0 = B1 + 2 * l
            norm_squares(act, v, lambda t: x_tile(2 * l, t))
            for i in range(8):
                norm_hi(act, v, HL_IN, i)
                if i < 2:
                    split_hi(act, l, 2 * i)
                    split_hi(act, l, 2 * i + 1)
                if i >= 4:
                    split_hi(act, l, i)
            post_gain(w0, a["g_post_mix_2"][l:l + 1, :])

            def copy(dst, src, scale=1.0):
                return nc.scalar.activation(dst, src, ACT.Copy, scale=scale)

            def evacuate(n):
                act.wait_ge(sem.proj, NPJ * l + n + 1)
                src = proj_bank(n)
                if n < 4:
                    copy(vn[:, n, :], src[:, 0:256])
                    last = copy(gf[:, n, :], src[:, 256:288])
                elif n < 6:
                    for g in range(KVG):
                        mine = src[HD * g:HD * g + HD, :]
                        copy(X2[n - 4][0:HD, g, :], mine)
                        last = copy(X2[n - 4][HD:P, g, 0:SEQ - 1], mine[:, 1:SEQ])
                elif n < 8:
                    last = copy(kraw[:, n - 6, :], src[:])
                elif n < 12:
                    last = copy(qT[:, n - 8, :], src[:], -SCALE2)
                elif n < 16:
                    last = copy(fv[:, n - 12, :], src[:])
                else:
                    dst, scale = (fq, -SCALE2) if n < 20 else (fk, 1.0)
                    for o in range(2):
                        last = copy(dst[0:HD, 2 * (n % 4) + o, :], src[HD * o:HD * o + HD, :], scale)
                last.then_inc(sem.proj_sb, 1)

            def gelu_hidden(i):
                act.wait_ge(sem.hid_ps, 2 * l + i + 1)
                for j in range(2):
                    bias = cols[:, R_B1 + 4 * i + 2 * l + j:R_B1 + 4 * i + 2 * l + j + 1]
                    src = ps[6 + i][:, 64 * j:64 * j + 2 * NCMP]
                    if i == 0:
                        dst = hidk[:, j, 0:2 * NCMP]
                    else:
                        dst = hidv[:, j, :, 0:NCMP]
                        src = src.rearrange("p (g n) -> p g n", g=KVG)
                    nc.scalar.activation(dst, src, ACT.Gelu_apprx_tanh, bias=bias).then_inc(sem.hid, 1)

            def cmp_exp(t):
                act.wait_ge(sem.cs_exp, 2 * (T * l + t) + 1)
                nc.scalar.activation(CP.rearrange("p g n -> p (g n)"), CS.rearrange("p h n -> p (h n)"), ACT.Exp)\
                    .then_inc(sem.cs_exp, 1)

            act.wait_ge(sem.hT, 8 * v + 8)
            for n in range(4):
                evacuate(n)
            act.wait_ge(sem.gate, 2 * l + 1)
            nc.scalar.activation(gx[:], gx[:], ACT.Exp, scale=-1.0).then_inc(sem.gate_e, 1)
            evacuate(4)
            evacuate(5)
            act.wait_ge(sem.ff_z, l + 1)
            nc.scalar.activation(ffm[:], ffz[:], ACT.Abs).then_inc(sem.ff_part, 1)
            act.wait_ge(sem.ff_part, 3 * l + 1)
            nc.scalar.activation(ffm[:], ffm[:], ACT.Exp, scale=-1.0).then_inc(sem.ff_part, 1)
            act.wait_ge(sem.ff_part, 3 * l + 2)
            nc.scalar.activation(ffm[:], ffm[:], ACT.Ln, bias=1.0).then_inc(sem.ff_part, 1)
            evacuate(6)
            evacuate(7)
            gelu_hidden(0)
            split_hi(act, l, 8)
            split_hi(act, l, 9)
            gelu_hidden(1)
            for j in range(10, 16):
                split_hi(act, l, j)
            for n in range(8, 16):
                evacuate(n)
                if n >= 12:
                    split_hi(act, l, n + 4)
            act.wait_ge(sem.ff_cum, 2 * (l + 1))
            act.wait_ge(sem.aug_ones, l + 1)
            act.dma_start(fk[HD:HD + 1, :, :], ffc[:]).then_inc(sem.ff_rows, 16)
            act.dma_start(fq[HD + 1:HD + 2, :, :], ffz[:]).then_inc(sem.ff_rows, 16)
            for n in range(16, 24):
                evacuate(n)
                if n < 20:
                    split_hi(act, l, n + 4)
                if n - 16 < T:
                    cmp_exp(n - 16)

            for u in range(NU + LAG):
                if u < NU:
                    act.wait_ge(sem.s_masked, NU * l + u + 1)
                    if u >= 4:
                        act.wait_ge(sem.pT_ps, NU * l + u - 3)
                    w = P * (u % 4 + 1)
                    nc.scalar.activation(PR[:, u % 4, 0:w], s_bank(u)[:, 0:w], ACT.Exp, bias=mn[:, u % 4:u % 4 + 1],
                                         scale=-1.0, accum_out=rs[:, u:u + 1]).then_inc(sem.s_exp, 1)
                z = u - LAG
                if z >= 0 and on_act(z):
                    act.wait_ge(sem.pT_ps, NU * l + z + 1)
                    if z >= 2:
                        act.wait_ge(sem.o_ps, NU * l + z - 1)
                    w = P * (z % 4 + 1)
                    copy(PT[:, z % 2, 0:w], ps[3 + z % 2][:, 0:w]).then_inc(sem.pT_act, 1)
                if u in OUT_SPLITS:
                    split_hi(act, l, J_OUT + OUT_SPLITS.index(u))
            split_hi(act, l, J_OUT + 7)
            for i in range(8):
                hi, _, whole = norm_parts(HL_MIX, i)
                act.wait_ge(sem.mixT, 8 * l + i + 1)
                copy(hi, whole).then_inc(sem.mixT_hi, 1)
            post_squares(act, w0, MIX, mixed(B1 + l))
            norm_squares(act, v + 1, lambda t: x_tile(2 * l + 1, t))
            for i in range(8):
                norm_hi(act, v + 1, HL_MLP, i)
                if 1 <= i <= AHEAD:
                    split_hi(act, l, J_MLP + i - 1)
            post_gain(w0 + 1, a["g_post_mlp_2"][l:l + 1, :])
            for j in range(2 * NF):
                if j + AHEAD < 2 * NF:
                    split_hi(act, l, J_MLP + j + AHEAD)
                g, i = divmod(j, 2 * FG)
                if i < FG:
                    f = FG * g + i
                    act.wait_ge(sem.up_ps, NF * l + f + 1)
                    if f >= 2:
                        act.wait_ge(sem.relu_sq, NF * l + f - 1)
                    nc.scalar.activation(relu[:, f % 2, :], ps[up_bank(g) + f % 4][:], ACT.Relu).then_inc(sem.relu, 1)
            post_squares(act, w0 + 1, MLP, lambda e: (sem.mlp_sum, mlp_count(l, NG - 1, 0) - 3 + e), MLP_BANK)

        proj_bank = lambda n: ps[n % 4 + (4 if n < 4 else 0)]
        AHEAD = 4

        def x_tile(i, t):
            n = B1 + i
            return (sem.x_new, T * (n - 1) + t + 1) if n else (x_in[t], 16)

        def two_dve(dve, l):
            v = 1 + 2 * l - V0
            w0 = B1 + 2 * l
            norm_dve(dve, v, low=HL_IN, behind_two=lambda: [split_lo(dve, l, j) for j in range(4)])
            for j in range(4, 8):
                split_lo(dve, l, j)

            def rotate(m):
                dve.wait_ge(sem.perm, NPM * l + m + 1)
                dve_link(nc.vector.tensor_tensor(rsin[:, m % 2, :], ps[4 + m % 2][:], sin2[:], ALU.mult))
                dve.wait_ge(sem.rot_cos, NPM * l + m + 1)
                if m < 2:
                    dst = (ksT, kwT)[m]
                    for g in range(KVG):
                        for o in range(2):
                            a_, b_ = slice(HD * g, HD * g + HD), slice(HD * o, HD * o + HD)
                            last = nc.vector.tensor_tensor(dst[b_, g, :], rcos[a_, m % 2, :], rsin[a_, m % 2, :], ALU.add)
                else:
                    last = nc.vector.tensor_tensor(qrT[:, m - 2, :], rcos[:, m % 2, :], rsin[:, m % 2, :], ALU.add)
                last.then_inc(sem.rot, 1)

            def compressed():
                dve.wait_ge(sem.hid, 4 * l + 4)
                for j in range(2):
                    last = nc.vector.tensor_copy(hidr[:, j, :, :, :], hidv[:, j, :, None, :].to_broadcast([P, KVG, 4, 32]))
                last.then_inc(sem.hid_rep, 1)
                dve.wait_ge(sem.kc_ps, l + 1)
                for o in range(2):
                    r = slice(HD * o, HD * o + HD)
                    last = nc.vector.tensor_scalar(kcBD[r, :, o, 0:NCMP], ps[6][r, 0:2 * NCMP].rearrange("p (g n) -> p g n", g=KVG),
                                                   cols[r, R_B2K + l:R_B2K + l + 1], None, ALU.add)
                last.then_inc(sem.kc, 1)
                dve.wait_ge(sem.vc_ps, l + 1)
                for i in range(4):
                    r = slice(32 * i, 32 * i + 32)
                    last = nc.vector.tensor_tensor(vBD[r, :, i, :], ps[7][r, 0:P].rearrange("p (g d) -> p g d", g=KVG),
                                                   b2v[r, l, None, :].to_broadcast([32, KVG, HD]), ALU.add)
                last.then_inc(sem.vc, 1)

            def cmp_softmax(t):
                dve.wait_ge(sem.cs_ps, T * l + t + 1)
                if t:
                    dve.wait_ge(sem.cs_pT_ps, T * l + t)
                dve_link(nc.vector.tensor_tensor(CS, ps[4][:, 0:256].rearrange("p (h n) -> p h n", n=32),
                                                 cmask[:, t, None, :].to_broadcast([P, NH, 32]), ALU.add))
                dve_link(nc.vector.tensor_reduce(cmn[:], CS, AX_X, ALU.min))
                nc.vector.tensor_tensor(CS, cmn[:, :, None].to_broadcast([P, NH, 32]), CS, ALU.subtract)\
                    .then_inc(sem.cs_exp, 1)
                dve.wait_ge(sem.cs_exp, 2 * (T * l + t) + 2)
                pv = CP.rearrange("p g (h n) -> p (g h) n", n=32)
                dve_link(nc.vector.tensor_reduce(csum[:], pv, AX_X, ALU.add))
                dve_link(nc.vector.reciprocal(csum[:], csum[:]))
                dve_link(nc.vector.scalar_tensor_tensor(csum[:], gate[:, t, :].rearrange("p (h b) -> p b h", b=3)[:, 0, :],
                                                        valid[:, t:t + 1], csum[:], ALU.mult, ALU.mult))
                nc.vector.tensor_tensor(pv, pv, csum[:, :, None].to_broadcast([P, NH, 32]), ALU.mult).then_inc(sem.cs_p, 1)

            def cmp_pT(t):
                dve.wait_ge(sem.cs_pT_ps, T * l + t + 1)
                if t:
                    dve.wait_ge(sem.cs_o_ps, T * l + t)
                nc.vector.tensor_copy(CX, ps[5][:, 0:256].rearrange("p (g n) -> p g n", g=KVG)).then_inc(sem.cs_pT, 1)

            def cmp_out(t):
                dve.wait_ge(sem.cs_o_ps, T * l + t + 1)
                nc.vector.tensor_copy(CO[:, t, :], ps[6][:]).then_inc(sem.cs_o, 1)

            dve.wait_ge(sem.proj_sb, NPJ * l + 4)
            nc.vector.tensor_tensor(gx[:], gf[:, :, 0:NGATE], gbias[:, l, None, :].to_broadcast([P, T, NGATE]), ALU.add)\
                .then_inc(sem.gate, 1)
            dve.wait_ge(sem.ff_T, l + 1)
            if l:
                dve.wait_ge(sem.ff_rows, 32 * l)
            nc.vector.tensor_scalar(ffz[:], ps[7][0:8, :], cols[0:8, R_BF + l:R_BF + l + 1], None, ALU.add)\
                .then_inc(sem.ff_z, 1)
            dve.wait_ge(sem.gate_e, l + 1)
            dve_link(nc.vector.tensor_scalar(gx[:], gx[:], 1.0, None, ALU.add))
            nc.vector.reciprocal(gate[:], gx[:]).then_inc(sem.gate, 1)
            dve.wait_ge(sem.ff_part, 3 * l + 3)
            dve_link(nc.vector.scalar_tensor_tensor(ffz[:], ffz[:], 0.0, ffm[:], ALU.min, ALU.subtract))
            nc.vector.tensor_tensor_scan(ffc[:], ones[0:8, 0:1].to_broadcast([8, SEQ]), ffz[:], 0.0, ALU.mult, ALU.add).then_inc(sem.ff_cum, 1)
            dve.wait_ge(sem.ff_cum, 2 * l + 1)
            nc.vector.tensor_scalar(ffz[:], ffc[:], -1.0, None, ALU.mult).then_inc(sem.ff_cum, 1)
            dve.wait_ge(sem.gate, 2 * l + 2)
            rotate(0)
            split_lo(dve, l, 8)
            split_lo(dve, l, 9)
            rotate(1)
            for j in range(10, 16):
                split_lo(dve, l, j)
            compressed()
            for m in range(2, 6):
                rotate(m)
            for j in range(16, 20):
                split_lo(dve, l, j)
            for t in range(T + 2):
                if 1 <= t <= 4:
                    split_lo(dve, l, 19 + t)
                if t < T:
                    cmp_softmax(t)
                if 1 <= t <= T:
                    cmp_pT(t - 1)
                if t >= 2:
                    cmp_out(t - 2)

            for u in range(NU + LAG + 2):
                if u < NU:
                    dve.wait_ge(sem.s_ps, NU * l + u + 1)
                    if u >= 4:
                        dve.wait_ge(sem.s_exp, NU * l + u - 3)
                    t = u % 4
                    w = P * (t + 1)
                    nc.vector.tensor_tensor_reduce(s_bank(u)[:, 0:w], s_bank(u)[:, 0:w], tri[:, SEQ - w:SEQ], 1.0,
                                                   3.0e38, ALU.add, ALU.min, mn[:, t:t + 1]).then_inc(sem.s_masked, 1)
                z = u - LAG
                if 0 <= z < NU and not on_act(z):
                    dve.wait_ge(sem.pT_ps, NU * l + z + 1)
                    if z >= 2:
                        dve.wait_ge(sem.o_ps, NU * l + z - 1)
                    w = P * (z % 4 + 1)
                    nc.vector.tensor_copy(PT[:, z % 2, 0:w], ps[3 + z % 2][:, 0:w]).then_inc(sem.pT_dve, 1)
                z = u - LAG - 2
                if z >= 0 and z % 4 == 3:
                    gr = z // 4
                    kind, h = HEADS[gr]
                    dve.wait_ge(sem.s_exp, NU * l + z + 1)
                    r = rg[:, gr % 3, :]
                    dve_link(nc.vector.reciprocal(r, rs[:, 4 * gr:4 * gr + 4]))
                    if kind != "fox":
                        b = 1 if kind == "sel" else 2
                        dve_link(nc.vector.tensor_tensor(r, r, gate[:, :, 3 * h + b], ALU.mult))
                    dve.wait_ge(sem.o_ps, NU * l + z + 1)
                    for t in range(T):
                        src = ps[5 + gr % 2][:, HD * t:HD * t + HD]
                        dst = o_of(kind, h, t)
                        if kind == "fox":
                            last = nc.vector.tensor_scalar(dst, src, r[:, t:t + 1], None, ALU.mult)
                        else:
                            base = CO[:, t, HD * h:HD * h + HD] if kind == "sel" else dst
                            last = nc.vector.scalar_tensor_tensor(dst, src, r[:, t:t + 1], base, ALU.mult, ALU.add)
                    last.then_inc(sem.o_sb, 1)

            for i in range(8):
                _, _, whole = norm_parts(HL_MIX, i)
                dve.wait_ge(sem.mixT_ps, 8 * l + i + 1)
                nc.vector.tensor_copy(whole, ps[i][:].rearrange("p (k n) -> p k n", k=4)).then_inc(sem.mixT, 1)
            post_add(dve, w0, MIX)
            norm_dve(dve, v + 1, low=HL_MLP, behind_two=lambda: [split_lo(dve, l, J_MLP + j) for j in range(2)])
            for j in range(2, AHEAD):
                split_lo(dve, l, J_MLP + j)
            for j in range(2 * NF):
                if j + AHEAD < 2 * NF:
                    split_lo(dve, l, J_MLP + j + AHEAD)
                g, i = divmod(j, 2 * FG)
                if i in (2 * FG - FG // 2 - 1, 2 * FG - 1) and (g, (i - FG) // (FG // 2)) != LAST_HALF:
                    add_outputs(dve, l, g, (i - FG) // (FG // 2), range(T))
            post_add(dve, w0 + 1, MLP, MLP_BANK, lambda e: e >= 4 and add_outputs(dve, l, *LAST_HALF, [e - 4]))

        def add_outputs(dve, l, g, half, tiles):
            if g:
                dve.wait_ge(sem.mlp_sum, mlp_count(l, g - 1, half))
            for t in tiles:
                dve.wait_ge(sem.down, down_count(l, g, half, t if (g, half) == LAST_HALF else FG // 2 - 1))
                bank, y = ps[down_bank(g, half) + t][:], Y[:, t, 512 * half:512 * half + 512]
                if g == 0:
                    last = nc.vector.tensor_copy(y, bank)
                else:
                    last = nc.vector.tensor_tensor(bank if g == NG - 1 else y, bank, y, ALU.add)
                last.then_inc(sem.mlp_sum, 1)

        def two_pool(pool, l):
            v = 1 + 2 * l - V0
            w0 = B1 + 2 * l
            norm_rstd(pool, v)
            norm_lo(pool, v, HL_IN)
            for i in range(2):
                pool.wait_ge(sem.proj_sb, NPJ * l + 5 + i)
                r0 = R_POS + 32 * i + LP * l
                for g in range(KVG):
                    src = window(X2[i], g)
                    last = nc.gpsimd.tensor_tensor(E[i][:, :, NCMP * g:NCMP * g + NCMP], src,
                                                   cols[:, r0:r0 + LP, None].to_broadcast([P, LP, NCMP]), ALU.add)
                last.then_inc(sem.cmp_E, 1)
            for m in range(NPM):
                pool.wait_ge(sem.proj_sb, NPJ * l + 7 + m)
                if m >= 2:
                    pool.wait_ge(sem.rot, NPM * l + m - 1)
                src = kraw[:, m, :] if m < 2 else qT[:, m - 2, :]
                nc.gpsimd.tensor_tensor(rcos[:, m % 2, :], src, cos2[:], ALU.mult).then_inc(sem.rot_cos, 1)
            pool.wait_ge(sem.proj, NPJ * l + 16)
            pool.wait_ge(sem.rot_cos, NPM * (l + 1))
            nc.gpsimd.memset(fq[HD:HD + 2, :, :], 1.0)
            nc.gpsimd.memset(fk[HD:HD + 2, :, :], 1.0).then_inc(sem.aug_ones, 1)
            pool.wait_ge(sem.aug_ones, l + 1)
            for k in range(KD):
                split_lo(pool, l, J_OUT + k)
            for i in range(8):
                hi, lo, whole = norm_parts(HL_MIX, i)
                pool.wait_ge(sem.mixT_hi, 8 * l + i + 1)
                nc.gpsimd.tensor_tensor(lo, whole, hi.bitcast(F32), ALU.subtract).then_inc(sem.mixT_lo, 1)
            post_factor(pool, w0, MIX)
            norm_rstd(pool, v + 1)
            norm_lo(pool, v + 1, HL_MLP)
            for f in range(NF):
                pool.wait_ge(sem.relu, NF * l + f + 1)
                r, i = relu[:, f % 2, :], f % FG
                pool_link(nc.gpsimd.tensor_tensor(r, r, r, ALU.mult))
                if f >= FG:
                    pool.wait_ge(sem.down, down_count(l, f // FG - 1, 1, i // 2))
                pool_link(nc.gpsimd.tensor_copy(uT_hi[:, i, :], r))
                nc.gpsimd.tensor_tensor(uT_lo[:, i, :], r, uT_hi[:, i, :].bitcast(F32), ALU.subtract).then_inc(sem.relu_sq, 1)
            post_factor(pool, w0 + 1, MLP)

        def window(x2, g):
            v = x2[:, g, 0:SEQ]
            ap = [list(d) for d in v.ap]
            return bass.AP(v.tensor, v.offset, [ap[0], [2, LP], [CMP_STRIDE, NCMP]])

        V0 = 0 if first else 1
        OUT_SPLITS = [74 + 3 * k for k in range(7)]
        LAG = 3
        s_bank = lambda u: ps[(7, 0, 1, 2)[u % 4]]
        on_act = lambda u: u % 2 == 1
        ACT_BEFORE = [sum(on_act(x) for x in range(u)) for u in range(NU)]
        N_ACT = sum(on_act(u) for u in range(NU))

        vectors1, vectors2 = [], []
        if first:
            vectors1 += [(R_PRE1, a["pre_norm_g"][0]), (R_QN, a["q_norm_g"][0]), (R_KVN, a["kv_norm_g"][0]),
                        (R_AO, a["attn_out_g"][0]), (R_SO, a["ssm_out_g"][0])]
        for l in range(DEPTH):
            vectors2 += [(R_NORM + 16 * l, a["g_pre_mix_2"][l]), (R_NORM + 16 * l + 8, a["g_pre_mlp_2"][l]),
                        (R_B1 + 2 * l, a["cmp_b1_k_2"][l]), (R_B1 + 4 + 2 * l, a["cmp_b1_v_2"][l]),
                        (R_POS + LP * l, a["cmp_pos_k_2"][l].rearrange("(k o) d -> (k o d)", o=2)),
                        (R_POS + 32 + LP * l, a["cmp_pos_v_2"][l].rearrange("(k o) d -> (k o d)", o=2))]
        small = [(swap2[:], a["c_swap2"]), (tri[:], a["c_tri"]), (cos2[:], a["c_cos2"]), (sin2[:], a["c_sin2"]),
                 (cmask[:], a["c_cmask"].rearrange("p (t n) -> p t n", t=T)), (valid[:], a["c_valid"])]
        for l in range(DEPTH):
            small += [(gbias[:, l, :], a["b_nsa_gate_2"][l:l + 1, :].to_broadcast([P, NGATE])),
                      (b2v[:, l, :], a["cmp_b2_v_2"][l:l + 1, :].to_broadcast([P, HD])),
                      (w2k[:, l, :, 0:HD], a["cmp_w2_k_2"][l].rearrange("(j p) d -> p j d", p=P)),
                      (w2k[:, l, :, HD:P], a["cmp_w2_k_2"][l].rearrange("(j p) d -> p j d", p=P)),
                      (w2v[:, l, :, :], a["cmp_w2_v_2"][l].rearrange("(j p) d -> p j d", p=P))]
        N_ROWS1, N_SMALL = 16 * len(vectors1), 16 * len(small)
        N_ROWS = N_ROWS1 + 16 * (len(vectors2) + 3)

        def turn_rows(pe):
            pe.wait_ge(sem.rows_in, N_ROWS)
            nc.tensor.transpose(ps[4][:, 0:ROWS], rows[:], ident[:]).then_inc(sem.cols_ps, 1)

        def copy_cols(dve):
            dve.wait_ge(sem.cols_ps, B1 + 1)
            nc.vector.tensor_copy(cols[:, R_NORM:ROWS], ps[4][:, R_NORM:ROWS]).then_inc(sem.cols_ready, 1)
            dve.wait_ge(sem.cols_ready, B1 + 1)

        block = ctx.enter_context(nc.Block())

        @block.sync
        def _(sp):
            for t in range(T):
                sp.dma_start(X[:, t, :], a["x"][P * t:P * t + P, :]).then_inc(x_in[t], 16)
            if first:
                sp.wait_ge(sem.rows_in, N_ROWS1)
                sp.wait_ge(sem.par_in, N_PAR)
            for u in units:
                for s, n in u.free:
                    sp.wait_ge(s, n)
                for where, src in u.pieces:
                    dst = slots(u)
                    if where is not None:
                        width = 512 if u.slots == 4 else P
                    if where is not None and where[0] == "q":
                        _, c, h, n = where
                        dst = dst[:, c:c + h * n].rearrange("p (h n) -> p h n", h=h)
                    elif where is not None:
                        dst = dst.rearrange("p (k c) -> p k c", c=width)[:, 0:src.shape[1], where[0]:where[0] + where[1]]
                    elif len(src.shape) == 3:
                        dst = dst.rearrange("p (k c) -> p k c", c=src.shape[2])[:, 0:src.shape[1], :]
                    else:
                        dst = dst[:, 0:src.shape[1]]
                    sp.dma_start(dst, src).then_inc(wring[u.slot], 16)
                if u.name == "ukv":
                    for q in range(1, NQ):
                        one_bc_dma(sp, q)
            sp.wait_ge(sem.out_done, 16 * T)

        @block.gpsimd
        def _(pool):
            nc.gpsimd.memset(neghalf[:], -0.5).then_inc(sem.const_set, 1)
            nc.gpsimd.memset(rows[:], 0.0).then_inc(sem.const_set, 1)
            nc.gpsimd.memset(ones[:], 1.0).then_inc(sem.const_set, 1)
            nc.gpsimd.memset(kcBD[:], 0.0).then_inc(sem.const_set, 1)
            nc.gpsimd.memset(vBD[:], 0.0).then_inc(sem.const_set, 1)
            nc.gpsimd.memset(hidv[:], 0.0).then_inc(sem.const_set, 1)
            pool.wait_ge(sem.const_set, 6)
            if first:
                one_pool(pool)
            if second:
                pool.wait_ge(sem.cols_ready, B1 + 1)
                pool.wait_ge(sem.small_in, N_SMALL)
                for l in range(DEPTH):
                    two_pool(pool, l)

        @block.scalar
        def _(act):
            act.dma_start(ident[:], a["c_ident"]).then_inc(sem.consts_in, 16)

            def load_rows(rows_, vectors):
                for r, src in vectors:
                    k = src.shape[0] // P
                    act.dma_start(rows_[r:r + k, :], src.rearrange("(k p) -> k p", p=P)).then_inc(sem.rows_in, 16)

            def load_small():
                if first:
                    act.wait_ge(sem.rows_in, N_ROWS1)
                act.wait_ge(sem.const_set, 6)
                load_rows(rows, vectors2)
                for o in range(2):
                    act.dma_start(rows[R_B2K:R_B2K + DEPTH, HD * o:HD * o + HD], a["cmp_b2_k_2"][0:DEPTH, :]).then_inc(sem.rows_in, 16)
                act.dma_start(rows[R_BF:R_BF + DEPTH, 0:8], a["b_forget_2"][0:DEPTH, :]).then_inc(sem.rows_in, 16)
                for dst, src in small:
                    act.dma_start(dst, src).then_inc(sem.small_in, 16)

            def post_gain(w, src):
                if w:
                    act.wait_ge(sem.post_y, 8 * w)
                act.dma_start(postg[:], src.to_broadcast([P, D])).then_inc(sem.postgain_in, 16)

            if first:
                load_rows(rows1, vectors1)
                one_act(act, post_gain, load_small)
            else:
                load_small()
            if second:
                act.wait_ge(sem.cols_ready, B1 + 1)
                act.wait_ge(sem.small_in, N_SMALL)
                for l in range(DEPTH):
                    two_act(act, l, post_gain)
            n = (B1 + 2 * DEPTH if second else 1)
            for t in range(T):
                act.wait_ge(sem.x_new, T * (n - 1) + t + 1)
                act.dma_start(out[P * t:P * t + P, :], X[:, t, :]).then_inc(sem.out_done, 16)

        @block.tensor
        def _(pe):
            pe.wait_ge(sem.consts_in, 16)
            pe.wait_ge(sem.const_set, 6)
            if first:
                pe.wait_ge(sem.rows_in, N_ROWS1)
                nc.tensor.transpose(ps[7][:, 0:R_NORM], rows1[:], ident[0:R_NORM, 0:R_NORM]).then_inc(sem.cols_ps, 1)
            else:
                turn_rows(pe)
            if first:
                one_pe(pe)
            if second:
                pe.wait_ge(sem.small_in, N_SMALL)
                for l in range(DEPTH):
                    two_pe(pe, l)

        @block.vector
        def _(dve):
            dve.wait_ge(sem.const_set, 6)
            if first:
                dve.wait_ge(sem.cols_ps, 1)
                nc.vector.tensor_copy(cols[:, 0:R_NORM], ps[7][:, 0:R_NORM]).then_inc(sem.cols_ready, 1)
                dve.wait_ge(sem.cols_ready, 1)
            else:
                copy_cols(dve)
            if first:
                one_dve(dve)
            if second:
                dve.wait_ge(sem.small_in, N_SMALL)
                for l in range(DEPTH):
                    two_dve(dve, l)


_INS = ["x", "positions", "pre_norm_g", "w_in", "q_norm_g", "w_uq", "kv_norm_g", "w_ukv", "attn_out_g",
        "s5_lam_re", "s5_lam_im", "s5_log_dt", "s5_b_re", "s5_b_im", "s5_c_re", "s5_c_im", "s5_d",
        "w_glu", "b_glu", "ssm_out_g", "w_out", "post_norm_g",
        "w_in_2", "b_nsa_gate_2", "b_forget_2", "cmp_pos_k_2", "cmp_w1_k_2", "cmp_b1_k_2", "cmp_w2_k_2", "cmp_b2_k_2",
        "cmp_pos_v_2", "cmp_w1_v_2", "cmp_b1_v_2", "cmp_w2_v_2", "cmp_b2_v_2", "w_out_2", "w_up_2", "w_down_2",
        "g_pre_mix_2", "g_post_mix_2", "g_pre_mlp_2", "g_post_mlp_2"]


def kernel(**inputs):
    import numpy as _np
    import concourse.bacc as _bacc
    from concourse import mybir as _mybir
    from concourse.bass_utils import run_bass_kernel_spmd as _run

    nc = _bacc.Bacc("TRN2", target_bir_lowering=False, num_devices=1)
    arrays, aps = {}, {}
    given = {name: _np.ascontiguousarray(inputs[name]) for name in _INS}
    given["x"] = given["x"].reshape(SEQ, D)
    given.update(constants())
    for name, value in given.items():
        arrays[f"in_{name}"] = value
        aps[name] = nc.dram_tensor(f"in_{name}", value.shape, _mybir.dt.from_np(value.dtype), kind="ExternalInput").ap()
    out = nc.dram_tensor("out", (SEQ, D), F32, kind="ExternalOutput").ap()
    build(nc, aps, out)
    r = _run(nc, [arrays], core_ids=[0])
    return r.results[0]["out"].reshape(1, SEQ, D)
```
